# Optimizing a Trainium2 kernel written in Bass

```python
import jax
import jax.numpy as jnp
from jax import lax
import numpy as np
import math
import jax, jax.numpy as jnp

D_MODEL = 1024
BATCH = 1
SEQ = 256
DEPTH = 1

M_HEADS = 4
M_HEAD_DIM = 128
M_WIDTH = M_HEADS * M_HEAD_DIM
M_CONV = 4
M_CHUNK = 64

A_HEADS = 8
A_HEAD_DIM = 64
A_WIDTH = A_HEADS * A_HEAD_DIM
MOBA_BLOCK = 256
MOBA_TOPK = 3
Q_BLOCK = 64
ROPE_THETA = 10000.0

D_FF = ((8 * D_MODEL + 3 * 256 - 1) // (3 * 256)) * 256

N_MOD = 6
IN_SPLITS = (M_WIDTH, M_WIDTH, M_WIDTH, M_WIDTH, M_HEADS, M_HEADS, A_WIDTH, A_WIDTH, A_WIDTH, D_MODEL, D_MODEL)
D_IN = 4 * M_WIDTH + 2 * M_HEADS + 3 * A_WIDTH + 2 * D_MODEL
F_GATE_OFFSET = 4 * M_WIDTH + M_HEADS
RMS_EPS = 1e-6


def rms_norm(x, g):
    xf = x.astype(jnp.float32)
    y = xf * lax.rsqrt(jnp.mean(xf * xf, axis=-1, keepdims=True) + RMS_EPS)
    return (y * g.astype(jnp.float32)).astype(x.dtype)

def modulate(h, shift, scale):
    return h * (1 + scale[:, None, :]) + shift[:, None, :]

def causal_dwconv(x, w, b):
    K = w.shape[0]
    S = x.shape[1]
    xp = jnp.pad(x, ((0, 0), (K - 1, 0), (0, 0)))
    y = b
    for j in range(K):
        y = y + xp[:, j:j + S, :] * w[j]
    return y

def split_heads(t, n_heads, head_dim):
    B, S, _ = t.shape
    return t.reshape(B, S, n_heads, head_dim).transpose(0, 2, 1, 3)

def merge_heads(t):
    B, H, S, Dh = t.shape
    return t.transpose(0, 2, 1, 3).reshape(B, S, H * Dh)

def rope(x, positions):
    half = x.shape[-1] // 2
    inv_freq = ROPE_THETA ** (-jnp.arange(half, dtype=jnp.float32) / half)
    ang = positions.astype(jnp.float32)[:, None, :, None] * inv_freq
    cos, sin = jnp.cos(ang), jnp.sin(ang)
    xf = x.astype(jnp.float32)
    x1, x2 = xf[..., :half], xf[..., half:]
    out = jnp.concatenate([x1 * cos - x2 * sin, x2 * cos + x1 * sin], axis=-1)
    return out.astype(x.dtype)

def mlstm_chunkwise(q, k, v, i_pre, f_pre):
    B, H, S, Dh = q.shape
    L = M_CHUNK
    NC = S // L
    f32 = jnp.float32
    q = q.astype(f32).reshape(B, H, NC, L, Dh)
    k = (k.astype(f32) * (Dh ** -0.5)).reshape(B, H, NC, L, Dh)
    v = v.astype(f32).reshape(B, H, NC, L, Dh)
    log_i = i_pre.astype(f32).reshape(B, H, NC, L)
    log_f = jax.nn.log_sigmoid(f_pre.astype(f32)).reshape(B, H, NC, L)
    b = jnp.cumsum(log_f, axis=-1)
    b_last = b[..., -1]
    a = b_last[..., None] - b + log_i

    def step(carry, inp):
        C, n, m = carry
        a_c, bl_c, k_c, v_c = inp
        m_new = jnp.maximum(bl_c + m, jnp.max(a_c, axis=-1))
        decay = jnp.exp(bl_c + m - m_new)
        w = jnp.exp(a_c - m_new[..., None])
        C_new = decay[..., None, None] * C + jnp.einsum('bhl,bhld,bhle->bhde', w, v_c, k_c)
        n_new = decay[..., None] * n + jnp.einsum('bhl,bhle->bhe', w, k_c)
        return (C_new, n_new, m_new), (C, n, m)

    init = (jnp.zeros((B, H, Dh, Dh), f32), jnp.zeros((B, H, Dh), f32), jnp.zeros((B, H), f32))
    xs = (jnp.moveaxis(a, 2, 0), jnp.moveaxis(b_last, 2, 0), jnp.moveaxis(k, 2, 0), jnp.moveaxis(v, 2, 0))
    _, (C_prev, n_prev, m_prev) = lax.scan(step, init, xs)
    C_prev = jnp.moveaxis(C_prev, 0, 2)
    n_prev = jnp.moveaxis(n_prev, 0, 2)
    m_prev = jnp.moveaxis(m_prev, 0, 2)

    causal = jnp.tril(jnp.ones((L, L), dtype=bool))
    D = b[..., :, None] - b[..., None, :] + log_i[..., None, :]
    D = jnp.where(causal, D, -jnp.inf)
    inter = b + m_prev[..., None]
    m_t = jnp.maximum(inter, jnp.max(D, axis=-1))
    W = jnp.exp(D - m_t[..., None])
    SW = jnp.einsum('bhctd,bhcsd->bhcts', q, k) * W
    inter_w = jnp.exp(inter - m_t)
    num = inter_w[..., None] * jnp.einsum('bhcde,bhcte->bhctd', C_prev, q) + jnp.einsum('bhcts,bhcsd->bhctd', SW, v)
    den = inter_w * jnp.einsum('bhce,bhcte->bhct', n_prev, q) + jnp.sum(SW, axis=-1)
    h = num / jnp.maximum(jnp.abs(den), jnp.exp(-m_t))[..., None]
    return h.reshape(B, H, S, Dh)

def moba_attention(q, k, v):
    B, H, S, Dh = q.shape
    NB = -(-S // MOBA_BLOCK)
    K_SEL = min(MOBA_TOPK, NB)
    pad = NB * MOBA_BLOCK - S
    NQ = S // Q_BLOCK
    scale = Dh ** -0.5
    kp = jnp.pad(k, ((0, 0), (0, 0), (0, pad), (0, 0)))
    vp = jnp.pad(v, ((0, 0), (0, 0), (0, pad), (0, 0)))
    kb = kp.reshape(B, H, NB, MOBA_BLOCK, Dh)
    vb = vp.reshape(B, H, NB, MOBA_BLOCK, Dh)
    kmean = jnp.mean(kb.astype(jnp.float32), axis=3).astype(k.dtype)
    bi = jnp.arange(B)[:, None, None, None]
    hi = jnp.arange(H)[None, :, None, None]
    blk_ids = jnp.arange(NB)

    def one_block(qi):
        q0 = qi * Q_BLOCK
        qc = lax.dynamic_slice_in_dim(q, q0, Q_BLOCK, axis=2)
        cur = q0 // MOBA_BLOCK
        gate = jnp.einsum('bhqd,bhnd->bhqn', qc, kmean).astype(jnp.float32)
        gate = jnp.where(blk_ids < cur, gate, -jnp.inf)
        _, gidx = lax.top_k(gate, K_SEL)
        valid = gidx < cur
        kg = kb[bi, hi, gidx]
        vg = vb[bi, hi, gidx]
        s_sel = jnp.einsum('bhqd,bhqjkd->bhqjk', qc, kg).astype(jnp.float32) * scale
        s_sel = jnp.where(valid[..., None], s_sel, -jnp.inf).reshape(B, H, Q_BLOCK, K_SEL * MOBA_BLOCK)
        k_own = lax.dynamic_slice_in_dim(kp, cur * MOBA_BLOCK, MOBA_BLOCK, axis=2)
        v_own = lax.dynamic_slice_in_dim(vp, cur * MOBA_BLOCK, MOBA_BLOCK, axis=2)
        s_own = jnp.einsum('bhqd,bhkd->bhqk', qc, k_own).astype(jnp.float32) * scale
        qpos = q0 + jnp.arange(Q_BLOCK)
        kpos = cur * MOBA_BLOCK + jnp.arange(MOBA_BLOCK)
        s_own = jnp.where(kpos[None, :] <= qpos[:, None], s_own, -jnp.inf)
        p = jax.nn.softmax(jnp.concatenate([s_sel, s_own], axis=-1), axis=-1).astype(v.dtype)
        p_sel = p[..., :K_SEL * MOBA_BLOCK].reshape(B, H, Q_BLOCK, K_SEL, MOBA_BLOCK)
        p_own = p[..., K_SEL * MOBA_BLOCK:]
        return jnp.einsum('bhqjk,bhqjkd->bhqd', p_sel, vg) + jnp.einsum('bhqk,bhkd->bhqd', p_own, v_own)

    outs = lax.map(one_block, jnp.arange(NQ))
    return outs.transpose(1, 2, 0, 3, 4).reshape(B, H, S, Dh)

def first_inputs(seed: int = 0) -> dict:
    key = jax.random.key(seed)
    ks = jax.random.split(key, 20)
    f32 = jnp.float32

    def nrm(k, shape, scale):
        return jax.random.normal(k, shape, f32) * scale

    x = nrm(ks[0], (BATCH, SEQ, D_MODEL), 1.0)
    c = nrm(ks[1], (BATCH, D_MODEL), 1.0)
    positions = jnp.broadcast_to(jnp.arange(SEQ, dtype=jnp.int32), (BATCH, SEQ))
    ada_w = nrm(ks[2], (DEPTH, D_MODEL, N_MOD * D_MODEL), 0.5 * D_MODEL ** -0.5)
    ada_b = nrm(ks[3], (DEPTH, N_MOD * D_MODEL), 0.02)
    norm1_g = 1.0 + nrm(ks[4], (DEPTH, D_MODEL), 0.02)
    norm2_g = 1.0 + nrm(ks[5], (DEPTH, D_MODEL), 0.02)
    normf_g = 1.0 + nrm(ks[6], (D_MODEL,), 0.02)
    w_in = nrm(ks[7], (DEPTH, D_MODEL, D_IN), D_MODEL ** -0.5)
    b_in = nrm(ks[8], (DEPTH, D_IN), 0.02)
    b_in = b_in.at[:, F_GATE_OFFSET:F_GATE_OFFSET + M_HEADS].add(jnp.linspace(3.0, 6.0, M_HEADS, dtype=f32))
    conv_w = nrm(ks[9], (DEPTH, M_CONV, 2 * M_WIDTH), M_CONV ** -0.5)
    conv_b = nrm(ks[10], (DEPTH, 2 * M_WIDTH), 0.02)
    m_norm_g = 1.0 + nrm(ks[11], (DEPTH, M_WIDTH), 0.02)
    p_mlstm = nrm(ks[12], (DEPTH, M_WIDTH, D_MODEL), M_WIDTH ** -0.5)
    p_moba = nrm(ks[13], (DEPTH, A_WIDTH, D_MODEL), A_WIDTH ** -0.5)
    w_out = nrm(ks[14], (DEPTH, D_MODEL, D_MODEL), D_MODEL ** -0.5)
    w_gate = nrm(ks[15], (DEPTH, D_MODEL, D_FF), D_MODEL ** -0.5)
    w_up = nrm(ks[16], (DEPTH, D_MODEL, D_FF), D_MODEL ** -0.5)
    w_down = nrm(ks[17], (DEPTH, D_FF, D_MODEL), D_FF ** -0.5)
    return {'x': x, 'c': c, 'positions': positions, 'ada_w': ada_w, 'ada_b': ada_b,
            'norm1_g': norm1_g, 'norm2_g': norm2_g, 'normf_g': normf_g, 'w_in': w_in, 'b_in': b_in,
            'conv_w': conv_w, 'conv_b': conv_b, 'm_norm_g': m_norm_g, 'p_mlstm': p_mlstm,
            'p_moba': p_moba, 'w_out': w_out, 'w_gate': w_gate, 'w_up': w_up, 'w_down': w_down}

def first_block(x, c, positions, ada_w, ada_b, norm1_g, norm2_g, normf_g, w_in, b_in,
              conv_w, conv_b, m_norm_g, p_mlstm, p_moba, w_out, w_gate, w_up, w_down):
    B, S, D = x.shape
    split_points = np.cumsum(IN_SPLITS)[:-1].tolist()
    c_act = jax.nn.silu(c)
    for l in range(DEPTH):
        mod = jnp.dot(c_act, ada_w[l]) + ada_b[l]
        sh1, sc1, g1, sh2, sc2, g2 = jnp.split(mod, N_MOD, axis=-1)

        h = modulate(rms_norm(x, norm1_g[l]), sh1, sc1)
        z = jnp.einsum('bsd,de->bse', h, w_in[l]) + b_in[l]
        mq, mk, mv, mo, mi, mf, aq, ak, av, ga, gb = jnp.split(z, split_points, axis=-1)

        qk = jax.nn.silu(causal_dwconv(jnp.concatenate([mq, mk], axis=-1), conv_w[l], conv_b[l]))
        mq, mk = jnp.split(qk, 2, axis=-1)
        hm = mlstm_chunkwise(split_heads(mq, M_HEADS, M_HEAD_DIM), split_heads(mk, M_HEADS, M_HEAD_DIM),
                             split_heads(mv, M_HEADS, M_HEAD_DIM), mi.transpose(0, 2, 1), mf.transpose(0, 2, 1))
        hm = rms_norm(hm.transpose(0, 2, 1, 3), m_norm_g[l].reshape(M_HEADS, M_HEAD_DIM))
        ym = (hm.reshape(B, S, M_WIDTH) * jax.nn.sigmoid(mo)).astype(x.dtype)

        qa = rope(split_heads(aq, A_HEADS, A_HEAD_DIM), positions)
        ka = rope(split_heads(ak, A_HEADS, A_HEAD_DIM), positions)
        va = split_heads(av, A_HEADS, A_HEAD_DIM)
        ya = merge_heads(moba_attention(qa, ka, va))

        merged = (jax.nn.sigmoid(ga) * jnp.einsum('bsm,md->bsd', ym, p_mlstm[l])
                  + jax.nn.sigmoid(gb) * jnp.einsum('bsa,ad->bsd', ya, p_moba[l]))
        x = x + g1[:, None, :] * jnp.einsum('bsd,de->bse', merged, w_out[l])

        h = modulate(rms_norm(x, norm2_g[l]), sh2, sc2)
        f = jax.nn.silu(jnp.einsum('bsd,df->bsf', h, w_gate[l])) * jnp.einsum('bsd,df->bsf', h, w_up[l])
        x = x + g2[:, None, :] * jnp.einsum('bsf,fd->bsd', f, w_down[l])
    return rms_norm(x, normf_g)


POOL_WINDOWS = (2, 4, 8, 16)
N_POOL_GROUPS = len(POOL_WINDOWS)
POOL_GROUP_DIM = D_MODEL // 8
POOL_WIDTH = N_POOL_GROUPS * POOL_GROUP_DIM

SSD_WIDTH = D_MODEL
SSD_HEAD_DIM = 64
SSD_HEADS = SSD_WIDTH // SSD_HEAD_DIM
SSD_GROUPS = 2
HEADS_PER_GROUP = SSD_HEADS // SSD_GROUPS
SSD_STATE = 128
SSD_CONV = 4
SSD_CHUNK = 128
CONV_DIM = SSD_WIDTH + 2 * SSD_GROUPS * SSD_STATE

MIX_WIDTH = POOL_WIDTH + SSD_WIDTH
IN_PROJ_DIM = POOL_WIDTH + SSD_WIDTH + CONV_DIM + SSD_HEADS

PEER_HEADS = 8
PEER_TOPK = 16
N_KEYS = 128
N_EXPERTS = N_KEYS * N_KEYS
D_KEY = 256
PEER_BLOCK = 128

EPS = 1e-6


def rmsnorm(x, g):
    xf = x.astype(jnp.float32)
    y = xf * lax.rsqrt(jnp.mean(xf * xf, axis=-1, keepdims=True) + EPS)
    return (y * g.astype(jnp.float32)).astype(x.dtype)

def modulate_2(h, shift, scale):
    return h * (1 + scale[:, None, :]) + shift[:, None, :]

def pool_mixer(u, pool_w, pool_b, pool_scale):
    Bsz, S, _ = u.shape
    ug = u.astype(jnp.float32).reshape(Bsz, S, N_POOL_GROUPS, POOL_GROUP_DIM)
    cs = jnp.cumsum(ug, axis=1)
    t = jnp.arange(S)
    pooled = []
    for gi, w in enumerate(POOL_WINDOWS):
        csg = cs[:, :, gi]
        cs_pad = jnp.pad(csg, ((0, 0), (w, 0), (0, 0)))
        win_sum = cs_pad[:, w:] - cs_pad[:, :S]
        count = jnp.minimum(t + 1, w).astype(jnp.float32)[None, :, None]
        pooled.append(win_sum / count)
    pooled = jnp.stack(pooled, axis=2)
    mixed = pooled - ug
    y = jnp.einsum("bsgc,gcd->bsgd", mixed, pool_w.astype(jnp.float32)) + pool_b.astype(jnp.float32)
    y = y * pool_scale.astype(jnp.float32)
    return y.reshape(Bsz, S, POOL_WIDTH).astype(u.dtype)

def ssd_chunked(xdt, a, b, c):
    Bsz, S, G, R, P = xdt.shape
    N = b.shape[-1]
    L = SSD_CHUNK
    nc = S // L
    xdt = xdt.reshape(Bsz, nc, L, G, R, P)
    b = b.reshape(Bsz, nc, L, G, N)
    c = c.reshape(Bsz, nc, L, G, N)
    a = a.reshape(Bsz, nc, L, G, R).transpose(0, 3, 4, 1, 2)
    a_cs = jnp.cumsum(a, axis=-1)

    causal = jnp.tril(jnp.ones((L, L), dtype=bool))
    seg = a_cs[..., :, None] - a_cs[..., None, :]
    decay = jnp.exp(jnp.where(causal, seg, -jnp.inf))
    cb = jnp.einsum("bclgn,bcsgn->bcgls", c, b)
    y_diag = jnp.einsum("bcgls,bgrcls,bcsgrp->bclgrp", cb, decay, xdt)

    decay_to_end = jnp.exp(a_cs[..., -1:] - a_cs)
    states = jnp.einsum("bclgn,bgrcl,bclgrp->bcgrpn", b, decay_to_end, xdt)
    chunk_decay = jnp.exp(a_cs[..., -1])

    def step(h, inp):
        st, dec = inp
        return h * dec[..., None, None] + st, h

    h0 = jnp.zeros((Bsz, G, R, P, N), jnp.float32)
    _, h_prev = lax.scan(step, h0, (jnp.moveaxis(states, 1, 0), jnp.moveaxis(chunk_decay, -1, 0)))
    y_off = jnp.einsum("bclgn,cbgrpn,bgrcl->bclgrp", c, h_prev, jnp.exp(a_cs))
    return (y_diag + y_off).reshape(Bsz, S, G, R, P)

def ssd_mixer(z, xbc, dt_raw, conv_w, conv_b, dt_bias, a_log, d_skip, ssd_norm):
    Bsz, S, _ = xbc.shape
    dtype = xbc.dtype
    xf = xbc.astype(jnp.float32)
    conv = lax.conv_general_dilated(
        xf, conv_w.astype(jnp.float32).reshape(SSD_CONV, 1, CONV_DIM),
        window_strides=(1,), padding=[(SSD_CONV - 1, 0)],
        dimension_numbers=("NWC", "WIO", "NWC"), feature_group_count=CONV_DIM)
    conv = jax.nn.silu(conv + conv_b.astype(jnp.float32))
    xs = conv[..., :SSD_WIDTH].reshape(Bsz, S, SSD_GROUPS, HEADS_PER_GROUP, SSD_HEAD_DIM)
    bs = conv[..., SSD_WIDTH:SSD_WIDTH + SSD_GROUPS * SSD_STATE].reshape(Bsz, S, SSD_GROUPS, SSD_STATE)
    cs = conv[..., SSD_WIDTH + SSD_GROUPS * SSD_STATE:].reshape(Bsz, S, SSD_GROUPS, SSD_STATE)

    dt = jax.nn.softplus(dt_raw.astype(jnp.float32) + dt_bias.astype(jnp.float32))
    dt = dt.reshape(Bsz, S, SSD_GROUPS, HEADS_PER_GROUP)
    A = -jnp.exp(a_log.astype(jnp.float32)).reshape(SSD_GROUPS, HEADS_PER_GROUP)
    y = ssd_chunked(xs * dt[..., None], dt * A, bs, cs)
    y = y + xs * d_skip.astype(jnp.float32).reshape(SSD_GROUPS, HEADS_PER_GROUP)[..., None]
    y = y.reshape(Bsz, S, SSD_WIDTH) * jax.nn.silu(z.astype(jnp.float32))
    return rmsnorm(y, ssd_norm).astype(dtype)

def peer(h, w_query, sub_keys1, sub_keys2, expert_down, expert_up):
    Bsz, S, D = h.shape
    T = Bsz * S
    hf = h.reshape(T, D)
    q = (hf @ w_query).reshape(T, PEER_HEADS, 2, D_KEY // 2)
    s1 = jnp.einsum("thk,hnk->thn", q[:, :, 0], sub_keys1).astype(jnp.float32)
    s2 = jnp.einsum("thk,hnk->thn", q[:, :, 1], sub_keys2).astype(jnp.float32)
    v1, i1 = lax.top_k(s1, PEER_TOPK)
    v2, i2 = lax.top_k(s2, PEER_TOPK)
    cand = (v1[..., :, None] + v2[..., None, :]).reshape(T, PEER_HEADS, PEER_TOPK * PEER_TOPK)
    cand_idx = (i1[..., :, None] * N_KEYS + i2[..., None, :]).reshape(T, PEER_HEADS, PEER_TOPK * PEER_TOPK)
    top_s, pos = lax.top_k(cand, PEER_TOPK)
    idx = jnp.take_along_axis(cand_idx, pos, axis=-1)
    gates = jax.nn.softmax(top_s, axis=-1).astype(h.dtype)

    nb = T // PEER_BLOCK

    def block_fn(args):
        hb, ib, gb = args
        u = expert_down[ib]
        act = jax.nn.gelu(jnp.einsum("td,thkd->thk", hb, u), approximate=False)
        v = expert_up[ib]
        return jnp.einsum("thk,thkd->td", gb * act, v)

    out = lax.map(block_fn, (hf.reshape(nb, PEER_BLOCK, D),
                             idx.reshape(nb, PEER_BLOCK, PEER_HEADS, PEER_TOPK),
                             gates.reshape(nb, PEER_BLOCK, PEER_HEADS, PEER_TOPK)))
    return out.reshape(Bsz, S, D)

def second_inputs(seed: int = 0) -> dict:
    key = jax.random.key(seed)
    ks = jax.random.split(key, 24)

    def nrm(k, shape, s):
        return jax.random.normal(k, shape, jnp.float32) * s

    x = nrm(ks[0], (BATCH, SEQ, D_MODEL), 1.0)
    c = nrm(ks[1], (BATCH, D_MODEL), 1.0)
    w_ada = nrm(ks[2], (DEPTH, D_MODEL, N_MOD * D_MODEL), 0.5 * D_MODEL ** -0.5)
    b_ada = nrm(ks[3], (DEPTH, N_MOD * D_MODEL), 0.02)
    norm_mix = 1.0 + nrm(ks[4], (DEPTH, D_MODEL), 0.02)
    norm_ffn = 1.0 + nrm(ks[5], (DEPTH, D_MODEL), 0.02)
    w_in = nrm(ks[6], (DEPTH, D_MODEL, IN_PROJ_DIM), D_MODEL ** -0.5)
    pool_w = nrm(ks[7], (DEPTH, N_POOL_GROUPS, POOL_GROUP_DIM, POOL_GROUP_DIM), POOL_GROUP_DIM ** -0.5)
    pool_b = nrm(ks[8], (DEPTH, N_POOL_GROUPS, POOL_GROUP_DIM), 0.02)
    pool_scale = 1.0 + nrm(ks[9], (DEPTH, N_POOL_GROUPS, POOL_GROUP_DIM), 0.1)
    conv_w = nrm(ks[10], (DEPTH, SSD_CONV, CONV_DIM), SSD_CONV ** -0.5)
    conv_b = nrm(ks[11], (DEPTH, CONV_DIM), 0.02)
    dt0 = jnp.exp(jax.random.uniform(ks[12], (DEPTH, SSD_HEADS), jnp.float32,
                                     minval=math.log(1e-3), maxval=math.log(1e-1)))
    dt_bias = dt0 + jnp.log(-jnp.expm1(-dt0))
    a_log = jnp.log(jax.random.uniform(ks[13], (DEPTH, SSD_HEADS), jnp.float32, minval=1.0, maxval=16.0))
    d_skip = 1.0 + nrm(ks[14], (DEPTH, SSD_HEADS), 0.1)
    ssd_norm = 1.0 + nrm(ks[15], (DEPTH, SSD_WIDTH), 0.02)
    w_out = nrm(ks[16], (DEPTH, MIX_WIDTH, D_MODEL), MIX_WIDTH ** -0.5)
    w_query = nrm(ks[17], (DEPTH, D_MODEL, PEER_HEADS * D_KEY), D_MODEL ** -0.5)
    sub_keys1 = nrm(ks[18], (DEPTH, PEER_HEADS, N_KEYS, D_KEY // 2), (D_KEY // 2) ** -0.5)
    sub_keys2 = nrm(ks[19], (DEPTH, PEER_HEADS, N_KEYS, D_KEY // 2), (D_KEY // 2) ** -0.5)
    expert_down = nrm(ks[20], (DEPTH, N_EXPERTS, D_MODEL), D_MODEL ** -0.5)
    expert_up = nrm(ks[21], (DEPTH, N_EXPERTS, D_MODEL), PEER_HEADS ** -0.5)
    norm_final = 1.0 + nrm(ks[22], (D_MODEL,), 0.02)
    return {"x": x, "c": c, "w_ada": w_ada, "b_ada": b_ada, "norm_mix": norm_mix, "norm_ffn": norm_ffn,
            "w_in": w_in, "pool_w": pool_w, "pool_b": pool_b, "pool_scale": pool_scale,
            "conv_w": conv_w, "conv_b": conv_b, "dt_bias": dt_bias, "a_log": a_log, "d_skip": d_skip,
            "ssd_norm": ssd_norm, "w_out": w_out, "w_query": w_query, "sub_keys1": sub_keys1,
            "sub_keys2": sub_keys2, "expert_down": expert_down, "expert_up": expert_up,
            "norm_final": norm_final}

def second_block(x, c, w_ada, b_ada, norm_mix, norm_ffn, w_in, pool_w, pool_b, pool_scale,
              conv_w, conv_b, dt_bias, a_log, d_skip, ssd_norm, w_out, w_query, sub_keys1,
              sub_keys2, expert_down, expert_up, norm_final):
    Bsz = x.shape[0]
    c_act = jax.nn.silu(c)
    s_z = POOL_WIDTH
    s_xbc = POOL_WIDTH + SSD_WIDTH
    s_dt = POOL_WIDTH + SSD_WIDTH + CONV_DIM
    for l in range(DEPTH):
        mod = (c_act @ w_ada[l] + b_ada[l]).reshape(Bsz, N_MOD, D_MODEL)
        shift_m, scale_m, gate_m, shift_f, scale_f, gate_f = [mod[:, i] for i in range(N_MOD)]

        h = modulate_2(rmsnorm(x, norm_mix[l]), shift_m, scale_m)
        proj = h @ w_in[l]
        y_pool = pool_mixer(proj[..., :s_z], pool_w[l], pool_b[l], pool_scale[l])
        y_ssd = ssd_mixer(proj[..., s_z:s_xbc], proj[..., s_xbc:s_dt], proj[..., s_dt:],
                          conv_w[l], conv_b[l], dt_bias[l], a_log[l], d_skip[l], ssd_norm[l])
        y = jnp.concatenate([y_pool, y_ssd], axis=-1) @ w_out[l]
        x = x + gate_m[:, None, :] * y

        h = modulate_2(rmsnorm(x, norm_ffn[l]), shift_f, scale_f)
        y = peer(h, w_query[l], sub_keys1[l], sub_keys2[l], expert_down[l], expert_up[l])
        x = x + gate_f[:, None, :] * y
    return rmsnorm(x, norm_final)


def setup_inputs(seed=0):
    out = dict(first_inputs(seed))
    for name, value in second_inputs(seed + 1).items():
        if name != "x":
            out[name + "_2"] = value
    return out


def reference(
    x, c, positions, ada_w, ada_b, norm1_g, norm2_g, normf_g, w_in, b_in, conv_w, conv_b,
    m_norm_g, p_mlstm, p_moba, w_out, w_gate, w_up, w_down, c_2, w_ada_2, b_ada_2, norm_mix_2,
    norm_ffn_2, w_in_2, pool_w_2, pool_b_2, pool_scale_2, conv_w_2, conv_b_2, dt_bias_2,
    a_log_2, d_skip_2, ssd_norm_2, w_out_2, w_query_2, sub_keys1_2, sub_keys2_2, expert_down_2,
    expert_up_2, norm_final_2,
):
    x = first_block(
        x, c, positions, ada_w, ada_b, norm1_g, norm2_g, normf_g, w_in, b_in, conv_w, conv_b,
        m_norm_g, p_mlstm, p_moba, w_out, w_gate, w_up, w_down,
    )
    return second_block(
        x, c_2, w_ada_2, b_ada_2, norm_mix_2, norm_ffn_2, w_in_2, pool_w_2, pool_b_2,
        pool_scale_2, conv_w_2, conv_b_2, dt_bias_2, a_log_2, d_skip_2, ssd_norm_2, w_out_2,
        w_query_2, sub_keys1_2, sub_keys2_2, expert_down_2, expert_up_2, norm_final_2,
    )


_drawn_inputs = setup_inputs


def setup_inputs(seed=0):
    import zlib

    import numpy as np

    out = dict(_drawn_inputs(seed))
    spreads = {}
    factors = {'ada_b': 2.704,
     'norm1_g': 8.0,
     'norm2_g': 7.099,
     'conv_b': 64.0,
     'm_norm_g': 8.0,
     'norm_mix_2': 6.003,
     'norm_ffn_2': 22.064,
     'pool_b_2': 8.0,
     'pool_scale_2': 3.61,
     'conv_b_2': 21.836,
     'd_skip_2': 200.0,
     'ssd_norm_2': 36.118,
     'norm_final_2': 25.711}
    for name, (base, spread) in spreads.items():
        noise = np.random.default_rng([zlib.crc32(name.encode()), seed]).standard_normal(out[name].shape)
        drawn = base * np.exp(spread * noise) if base else spread * noise
        out[name] = jnp.asarray(drawn.astype(out[name].dtype))
    for name, factor in factors.items():
        out[name] = (out[name] * factor).astype(out[name].dtype)
    return out
```

```python
from contextlib import ExitStack, contextmanager

import concourse.bass as bass
from concourse import mybir

F32 = mybir.dt.float32
I32 = mybir.dt.int32
U32 = mybir.dt.uint32
ALU = mybir.AluOpType
ACT = mybir.ActivationFunctionType
AX = mybir.AxisListType

P = 128
T = 256
NT = T // P
D = 1024
KC = D // P
MH, MD = 4, 128
AH, AD = 8, 64
FF = 2816
FC = FF // P
CONV = 4
SH, SP = 16, 64
SG = 2
POOLS = (2, 4, 8, 16)
NPOOL = len(POOLS)
XBC = 12
MIXC = NPOOL + KC
QH, NK, TOPK = 8, 128, 16
EPS = 1e-6
FAR = -1e30
LOWEST = -3.0e38
MAGIC = 12582912.0
TWO_PI = (6.28125, 0.0019350051879882812, 3.0199157663446432e-07)
PI_BELOW = 3.1415925
SCRATCH = 2048

Z_MQ, Z_MK, Z_MO, Z_GA, Z_GB, Z_N = 0, 4, 8, 12, 20, 28
TOK_BLOCKS = 4

COLS = {}
for _name, _width in (
    ("ada_b", 48), ("norm1", 8), ("norm2", 8), ("normf", 8), ("b_feat", Z_N), ("conv_w", 32), ("conv_b", 8),
    ("m_norm", 4), ("ada_b2", 48), ("norm_mix", 8), ("norm_ffn", 8), ("norm_final", 8), ("pool_b", 4),
    ("pool_scale", 4), ("conv_w2", 48), ("conv_b2", 12), ("d_skip", 8), ("ssd_norm", 8), ("b_i", 1), ("b_f", 1),
    ("dt_bias", 1), ("a_log", 1), ("inv_freq", 32),
):
    COLS[_name] = (sum(w for _, w in COLS.values()), _width)
NCOLS = sum(w for _, w in COLS.values())

STREAM = (("tok", 8), ("feat", 14), ("proj", 4), ("wout", 4), ("gateup", 22), ("down", 11), ("win2", 12),
          ("wout2", 6), ("query", 8), ("expert_down", 64), ("expert_up", 64))
SLOTS = 4

RING_A = (("ssq1", 1), ("feat", 28), ("qkT", 8), ("probsT", 8), ("attn", 4), ("ssq2", 1), ("gate", 22),
          ("ssqf", 1), ("ssq_mix", 1), ("win2", 24), ("ssq_ssd", 1), ("ssq_ffn", 1), ("query", 16),
          ("experts", 128), ("ssq_final", 1))
RING_D = (("gates", 2), ("tok", 8), ("gate_cols", 1), ("attn_scores", 8), ("m_decay", 4), ("m_scores", 4),
          ("m_out", 4), ("ymT", 4), ("proj", 16), ("wout", 8), ("up", 22), ("down", 4), ("dt", 1), ("pool", 4),
          ("dt_cols", 1), ("xs_tok", 4), ("cb", 2), ("ssd", 24), ("wout2", 4), ("scores", 16), ("picksT", 3),
          ("spread", 256), ("expert_up", 4))
BANKS = 4


def starts(stages):
    at, n = {}, 0
    for name, count in stages:
        at[name] = n
        n += count
    return at


PAIR_AT, A_AT, D_AT = starts(STREAM), starts(RING_A), starts(RING_D)


class Count:

    def __init__(self):
        self.n = 0
        self.loop = None

    def value(self, back=0):
        return self.n - back if self.loop is None else self.loop + (self.n - back)


@contextmanager
def repeat(eng, times, per):
    before = {c: c.n for c in per}
    with eng.Fori(0, times) as i:
        for c, k in per.items():
            c.loop = i * k
        yield i
    for c, k in per.items():
        assert c.n - before[c] == k, (c.n - before[c], k)
        c.loop, c.n = None, before[c] + k * times


class Own:

    def __init__(self, eng, sem):
        self.eng, self.sem, self.count = eng, sem, Count()

    def __call__(self, ins):
        ins.then_inc(self.sem, 1)
        self.count.n += 1
        self.eng.wait_ge(self.sem, self.count.value())


class Fill:

    def __init__(self, pe, psum, ready, drained):
        self.pe, self.psum, self.ready, self.drained, self.count = pe, psum, ready, drained, Count()

    def bank(self):
        n = self.count.n
        self.count.n += 1
        assert n >= BANKS or self.count.loop is None
        if n >= BANKS:
            self.pe.wait_ge(self.drained, self.count.value(BANKS))
        return self.psum[:, n % BANKS, :]

    def full(self, ins):
        ins.then_inc(self.ready, 1)


class Empty:

    def __init__(self, eng, psum, ready, drained):
        self.eng, self.psum, self.ready, self.drained, self.count = eng, psum, ready, drained, Count()

    def bank(self):
        n = self.count.n
        self.count.n += 1
        self.eng.wait_ge(self.ready, self.count.value())
        return self.psum[:, n % BANKS, :]

    def free(self, ins, settle=False):
        ins.then_inc(self.drained, 1)
        if settle:
            self.eng.wait_ge(self.drained, self.count.value())


def two_mixers_program(nc, x, c, c_2, pos, cols_in, bias_tok, w_gates, w_dt, pool_w, keys, ada, ada2,
                       tok, feat, proj, wout, gateup, down, win2, wout2, query, expert_down, expert_up, out):
    with ExitStack() as ctx:
        def sb(name, shape, dt=F32):
            return ctx.enter_context(nc.sbuf_tensor(name, shape, dt))

        sems = {}

        def sem(name):
            if name not in sems:
                sems[name] = ctx.enter_context(nc.semaphore(name))
            return sems[name]

        psA = ctx.enter_context(nc.psum_tensor("psA", [P, BANKS, 512], F32))
        psD = ctx.enter_context(nc.psum_tensor("psD", [P, BANKS, 512], F32))

        ring = sb("ring", [P, SLOTS, 2, 1024])
        xT = sb("xT", [P, KC, T])
        hT = sb("hT", [P, KC, T])
        bench = sb("bench", [P, 4096])
        arena = sb("arena", [P, 32768])
        ident = sb("ident", [P, P])
        ones = sb("ones", [P, P])
        mask_ts = sb("mask_ts", [P, T])
        mask_st = sb("mask_st", [P, T])
        cols = sb("cols", [P, NCOLS])
        mods = sb("mods", [P, 48])
        scale_cols = sb("scale_cols", [P, 2, KC])
        eps = sb("eps", [P, 1])
        late = sb("late", [P, 2304])

        taken = [0]

        def part(tensor, at, *shape):
            n = 1
            for s in shape:
                n *= s
            v = tensor[:, at:at + n]
            names = "abcd"[:len(shape)]
            if len(shape) > 1:
                v = v.rearrange(f"p ({' '.join(names)}) -> p {' '.join(names)}",
                                **{k: s for k, s in zip(names[1:], shape[1:])})
            return v

        def temp(*shape):
            at = taken[0]
            n = 1
            for s in shape:
                n *= s
            taken[0] += n
            assert taken[0] <= 32768, taken[0]
            return part(arena, at, *shape)

        ADA_SLOTS = 3
        ada_ring = temp(ADA_SLOTS, D)
        c_row = temp(2, D)
        b_tok = temp(TOK_BLOCKS, 512)
        zT = temp(Z_N, T)
        toks = temp(NT, 3 * 512)
        v_ext = temp(NT, MH, MD + 1)
        xn = temp(KC, T)
        qkT = temp(2, 4, T)
        convT = temp(2 * MH, T)
        probs = temp(AH, 3 * P)
        yaT = temp(4, T)
        ymT = temp(MH, T)
        nd = temp(NT * MH, MD + 1)
        trig = temp(4, NT, 32)
        assert taken[0] <= 32768
        probsT = part(bench, 0, AH, 3 * P)
        turn = part(xn.rearrange("p a b -> p (a b)"), 0, 2, 2, 16, 32)
        mw = part(xn.rearrange("p a b -> p (a b)"), 0, MH, 3 * P)
        mT = hT
        fT = part(arena, ADA_SLOTS * D + 4096, FC, T)
        assert FC <= Z_N

        after = ADA_SLOTS * D + 2 * D
        keysT = part(arena, after, 16, NK)
        z2T = part(arena, after + 2048, 24, T)
        at = after + 2048 + 24 * T
        xbcT = part(arena, at, XBC, T)
        at += XBC * T
        mixT = part(arena, at, MIXC, T)
        at += MIXC * T
        xs_tok = part(arena, at, NT, D)
        at += NT * D
        cbT = part(arena, at, SG, 3 * P)
        at += SG * 3 * P
        ssd_w = part(arena, at, 4, 3 * P)
        at += 4 * 3 * P
        PADDED = T + 16
        pool_a = part(arena, at, NPOOL, PADDED)
        at += NPOOL * PADDED
        pool_b = part(arena, at, NPOOL, PADDED)
        at += NPOOL * PADDED
        inv_t = part(arena, at, T)
        at += T
        pool_wt = part(arena, at, NPOOL, P)
        at += NPOOL * P
        xn2 = part(arena, at, KC, T)
        at += KC * T
        wg_gates = part(bench, 0, KC, 8)
        w_dts = part(arena, at, KC, SH)
        at += KC * SH
        assert at <= 32768, at

        U = arena[:, :].rearrange("p (e t) -> p e t", t=T)

        def row(i):
            return late[:, i * T:(i + 1) * T]
        r_i, r_f, r_abs, r_e, r_u, r_t, r_l, r_s = [row(i) for i in range(8)]
        small = part(late, 2048, 256)
        m_cols = part(small, 0, 2, MH, NT)
        mx = part(small, 16, 16)
        nmx = part(small, 32, 16)
        sums = part(small, 48, 16)
        rsums = part(small, 64, 16)
        m_stat = part(small, 80, 5, NT * MH)
        s_cols = part(small, 128, 2, NT, SH)
        a_col = part(small, 192, 2)
        posf = part(small, 200, 2)
        rinv = sb("rinv", [P, T])
        rms = sb("rms", [P, T])
        pos_i = sb("pos_i", [P, NT], I32)

        scores = part(bench, 0, NT, 2 * QH, NK)
        eq = part(bench, 0, NT * QH * TOPK, TOPK)
        iota_k = rms[:, P:2 * P]
        top_v = part(late, 0, NT * QH, TOPK)
        pick_a = part(late, 256, NT * QH, TOPK)
        pick_b = part(late, 512, NT * QH, TOPK)
        idx = part(late, 768, NT * QH, 2, TOPK)
        picked = part(late, 1280, 3, NT * QH * TOPK)
        picksT = part(late, 0, 3, T)
        stage = part(rinv, 0, T)
        work = part(rinv, 0, 2, NK)
        work2 = part(rms, 0, NK)
        cand = part(mask_ts, 0, TOPK, TOPK)
        cand2 = mask_st
        v16 = part(small, 208, 2, TOPK)
        i16 = sb("i16", [P, 3, TOPK], U32)
        ONEHOTS = 4
        hot = part(bench, 0, ONEHOTS, 2, NK)

        def col(name, j=0, n=1, parts=P):
            a, w = COLS[name]
            assert j + n <= w
            return cols[0:parts, a + j:a + j + n]

        def sel(h, heads):
            return ident[0:heads, h:h + 1].broadcast_to([heads, P])

        full = [sem(f"slot_full{s}") for s in range(SLOTS)]
        ada_full = [sem(f"ada_full{s}") for s in range(ADA_SLOTS)]
        pair_used, ada_used = sem("pair_used"), sem("ada_used")
        a_ready, a_drained = sem("a_ready"), sem("a_drained")
        d_ready, d_drained = sem("d_ready"), sem("d_drained")

        block = ctx.enter_context(nc.Block())

        @block.sync
        def _(sp):
            sp.dma_start(cols[:, :], cols_in[:, :]).then_inc(sem("cols_in"), 16)
            for k, cc in enumerate((c, c_2)):
                sp.dma_start(c_row[:, k, :], cc.broadcast_to([P, D])).then_inc(sem("c_in"), 16)
            sp.dma_start(pos_i[:, :], pos[:, :]).then_inc(sem("pos_in"), 16)
            sp.dma_start(xT[:, :, :], x[:, :, :]).then_inc(sem("x_in"), 16)
            sp.dma_start(wg_gates, w_gates[:, :, :]).then_inc(sem("w_gates_in"), 16)
            sp.dma_start(b_tok, bias_tok.rearrange("a b -> () (a b)").broadcast_to([P, 2048]).rearrange(
                "p (a b) -> p a b", a=TOK_BLOCKS)).then_inc(sem("b_tok_in"), 16)
            pairs = Count()

            def load(src):
                n = pairs.n
                pairs.n += 1
                if n >= SLOTS:
                    sp.wait_ge(pair_used, pairs.value(SLOTS))
                sp.dma_start(ring[:, n % SLOTS, :, :].rearrange("p a b -> p (a b)"), src).then_inc(full[n % SLOTS], 16)

            def stream(src, n):
                turns, rest = divmod(n, SLOTS)
                peel = SLOTS if pairs.n == 0 else 0
                for j in range(peel):
                    load(src[j])
                if turns * SLOTS > peel:
                    with repeat(sp, turns - peel // SLOTS, {pairs: SLOTS}) as i:
                        for j in range(SLOTS):
                            load(src[i * SLOTS + (peel + j)])
                for j in range(turns * SLOTS, n):
                    load(src[j])

            stream(tok, 8)
            stream(feat, 14)
            stream(proj, 4)
            stream(wout, 4)
            stream(gateup, 22)
            stream(down, 11)
            sp.wait_ge(d_drained, D_AT["down"] + 4)
            sp.dma_start(pool_wt, pool_w[:, :, :]).then_inc(sem("pool_w_in"), 16)
            sp.dma_start(w_dts, w_dt[:, :, :]).then_inc(sem("w_dt_in"), 16)
            sp.dma_start(keysT, keys[:, :, :]).then_inc(sem("keys_in"), 16)
            stream(win2, 12)
            stream(wout2, 6)
            stream(query, 8)
            stream(expert_down, 64)
            stream(expert_up, 64)
            sp.wait_ge(sem("y_ready"), KC)
            sp.dma_start(out[:, :, :], hT[:, :, :]).then_inc(sem("out_stored"), 16)
            sp.wait_ge(sem("out_stored"), 16)

        @block.gpsimd
        def _(pool):
            own = Own(pool, sem("pool_own"))
            own(nc.gpsimd.memset(ident[:, :], 0.0))
            own(nc.gpsimd.affine_select(out=ident[:, :], in_=ident[:, :], compare_op=ALU.not_equal, fill=1.0,
                                        base=0, pattern=[[-1, P]], channel_multiplier=1))
            own(nc.gpsimd.memset(mask_ts[:, :], 0.0))
            own(nc.gpsimd.memset(mask_st[:, :], 0.0))
            own(nc.gpsimd.affine_select(out=mask_ts[:, P:T], in_=mask_ts[:, P:T], compare_op=ALU.is_ge, fill=FAR,
                                        base=0, pattern=[[-1, P]], channel_multiplier=1))
            own(nc.gpsimd.affine_select(out=mask_st[:, 0:P], in_=mask_st[:, 0:P], compare_op=ALU.is_ge, fill=FAR,
                                        base=0, pattern=[[1, P]], channel_multiplier=-1))
            nc.gpsimd.memset(ones[:, :], 1.0).then_inc(sem("consts"), 1)

            n = 0
            for src in (ada, ada2):
                for j in range(48):
                    s = n % ADA_SLOTS
                    if n >= ADA_SLOTS:
                        pool.wait_ge(ada_used, n - ADA_SLOTS + 1)
                    pool.dma_start(ada_ring[:, s, :], src[j]).then_inc(ada_full[s], 16)
                    n += 1
            pool.wait_ge(d_drained, D_AT["down"] + 4)
            nc.gpsimd.iota(inv_t, [[1, T]], base=1, channel_multiplier=0,
                           allow_small_or_imprecise_dtypes=True).then_inc(sem("t_row"), 1)
            for g in range(SG):
                pool.wait_ge(d_drained, D_AT["cb"] + g + 1)
                for a in (0, 2 * P):
                    nc.gpsimd.affine_select(out=cbT[:, g, a:a + P], in_=cbT[:, g, a:a + P], compare_op=ALU.is_ge,
                                            fill=0.0, base=0, pattern=[[1, P]],
                                            channel_multiplier=-1).then_inc(sem("cb_masked"), 1)
            pool.wait_ge(sem("h_ready"), 4 * KC)
            nc.gpsimd.iota(iota_k, [[1, NK]], base=0, channel_multiplier=0,
                           allow_small_or_imprecise_dtypes=True).then_inc(sem("iota"), 1)

        @block.scalar
        def _(act):
            A = Empty(act, psA, a_ready, a_drained)
            own = Own(act, sem("act_own"))
            act.wait_ge(sem("c_in"), 32)
            nc.scalar.activation(c_row[:, :, :], c_row[:, :, :], ACT.Silu).then_inc(sem("c_act"), 1)

            def norm(src, sq, width, gains=None, shifts=None, dst=None, done=None):
                nc.scalar.activation(sq, src, ACT.Square).then_inc(sem("sq_ready"), 1)
                b = A.bank()
                A.free(nc.scalar.activation(rms[:, :], b[:, 0:T], ACT.Sqrt, bias=eps[:, 0:1], scale=1.0 / width))
                norm.n += 1
                if dst is None:
                    return
                act.wait_ge(sem("xn_ready"), norm.n)
                for j in range(KC):
                    nc.scalar.activation(dst[:, j, :], sq[:, j, :], ACT.Identity,
                                         bias=0.0 if shifts is None else shifts[:, j:j + 1],
                                         scale=gains[:, j:j + 1]).then_inc(done, 1)
            norm.n = 0

            act.wait_ge(sem("x_in"), 16)
            act.wait_ge(sem("eps_set"), 1)
            norm(xT[:, :, :], xn, D, scale_cols[:, 0, :], mods[:, 0:KC], hT, sem("h_ready"))

            def log1p_exp(k):
                n = MH if k == 0 else SH
                act.wait_ge(sem("row_abs"), k + 1)
                nc.scalar.activation(r_e[0:n, :], r_abs[0:n, :], ACT.Exp, scale=-1.0).then_inc(sem("row_exp"), 1)
                act.wait_ge(sem("row_u"), k + 1)
                nc.scalar.activation(r_l[0:n, :], r_u[0:n, :], ACT.Ln).then_inc(sem("row_ln"), 1)

            log1p_exp(0)
            act.wait_ge(sem("m_rows"), 1)
            nc.scalar.activation(r_e[0:MH, :], r_t[0:MH, :], ACT.Exp, scale=-1.0).then_inc(sem("exp_m"), 1)
            act.wait_ge(sem("angles"), 1)
            nc.scalar.activation(trig[:, 0:2, :, :], trig[:, 0:2, :, :], ACT.Sin).then_inc(sem("trig"), 1)

            def drain_feat(j):
                A.free(nc.scalar.activation(zT[:, j, :], A.bank()[:, 0:T], ACT.Identity,
                                            bias=cols[:, bass.ds(j + COLS["b_feat"][0], 1)]))
            with repeat(act, 3, {A.count: 8}) as i:
                for j in range(8):
                    drain_feat(i * 8 + j)
            for j in range(24, Z_N):
                drain_feat(j)
            act.wait_ge(a_drained, A_AT["feat"] + Z_N)
            nc.scalar.activation(zT[:, Z_MO:Z_N, :], zT[:, Z_MO:Z_N, :], ACT.Sigmoid).then_inc(sem("sig_ready"), 1)
            for j in range(2 * MH):
                act.wait_ge(sem("conv_ready"), j + 1)
                nc.scalar.activation(convT[:, j, :], convT[:, j, :], ACT.Silu,
                                     bias=col("conv_b", j)).then_inc(sem("m_qk"), 1)
            for j in range(8):
                A.free(nc.scalar.copy(qkT[:, j % 2, j // 2, :], A.bank()[:, 0:T]))
            act.wait_ge(sem("nmx"), 1)
            for h in range(AH):
                for t in range(NT):
                    p = probs[:, h, 0:P] if t == 0 else probs[:, h, P:3 * P]
                    k = h * NT + t
                    nc.scalar.activation(p, p, ACT.Exp, bias=nmx[:, k:k + 1], scale=AD ** -0.5,
                                         accum_out=sums[:, k:k + 1]).then_inc(sem("exps"), 1)
            for h in range(MH):
                act.wait_ge(sem("m_args"), h + 1)
                for s in range(NT):
                    a = mw[:, h, 0:T] if s == 0 else mw[:, h, T:3 * P]
                    nc.scalar.activation(a, a, ACT.Exp, bias=m_cols[:, 0, h, s:s + 1]).then_inc(sem("m_w"), 1)
            for h in range(AH):
                A.free(nc.scalar.copy(probsT[:, h, :], A.bank()[:, 0:3 * P]))
            for j in range(4):
                A.free(nc.scalar.copy(yaT[:, j, :], A.bank()[:, 0:T]))
            act.wait_ge(sem("m_ms"), 1)
            nc.scalar.activation(m_stat[:, 3, :], m_stat[:, 2, :], ACT.Sqrt, bias=eps[:, 0:1],
                                 scale=1.0 / MD).then_inc(sem("m_rms"), 1)

            act.wait_ge(d_drained, D_AT["wout"] + 8)
            norm(xT[:, :, :], xn, D, scale_cols[:, 1, :], mods[:, 3 * KC:4 * KC], hT, sem("h_ready"))

            def drain_gate(j):
                A.free(nc.scalar.activation(fT[:, j, :], A.bank()[:, 0:T], ACT.Silu))
            with repeat(act, 5, {A.count: 4}) as i:
                for j in range(4):
                    drain_gate(i * 4 + j)
            for j in range(20, FC):
                drain_gate(j)
            act.wait_ge(d_drained, D_AT["down"] + 4)
            norm(xT[:, :, :], xn2, D, col("normf", 0, KC), None, xT, sem("x_normed"))
            act.wait_ge(sem("x_normed"), KC)
            norm(xT[:, :, :], xn2, D, scale_cols[:, 0, :], mods[:, 0:KC], hT, sem("h_ready"))

            def drain_win2(j):
                A.free(nc.scalar.copy(z2T[:, j, :], A.bank()[:, 0:T]))
            with repeat(act, 3, {A.count: 8}) as i:
                for j in range(8):
                    drain_win2(i * 8 + j)
            nc.scalar.activation(a_col[0:SH, 0:1], col("a_log", parts=SH), ACT.Exp).then_inc(sem("a_exp"), 1)
            log1p_exp(1)
            act.wait_ge(a_drained, A_AT["win2"] + MIXC)
            nc.scalar.activation(z2T[:, NPOOL:MIXC, :], z2T[:, NPOOL:MIXC, :], ACT.Silu).then_inc(sem("z_silu"), 1)
            for j in range(XBC):
                act.wait_ge(sem("conv2_ready"), j + 1)
                nc.scalar.activation(xbcT[:, j, :], xbcT[:, j, :], ACT.Silu,
                                     bias=col("conv_b2", j)).then_inc(sem("xbc"), 1)
            for h in range(SH):
                act.wait_ge(sem("ssd_args"), h + 1)
                nc.scalar.activation(ssd_w[:, h % 4, :], ssd_w[:, h % 4, :], ACT.Exp).then_inc(sem("ssd_exp"), 1)
            act.wait_ge(sem("ssd_y"), KC)
            norm(mixT[:, NPOOL:MIXC, :], xn2, D)
            act.wait_ge(d_drained, D_AT["wout2"] + 4)
            norm(xT[:, :, :], xn2, D, scale_cols[:, 1, :], mods[:, 3 * KC:4 * KC], hT, sem("h_ready"))
            for j in range(2 * QH):
                b = A.bank()
                if j >= 4:
                    act.wait_ge(d_ready, D_AT["scores"] + j - 4 + 1)
                A.free(nc.scalar.copy(xn2[:, j % 4, :], b[:, 0:T]))
            act.wait_ge(d_drained, D_AT["scores"] + 2 * QH)
            with repeat(act, 16, {A.count: 8}) as i:
                for j in range(8):
                    A.free(nc.scalar.activation(U[:, i * 8 + j, :], A.bank()[:, 0:T], ACT.Gelu))
            act.wait_ge(sem("gate_args"), 1)
            nc.scalar.activation(picked[:, 2, :], picked[:, 2, :], ACT.Exp).then_inc(sem("gate_exp"), 1)
            act.wait_ge(d_drained, D_AT["expert_up"] + 4)
            norm(xT[:, :, :], U[:, 0:KC, :], D, col("norm_final", 0, KC), None, hT, sem("y_ready"))

        @block.vector
        def _(dve):
            Dr = Empty(dve, psD, d_ready, d_drained)
            own = Own(dve, sem("dve_own"))
            V = nc.vector
            V.memset(eps[:, :], EPS).then_inc(sem("eps_set"), 1)
            own(V.memset(v_ext[:, :, :, MD:MD + 1], 1.0))
            dve.wait_ge(sem("consts"), 1)
            dve.wait_ge(sem("cols_in"), 16)

            ada_n = Count()

            def ada_blocks(vec, first):
                for k in range(KC):
                    s = ada_n.n % ADA_SLOTS
                    dve.wait_ge(ada_full[s], 16 * (ada_n.n // ADA_SLOTS + 1))
                    own(V.scalar_tensor_tensor(out=ada_ring[:, s, :], in0=ada_ring[:, s, :], scalar=1.0,
                                               in1=c_row[:, first, :], op0=ALU.mult, op1=ALU.mult,
                                               accum_out=mods[:, vec * KC + k:vec * KC + k + 1]))
                    ada_n.n += 1
                    dve.sem_inc(ada_used, 1)

            def ada_vectors(lo, hi, bias, which):
                for v in range(lo, hi):
                    ada_blocks(v, which)
                own(V.tensor_tensor(mods[:, lo * KC:hi * KC], mods[:, lo * KC:hi * KC],
                                    col(bias, lo * KC, (hi - lo) * KC), ALU.add))

            def gains(k, vec, name):
                own(V.scalar_tensor_tensor(out=scale_cols[:, k, :], in0=mods[:, vec * KC:(vec + 1) * KC], scalar=1.0,
                                           in1=col(name, 0, KC), op0=ALU.add, op1=ALU.mult))

            def norm(src, dst):
                norm.n += 1
                dve.wait_ge(a_drained, A_AT[norm.names[norm.n - 1]] + 1)
                own(V.reciprocal(rinv[:, :], rms[:, :]))
                V.tensor_tensor(dst, src, rinv[:, :].unsqueeze(1).broadcast_to([P, KC, T]),
                                ALU.mult).then_inc(sem("xn_ready"), 1)
            norm.n = 0
            norm.names = ("ssq1", "ssq2", "ssqf", "ssq_mix", "ssq_ssd", "ssq_ffn", "ssq_final")

            dve.wait_ge(sem("c_act"), 1)
            ada_vectors(0, 2, "ada_b", 0)
            gains(0, 1, "norm1")
            norm(xT[:, :, :], xn)

            own(V.memset(r_s[0:SH, :], 0.0))
            Dr.free(V.tensor_scalar(r_i[0:MH, :], Dr.bank()[0:MH, 0:T], col("b_i", parts=MH), None, ALU.add))
            Dr.free(V.tensor_scalar(r_f[0:MH, :], Dr.bank()[0:MH, 0:T], col("b_f", parts=MH), None, ALU.add),
                    settle=True)

            def log1p_exp(k, n):
                V.scalar_tensor_tensor(out=r_abs[0:n, :], in0=r_f[0:n, :], scalar=-1.0, in1=r_f[0:n, :],
                                       op0=ALU.mult, op1=ALU.max).then_inc(sem("row_abs"), 1)
                dve.wait_ge(sem("row_exp"), k + 1)
                V.tensor_scalar(r_u[0:n, :], r_e[0:n, :], 1.0, None, ALU.add).then_inc(sem("row_u"), 1)
                dve.wait_ge(sem("row_u"), k + 1)
                own(V.tensor_scalar(r_t[0:n, :], r_u[0:n, :], -1.0, None, ALU.add))
                own(V.tensor_tensor(r_t[0:n, :], r_e[0:n, :], r_t[0:n, :], ALU.subtract))
                own(V.reciprocal(r_abs[0:n, :], r_u[0:n, :]))
                own(V.tensor_tensor(r_t[0:n, :], r_t[0:n, :], r_abs[0:n, :], ALU.mult))
                dve.wait_ge(sem("row_ln"), k + 1)
                own(V.tensor_tensor(r_l[0:n, :], r_l[0:n, :], r_t[0:n, :], ALU.add))

            log1p_exp(0, MH)
            R = slice(0, MH)
            own(V.scalar_tensor_tensor(out=r_f[R, :], in0=r_f[R, :], scalar=0.0, in1=r_l[R, :],
                                       op0=ALU.min, op1=ALU.subtract))
            own(V.tensor_tensor_scan(r_abs[R, :], r_f[R, :], r_s[R, :], 0.0, ALU.add, ALU.add))
            own(V.tensor_tensor(r_i[R, :], r_i[R, :], r_abs[R, :], ALU.subtract))
            own(V.tensor_tensor_scan(r_u[R, :], r_i[R, :], r_i[R, :], 0.0, ALU.max, ALU.max))
            V.tensor_tensor(r_t[R, :], r_abs[R, :], r_u[R, :], ALU.add).then_inc(sem("m_rows"), 1)
            V.tensor_scalar(r_f[R, :], r_u[R, :], -1.0, None, ALU.mult).then_inc(sem("neg_m"), 1)

            dve.wait_ge(sem("pos_in"), 16)
            own(V.tensor_copy(posf, pos_i[:, :]))
            for t in range(NT):
                own(V.tensor_scalar(trig[:, 2, t, :], col("inv_freq", 0, 32), posf[:, t:t + 1], None, ALU.mult))
            ang = trig[:, 2, :, :]
            for k, quarter in ((0, 0.25), (1, 0.0)):
                r = trig[:, k, :, :]
                own(V.tensor_scalar(trig[:, 3, :, :], ang, 1.0 / 6.283185307179586, quarter, ALU.mult, ALU.add))
                own(V.tensor_scalar(trig[:, 3, :, :], trig[:, 3, :, :], MAGIC, -MAGIC, ALU.add, ALU.add))
                for n, piece in enumerate(TWO_PI):
                    own(V.scalar_tensor_tensor(out=r, in0=trig[:, 3, :, :], scalar=-piece, in1=ang if n == 0 else r,
                                               op0=ALU.mult, op1=ALU.add))
                if quarter:
                    own(V.tensor_scalar(r, r, 1.5707963267948966, None, ALU.add))
                last = V.tensor_scalar(r, r, PI_BELOW, -PI_BELOW, ALU.min, ALU.max)
                if k == 0:
                    own(last)
            last.then_inc(sem("angles"), 1)

            dve.wait_ge(sem("b_tok_in"), 16)
            for b in range(TOK_BLOCKS):
                for t in range(NT):
                    if b < 3:
                        Dr.free(V.tensor_tensor(toks[:, t, b * 512:(b + 1) * 512], Dr.bank(), b_tok[:, b, :], ALU.add),
                                settle=True)
                    else:
                        Dr.free(V.tensor_tensor(v_ext[:, t, :, 0:MD],
                                                Dr.bank().rearrange("p (h d) -> p h d", h=MH),
                                                b_tok[:, b, :].rearrange("p (h d) -> p h d", h=MH), ALU.add))
            dve.wait_ge(sem("trig"), 1)
            for t in range(NT):
                halves = toks[:, t, 0:1024].rearrange("p (h z d) -> p z h d", z=2, d=32)
                cos = trig[:, 0, t, :].unsqueeze(1).broadcast_to([P, 16, 32])
                sin = trig[:, 1, t, :].unsqueeze(1).broadcast_to([P, 16, 32])
                for z in range(2):
                    V.tensor_tensor(turn[:, 0, z, :, :], halves[:, z, :, :], cos, ALU.mult)
                    own(V.tensor_tensor(turn[:, 1, z, :, :], halves[:, z, :, :], sin, ALU.mult))
                V.tensor_tensor(halves[:, 0, :, :], turn[:, 0, 0, :, :], turn[:, 1, 1, :, :],
                                ALU.subtract).then_inc(sem("roped"), 1)
                V.tensor_tensor(halves[:, 1, :, :], turn[:, 0, 1, :, :], turn[:, 1, 0, :, :],
                                ALU.add).then_inc(sem("roped"), 1)
                dve.wait_ge(sem("roped"), 2 * t + 2)

            ada_vectors(2, 6, "ada_b", 0)
            gains(1, 4, "norm2")

            def conv(j, src, dst, weights, ready, first):
                dve.wait_ge(a_drained, j + (first + 1))
                w = COLS[weights][0]

                def tap(k):
                    return cols[:, bass.ds(j * CONV + (w + k), 1)]
                own(V.tensor_scalar(dst[:, j, :], src[:, j, :], tap(CONV - 1), None, ALU.mult))
                for back in range(1, CONV):
                    last = V.scalar_tensor_tensor(out=dst[:, j, back:T], in0=src[:, j, 0:T - back],
                                                  scalar=tap(CONV - 1 - back), in1=dst[:, j, back:T],
                                                  op0=ALU.mult, op1=ALU.add)
                    if back < CONV - 1:
                        own(last)
                last.then_inc(ready, 1)
            with repeat(dve, 2 * MH, {own.count: CONV - 1}) as j:
                conv(j, zT[:, 0:2 * MH, :], convT, "conv_w", sem("conv_ready"), A_AT["feat"])

            b = Dr.bank()
            Dr.free(V.tensor_copy(m_cols.rearrange("p k h t -> p k t h"),
                                  b[:, 0:16].rearrange("p (k t h) -> p k t h", k=2, t=NT)), settle=True)
            dve.sem_inc(sem("m_cols"), 1)

            for h in range(AH):
                b = Dr.bank()
                own(V.tensor_tensor_reduce(probs[:, h, 0:P], b[:, 0:P], mask_ts[:, P:T], 1.0, LOWEST,
                                           ALU.add, ALU.max, mx[:, 2 * h:2 * h + 1]))
                Dr.free(V.tensor_tensor_reduce(probs[:, h, P:3 * P], b[:, P:3 * P], mask_ts[:, :], 1.0, LOWEST,
                                               ALU.add, ALU.max, mx[:, 2 * h + 1:2 * h + 2]), settle=True)
            V.tensor_scalar(nmx, mx, -(AD ** -0.5), None, ALU.mult).then_inc(sem("nmx"), 1)
            for h in range(MH):
                b = Dr.bank()
                V.tensor_tensor(mw[:, h, T:3 * P], b[:, P:T], mask_st[:, 0:P], ALU.add)
                Dr.free(V.tensor_tensor(mw[:, h, 0:T], b[:, 0:T], mask_st[:, :], ALU.add), settle=True)
                dve.sem_inc(sem("m_args"), 1)
            dve.wait_ge(sem("exps"), AH * NT)
            own(V.reciprocal(rsums, sums))
            for h in range(AH):
                for t in range(NT):
                    p = probs[:, h, 0:P] if t == 0 else probs[:, h, P:3 * P]
                    k = h * NT + t
                    V.tensor_scalar(p, p, rsums[:, k:k + 1], None, ALU.mult).then_inc(sem("probs"), 1)
            for h in range(MH):
                dve.wait_ge(sem("m_w"), 2 * h + 2)
                Dr.free(V.scalar_tensor_tensor(out=mw[:, h, :], in0=Dr.bank()[:, 0:3 * P], scalar=MD ** -0.5,
                                               in1=mw[:, h, :], op0=ALU.mult, op1=ALU.mult))
            for h in range(MH):
                Dr.free(V.tensor_copy(nd[:, 2 * h:2 * h + 2, :],
                                      Dr.bank()[:, 0:2 * (MD + 1)].rearrange("p (t d) -> p t d", t=NT)), settle=True)
            den = nd[:, :, MD:MD + 1].rearrange("p a b -> p (a b)")
            own(V.scalar_tensor_tensor(out=m_stat[:, 0, :], in0=den, scalar=-1.0, in1=den,
                                       op0=ALU.mult, op1=ALU.max))
            own(V.tensor_tensor(m_stat[:, 0, :], m_stat[:, 0, :], m_cols[:, 1, :, :].rearrange("p h t -> p (h t)"),
                                ALU.max))
            own(V.reciprocal(m_stat[:, 1, :], m_stat[:, 0, :]))
            own(V.tensor_tensor(nd[:, :, 0:MD], nd[:, :, 0:MD],
                                m_stat[:, 1, :].unsqueeze(2).broadcast_to([P, NT * MH, MD]), ALU.mult))
            for k in range(NT * MH):
                own(V.tensor_tensor_reduce(xn[:, 0, 0:MD], nd[:, k, 0:MD], nd[:, k, 0:MD], 1.0, 0.0,
                                           ALU.mult, ALU.add, m_stat[:, 2, k:k + 1]))
            dve.sem_inc(sem("m_ms"), 1)
            dve.wait_ge(sem("m_rms"), 1)
            own(V.reciprocal(m_stat[:, 4, :], m_stat[:, 3, :]))
            V.tensor_tensor(nd[:, :, 0:MD], nd[:, :, 0:MD],
                            m_stat[:, 4, :].unsqueeze(2).broadcast_to([P, NT * MH, MD]),
                            ALU.mult).then_inc(sem("m_normed"), 1)
            dve.wait_ge(sem("sig_ready"), 1)
            for h in range(MH):
                Dr.free(V.scalar_tensor_tensor(out=ymT[:, h, :], in0=Dr.bank()[:, 0:T], scalar=col("m_norm", h),
                                               in1=zT[:, Z_MO + h, :], op0=ALU.mult, op1=ALU.mult))
            for j in range(KC):
                Dr.free(V.tensor_tensor(mT[:, j, :], Dr.bank()[:, 0:T], zT[:, Z_GA + j, :], ALU.mult))
                Dr.free(V.tensor_tensor(xn[:, j, :], Dr.bank()[:, 0:T], zT[:, Z_GB + j, :], ALU.mult), settle=True)
                V.tensor_tensor(mT[:, j, :], mT[:, j, :], xn[:, j, :], ALU.add).then_inc(sem("merged"), 1)

            def residual(j, bank, vec):
                return V.scalar_tensor_tensor(out=xT[:, j, :], in0=bank, scalar=mods[:, vec * KC + j:vec * KC + j + 1],
                                              in1=xT[:, j, :], op0=ALU.mult, op1=ALU.add)

            def residual_all(vec):
                for k in range(BANKS):
                    b = Dr.bank()
                    residual(2 * k, b[:, 0:T], vec)
                    Dr.free(residual(2 * k + 1, b[:, T:2 * T], vec), settle=True)

            for j in range(KC):
                Dr.free(residual(j, Dr.bank()[:, 0:T], 2), settle=True)
            norm(xT[:, :, :], xn)

            def drain_up(j):
                b = Dr.bank()
                dve.wait_ge(a_drained, j + (A_AT["gate"] + 1))
                Dr.free(V.tensor_tensor(fT[:, j, :], b[:, 0:T], fT[:, j, :], ALU.mult))
            with repeat(dve, 5, {Dr.count: 4}) as i:
                for j in range(4):
                    drain_up(i * 4 + j)
            for j in range(20, FC):
                drain_up(j)
            residual_all(5)
            norm(xT[:, :, :], xn2)
            ada_vectors(0, 6, "ada_b2", 1)
            gains(0, 1, "norm_mix")
            norm(xT[:, :, :], xn2)
            gains(1, 4, "norm_ffn")

            S = slice(0, SH)
            own(V.memset(r_s[S, :], 0.0))
            Dr.free(V.tensor_scalar(r_f[S, :], Dr.bank()[S, 0:T], col("dt_bias", parts=SH), None, ALU.add),
                    settle=True)
            log1p_exp(1, SH)
            own(V.scalar_tensor_tensor(out=r_i[S, :], in0=r_f[S, :], scalar=0.0, in1=r_l[S, :],
                                       op0=ALU.max, op1=ALU.add))
            dve.wait_ge(sem("a_exp"), 1)
            own(V.tensor_scalar(r_t[S, :], r_i[S, :], a_col[S, 0:1], -1.0, ALU.mult, ALU.mult))
            V.tensor_tensor_scan(r_u[S, :], r_t[S, :], r_s[S, :], 0.0, ALU.add, ALU.add).then_inc(sem("dt_rows"), 1)

            dve.wait_ge(sem("t_row"), 1)
            own(V.memset(pool_a[:, :, 0:16], 0.0))
            own(V.memset(pool_b[:, :, 0:16], 0.0))
            dve.wait_ge(a_drained, A_AT["win2"] + NPOOL)
            own(V.tensor_copy(pool_a[:, :, 16:PADDED], z2T[:, 0:NPOOL, :]))
            bufs = [pool_a, pool_b]
            for g in range(NPOOL):
                w = POOLS[g] // 2
                a, b = bufs[g % 2], bufs[(g + 1) % 2]
                own(V.tensor_tensor(b[:, g:NPOOL, 16:PADDED], a[:, g:NPOOL, 16:PADDED],
                                    a[:, g:NPOOL, 16 - w:PADDED - w], ALU.add))
            own(V.reciprocal(inv_t, inv_t))
            for g in range(NPOOL):
                win = bufs[(g + 1) % 2][:, g, 16:PADDED]
                own(V.scalar_tensor_tensor(out=win, in0=inv_t, scalar=1.0 / POOLS[g], in1=win,
                                           op0=ALU.max, op1=ALU.mult))
                V.tensor_tensor(win, win, z2T[:, g, :], ALU.subtract).then_inc(sem("pooled"), 1)
            with repeat(dve, XBC, {own.count: CONV - 1}) as j:
                conv(j, z2T[:, MIXC:MIXC + XBC, :], xbcT, "conv_w2", sem("conv2_ready"), A_AT["win2"] + MIXC)
            for g in range(NPOOL):
                Dr.free(V.tensor_scalar(mixT[:, g, :], Dr.bank()[:, 0:T], col("pool_b", g), col("pool_scale", g),
                                        ALU.add, ALU.mult))
            b = Dr.bank()
            Dr.free(V.tensor_copy(s_cols.rearrange("p k t h -> p (k t h)"), b[:, 0:4 * SH]), settle=True)
            for j in range(4):
                t, half = divmod(j, 2)
                Dr.free(V.tensor_copy(xs_tok[:, t, half * 512:(half + 1) * 512], Dr.bank()))
            for g in range(SG):
                Dr.free(V.tensor_copy(cbT[:, g, :], Dr.bank()[:, 0:3 * P]))

            def ssd_args(h):
                b = Dr.bank()
                own(V.tensor_scalar(ssd_w[:, h % 4, 0:T], b[:, 0:T], s_cols[:, 0, 0, h:h + 1], 0.0,
                                    ALU.subtract, ALU.min))
                Dr.free(V.tensor_scalar(ssd_w[:, h % 4, T:3 * P], b[:, P:T], s_cols[:, 0, 1, h:h + 1], 0.0,
                                        ALU.subtract, ALU.min), settle=True)
                dve.sem_inc(sem("ssd_args"), 1)

            def ssd_weights(h):
                g = h // (SH // SG)
                dve.wait_ge(sem("cb_masked"), 2 * g + 2)
                dve.wait_ge(sem("ssd_exp"), h + 1)
                for s, (a, e) in enumerate(((0, T), (T, 3 * P))):
                    w = ssd_w[:, h % 4, a:e]
                    V.scalar_tensor_tensor(out=w, in0=w, scalar=s_cols[:, 1, s, h:h + 1], in1=cbT[:, g, a:e],
                                           op0=ALU.mult, op1=ALU.mult).then_inc(sem("ssd_w"), 1)

            def ssd_out(j):
                Dr.free(V.scalar_tensor_tensor(out=mixT[:, NPOOL + j, :], in0=xbcT[:, j, :], scalar=col("d_skip", j),
                                               in1=Dr.bank()[:, 0:T], op0=ALU.mult, op1=ALU.add), settle=True)
                V.tensor_tensor(mixT[:, NPOOL + j, :], mixT[:, NPOOL + j, :], z2T[:, NPOOL + j, :],
                                ALU.mult).then_inc(sem("ssd_y"), 1)
            dve.wait_ge(sem("z_silu"), 1)
            dve.wait_ge(sem("xbc"), XBC)
            for j in range(KC + 1):
                if j < KC:
                    ssd_args(2 * j)
                    ssd_args(2 * j + 1)
                if j >= 1:
                    ssd_weights(2 * j - 2)
                    ssd_weights(2 * j - 1)
                    ssd_out(j - 1)
            dve.wait_ge(a_drained, A_AT["ssq_ssd"] + 1)
            norm.n += 1
            own(V.reciprocal(rinv[:, :], rms[:, :]))
            for j in range(KC):
                y = mixT[:, NPOOL + j, :]
                last = V.scalar_tensor_tensor(out=y, in0=y, scalar=col("ssd_norm", j), in1=rinv[:, :],
                                              op0=ALU.mult, op1=ALU.mult)
                last.then_inc(sem("ssd_normed"), 1)
            dve.sem_inc(sem("xn_ready"), 1)
            residual_all(2)
            norm(xT[:, :, :], xn2)

            for j in range(2 * QH):
                Dr.free(V.tensor_copy(scores[:, :, j, :], Dr.bank()[:, 0:NT * NK].rearrange("p (t n) -> p t n", t=NT)),
                        settle=j == 2 * QH - 1)
            dve.wait_ge(sem("h_ready"), 4 * KC)

            def apart(ins):
                own(ins)
                dve.sem_inc(sem("top_steps"), 1)

            def top16(vals, ids, src, spare):
                apart(V.max(vals[:, 0:8], src))
                V.max_index(ids[:, 0:8], vals[:, 0:8], src)
                apart(V.match_replace(spare, vals[:, 0:8], src, LOWEST))
                apart(V.max(vals[:, 8:16], spare))
                apart(V.max_index(ids[:, 8:16], vals[:, 8:16], spare))

            with repeat(dve, NT * QH, {own.count: 1 + 4 * 3 + 1 + 1 + 5}) as k:
                flat = scores.rearrange("p t j n -> p (t j) n")
                apart(V.tensor_copy(work, flat[:, bass.ds(k * 2, 2), :]))
                for z in range(2):
                    top16(v16[:, z, :], i16[:, z, :], work[:, z, :], work2)
                own(V.tensor_copy(idx[:, k, :, :], i16[:, 0:2, :]))
                apart(V.tensor_tensor(cand[:, :, :], v16[:, 0, :].unsqueeze(2).broadcast_to([P, TOPK, TOPK]),
                                    v16[:, 1, :].unsqueeze(1).broadcast_to([P, TOPK, TOPK]), ALU.add))
                top16(v16[:, 0, :], i16[:, 2, :], cand[:, :, :].rearrange("p a b -> p (a b)"), cand2[:, :])
                own(V.tensor_copy(top_v[:, k, :], v16[:, 0, :]))
                own(V.tensor_scalar(i16[:, 0, :], i16[:, 2, :], 4, None, ALU.logical_shift_right))
                own(V.tensor_scalar(i16[:, 1, :], i16[:, 2, :], 15, None, ALU.bitwise_and))
                own(V.tensor_copy(pick_a[:, k, :], i16[:, 0, :]))
                own(V.tensor_copy(pick_b[:, k, :], i16[:, 1, :]))
            dve.wait_ge(sem("iota"), 1)
            for z, pick in ((0, pick_a), (1, pick_b)):
                own(V.tensor_tensor(eq, pick.rearrange("p a k -> p (a k)").unsqueeze(2).broadcast_to([P, 256, TOPK]),
                                    iota_k[:, 0:TOPK].unsqueeze(1).broadcast_to([P, 256, TOPK]), ALU.is_equal))
                own(V.tensor_tensor(eq.rearrange("p (a k) i -> p a k i", k=TOPK),
                                    eq.rearrange("p (a k) i -> p a k i", k=TOPK),
                                    idx[:, :, z, :].unsqueeze(2).broadcast_to([P, NT * QH, TOPK, TOPK]), ALU.mult))
                own(V.tensor_reduce(picked[:, z, :], eq, AX.X, ALU.add))
            gates = picked[:, 2, :].rearrange("p (a k) -> p a k", k=TOPK)
            V.tensor_tensor(gates, top_v, top_v[:, :, 0:1].broadcast_to([P, NT * QH, TOPK]),
                            ALU.subtract).then_inc(sem("gate_args"), 1)
            dve.wait_ge(sem("gate_exp"), 1)
            own(V.tensor_reduce(mx, gates, AX.X, ALU.add))
            own(V.reciprocal(rsums, mx))
            V.tensor_tensor(gates, gates, rsums.unsqueeze(2).broadcast_to([P, NT * QH, TOPK]),
                            ALU.mult).then_inc(sem("picked"), 1)
            for z in range(3):
                Dr.free(V.tensor_copy(picksT[:, z, :], Dr.bank()[:, 0:T]), settle=True)

            hots = Count()

            def one_hots(t):
                n = hots.n
                hots.n += 1
                if n >= ONEHOTS:
                    dve.wait_ge(d_ready, hots.value(ONEHOTS) + D_AT["spread"])
                h = hot[:, n % ONEHOTS, :, :]
                V.tensor_scalar(h[:, 0, :], iota_k, picksT[:, 0, bass.ds(t, 1)], None,
                                ALU.is_equal).then_inc(sem("one_hots"), 1)
                V.tensor_scalar(h[:, 1, :], iota_k, picksT[:, 1, bass.ds(t, 1)], picksT[:, 2, bass.ds(t, 1)],
                                ALU.is_equal, ALU.mult).then_inc(sem("one_hots"), 1)

            def gate_experts(t):
                b = Dr.bank()
                u = U[:, :, bass.ds(t, 1)].rearrange("p e t -> p (e t)")
                Dr.free(V.tensor_tensor(u, b[:, 0:NK], u, ALU.mult))
            dve.wait_ge(a_drained, A_AT["experts"] + P)
            for t in range(4):
                one_hots(t)
            with repeat(dve, (T - 4) // 4, {hots: 4, Dr.count: 4}) as i:
                for t in range(4):
                    gate_experts(i * 4 + t)
                    one_hots(i * 4 + (t + 4))
            for t in range(T - 4, T):
                gate_experts(t)
            dve.wait_ge(d_drained, D_AT["spread"] + T)
            residual_all(5)
            norm(xT[:, :, :], U[:, 0:KC, :])

        @block.tensor
        def _(pe):
            A = Fill(pe, psA, a_ready, a_drained)
            Dr = Fill(pe, psD, d_ready, d_drained)
            mm = nc.tensor.matmul
            pairs = Count()
            norms = Count()

            def pair():
                n = pairs.n
                pairs.n += 1
                s = n % SLOTS
                at = 16 * (n // SLOTS + 1)
                pe.wait_ge(full[s], at if pairs.loop is None else pairs.loop * (16 // SLOTS) + at)
                return ring[:, s, :, :]

            def begun(ins):
                if pairs.n > 1:
                    ins.then_inc(pair_used, 1)

            def ssq(src):
                norms.n += 1
                pe.wait_ge(sem("sq_ready"), norms.n)
                b = A.bank()
                for j in range(KC):
                    last = mm(b[:, 0:T], ones[:, :], src[:, j, :], start=j == 0, stop=j == KC - 1)
                A.full(last)

            def blocks(R, w, rhs, n=KC, opens=False):
                b = R.bank()
                for k in range(n):
                    last = mm(b[:, 0:T], w[:, k * P:(k + 1) * P], rhs[:, k, :], start=k == 0, stop=k == n - 1)
                    if k == 0 and opens:
                        begun(last)
                R.full(last)

            def columns(R, turns, rest, rhs, second=None):
                def one():
                    w = pair()
                    for u in range(2):
                        blocks(R if u == 0 or second is None else second, w[:, u, :], rhs, opens=u == 0)
                per = {pairs: SLOTS, R.count: 2 * SLOTS if second is None else SLOTS}
                if second is not None:
                    per[second.count] = SLOTS
                if R.count.n < BANKS:
                    turns -= 1
                    for _ in range(SLOTS):
                        one()
                with repeat(pe, turns, per):
                    for _ in range(SLOTS):
                        one()
                for _ in range(rest):
                    one()

            def row_blocks(npairs, rhs, first_wait=None):
                banks = [Dr.bank() for _ in range(BANKS)]
                rows = 2 * npairs

                def one(k, first, last_pair):
                    w = pair()
                    for u in range(2):
                        for n in range(KC):
                            last = mm(banks[n // 2][:, (n % 2) * T:(n % 2 + 1) * T], w[:, u, n * P:(n + 1) * P],
                                      rhs[:, k * 2 + u, :], start=first and u == 0 and n % 2 == 0,
                                      stop=last_pair and u == 1, skip_group_check=True)
                            if u == 0 and n == 0:
                                begun(last)
                            if last_pair and u == 1 and n % 2 == 1:
                                Dr.full(last)
                head = 1
                turns, rest = divmod(npairs - 2, SLOTS)
                one(0, True, False)
                if turns:
                    with repeat(pe, turns, {pairs: SLOTS}) as i:
                        for j in range(SLOTS):
                            one(i * SLOTS + (head + j), False, False)
                for j in range(rest):
                    one(head + turns * SLOTS + j, False, False)
                one(npairs - 1, False, True)

            pe.wait_ge(sem("consts"), 1)
            ssq(xn)
            pe.wait_ge(sem("w_gates_in"), 16)
            pe.wait_ge(sem("h_ready"), KC)
            for g in range(2):
                b = Dr.bank()
                for k in range(KC):
                    last = mm(b[0:MH, 0:T], wg_gates[:, k, g * MH:(g + 1) * MH], hT[:, k, :],
                              start=k == 0, stop=k == KC - 1)
                Dr.full(last)
            for blk in range(TOK_BLOCKS):
                bs = [Dr.bank() for _ in range(NT)]
                for half in range(2):
                    w = pair().rearrange("p a b -> p (a b)").rearrange("p (k n) -> p k n", n=512)
                    for k in range(4):
                        kc = half * 4 + k
                        for t in range(NT):
                            last = mm(bs[t], hT[:, kc, t * P:(t + 1) * P], w[:, k, :], start=kc == 0, stop=kc == KC - 1)
                            if k == 0 and t == 0:
                                begun(last)
                            if kc == KC - 1:
                                Dr.full(last)
            columns(A, 3, 2, hT)

            pe.wait_ge(sem("exp_m"), 1)
            b = Dr.bank()
            for k, src in ((0, r_i), (1, r_e)):
                for t in range(NT):
                    at = (k * NT + t) * MH
                    last = nc.tensor.transpose(b[:, at:at + MH], src[0:MH, t * P:(t + 1) * P], ident[0:MH, 0:MH])
            Dr.full(last)
            pe.wait_ge(sem("roped"), 2 * NT)
            for j in range(8):
                b = A.bank()
                z, pr = j % 2, j // 2
                for t in range(NT):
                    last = nc.tensor.transpose(b[:, t * P:(t + 1) * P],
                                               toks[:, t, z * 512 + pr * P:z * 512 + (pr + 1) * P], ident[:, :])
                A.full(last)
            for h in range(AH):
                pe.wait_ge(a_drained, A_AT["qkT"] + 2 * (h // 2) + 2)
                lo = (h % 2) * AD
                q, k = qkT[lo:lo + AD, 0, h // 2, :], qkT[lo:lo + AD, 1, h // 2, :]
                b = Dr.bank()
                mm(b[:, 0:P], q[:, 0:P], k[:, 0:P], start=True, stop=True)
                Dr.full(mm(b[:, P:3 * P], q[:, P:T], k[:, 0:T], start=True, stop=True))
            pe.wait_ge(sem("neg_m"), 1)
            for h in range(MH):
                b = Dr.bank()
                Dr.full(mm(b[:, 0:T], sel(h, MH), r_f[0:MH, :], start=True, stop=True))
            pe.wait_ge(sem("m_qk"), 2 * MH)
            for h in range(MH):
                q, k = convT[:, h, :], convT[:, MH + h, :]
                b = Dr.bank()
                mm(b[:, 0:T], k[:, 0:P], q, start=True, stop=True)
                Dr.full(mm(b[:, T:3 * P], k[:, P:T], q[:, P:T], start=True, stop=True))
            for h in range(AH):
                pe.wait_ge(sem("probs"), NT * (h + 1))
                b = A.bank()
                for n in range(3):
                    last = nc.tensor.transpose(b[:, n * P:(n + 1) * P],
                                               probs[:, h, (0, P, 2 * P)[n]:(0, P, 2 * P)[n] + P], ident[:, :])
                A.full(last)
            for pr in range(4):
                b = A.bank()
                for z in range(2):
                    h = 2 * pr + z
                    pe.wait_ge(a_drained, A_AT["probsT"] + h + 1)
                    o = b[z * AD:(z + 1) * AD, :]
                    mm(o[:, 0:T], toks[:, 0, 1024 + h * AD:1024 + (h + 1) * AD], probsT[:, h, 0:T],
                       start=True, stop=False, skip_group_check=True)
                    last = mm(o[:, P:T], toks[:, 1, 1024 + h * AD:1024 + (h + 1) * AD], probsT[:, h, T:3 * P],
                              start=False, stop=True, skip_group_check=True)
                A.full(last)
            for h in range(MH):
                pe.wait_ge(d_drained, D_AT["m_scores"] + h + 1)
                b = Dr.bank()
                mm(b[:, 0:MD + 1], mw[:, h, 0:P], v_ext[:, 0, h, :], start=True, stop=True)
                mm(b[:, MD + 1:2 * (MD + 1)], mw[:, h, P:T], v_ext[:, 0, h, :], start=True, stop=False)
                Dr.full(mm(b[:, MD + 1:2 * (MD + 1)], mw[:, h, T:3 * P], v_ext[:, 1, h, :], start=False, stop=True))
            pe.wait_ge(sem("m_normed"), 1)
            for h in range(MH):
                b = Dr.bank()
                for t in range(NT):
                    last = nc.tensor.transpose(b[:, t * P:(t + 1) * P], nd[:, 2 * h + t, 0:MD], ident[:, :])
                Dr.full(last)
            pe.wait_ge(d_drained, D_AT["ymT"] + MH)
            pe.wait_ge(a_drained, A_AT["attn"] + 4)
            for _ in range(4):
                w = pair()
                for u in range(2):
                    blocks(Dr, w[:, u, 0:512], ymT, n=4, opens=u == 0)
                    blocks(Dr, w[:, u, 512:1024], yaT, n=4)
            pe.wait_ge(sem("merged"), KC)
            columns(Dr, 1, 0, mT)
            ssq(xn)
            pe.wait_ge(sem("h_ready"), 2 * KC)
            columns(A, 5, 2, hT, Dr)
            pe.wait_ge(d_drained, D_AT["up"] + FC)
            row_blocks(11, fT)
            ssq(xn2)
            ssq(xn2)
            pe.wait_ge(sem("h_ready"), 3 * KC)
            pe.wait_ge(sem("w_dt_in"), 16)
            b = Dr.bank()
            for k in range(KC):
                last = mm(b[0:SH, 0:T], w_dts[:, k, :], hT[:, k, :], start=k == 0, stop=k == KC - 1)
            Dr.full(last)
            columns(A, 3, 0, hT)
            pe.wait_ge(sem("pool_w_in"), 16)
            for g in range(NPOOL):
                pe.wait_ge(sem("pooled"), g + 1)
                b = Dr.bank()
                Dr.full(mm(b[:, 0:T], pool_wt[:, g, :], (pool_b, pool_a)[g % 2][:, g, 16:PADDED],
                           start=True, stop=True))
            pe.wait_ge(sem("dt_rows"), 1)
            b = Dr.bank()
            for k, src in ((0, r_u), (1, r_i)):
                for t in range(NT):
                    at = (k * NT + t) * SH
                    last = nc.tensor.transpose(b[:, at:at + SH], src[0:SH, t * P:(t + 1) * P], ident[0:SH, 0:SH])
            Dr.full(last)
            pe.wait_ge(sem("xbc"), XBC)
            for j in range(4):
                t, half = divmod(j, 2)
                b = Dr.bank()
                for k in range(4):
                    last = nc.tensor.transpose(b[:, k * P:(k + 1) * P], xbcT[:, half * 4 + k, t * P:(t + 1) * P],
                                               ident[:, :])
                Dr.full(last)
            for g in range(SG):
                bs_, cs_ = xbcT[:, KC + g, :], xbcT[:, KC + SG + g, :]
                b = Dr.bank()
                mm(b[:, 0:T], bs_[:, 0:P], cs_, start=True, stop=True)
                Dr.full(mm(b[:, T:3 * P], bs_[:, P:T], cs_[:, P:T], start=True, stop=True))

            def ssd_decay(h):
                b = Dr.bank()
                Dr.full(mm(b[:, 0:T], sel(h, SH), r_u[0:SH, :], start=True, stop=True))

            def ssd_pair(j):
                b = Dr.bank()
                for z in range(2):
                    h = 2 * j + z
                    pe.wait_ge(sem("ssd_w"), 2 * h + 2)
                    o = b[z * SP:(z + 1) * SP, :]
                    w = ssd_w[:, h % 4, :]
                    mm(o[:, 0:T], xs_tok[:, 0, h * SP:(h + 1) * SP], w[:, 0:T], start=True, stop=False,
                       skip_group_check=True)
                    last = mm(o[:, P:T], xs_tok[:, 1, h * SP:(h + 1) * SP], w[:, T:3 * P], start=False, stop=True,
                              skip_group_check=True)
                Dr.full(last)
            for j in range(KC + 1):
                if j < KC:
                    ssd_decay(2 * j)
                    ssd_decay(2 * j + 1)
                if j >= 1:
                    ssd_pair(j - 1)
            ssq(xn2)
            pe.wait_ge(sem("ssd_normed"), KC)
            row_blocks(6, mixT)
            ssq(xn2)
            pe.wait_ge(sem("h_ready"), 4 * KC)
            pe.wait_ge(sem("keys_in"), 16)

            def key_scores(j):
                pe.wait_ge(a_drained, A_AT["query"] + j + 1)
                b = Dr.bank()
                for t in range(NT):
                    last = mm(b[:, t * NK:(t + 1) * NK], xn2[:, j % 4, t * P:(t + 1) * P], keysT[:, j, :],
                              start=True, stop=True)
                Dr.full(last)
            for p_ in range(QH):
                w = pair()
                for u in range(2):
                    blocks(A, w[:, u, :], hT, opens=u == 0)
                    if 2 * p_ + u >= 1:
                        key_scores(2 * p_ + u - 1)
            key_scores(2 * QH - 1)
            columns(A, 16, 0, hT)
            pe.wait_ge(sem("picked"), 1)
            for z in range(3):
                b = Dr.bank()
                for t in range(NT):
                    last = nc.tensor.transpose(b[:, t * P:(t + 1) * P], picked[:, z, t * P:(t + 1) * P], ident[:, :])
                Dr.full(last)
            one_hot = Count()
            with repeat(pe, T // 4, {Dr.count: 4, one_hot: 4}):
                for _ in range(4):
                    n = one_hot.n
                    one_hot.n += 1
                    pe.wait_ge(sem("one_hots"), one_hot.loop * 2 + 2 * (n + 1))
                    b = Dr.bank()
                    h = hot[:, n % ONEHOTS, :, :]
                    Dr.full(mm(b[:, 0:NK], h[:, 0, :], h[:, 1, :], start=True, stop=True))
            pe.wait_ge(d_drained, D_AT["spread"] + T)
            row_blocks(64, U)
            ssq(U[:, 0:KC, :])


def kernel(**inputs):
    import numpy as np
    import concourse.bacc as bacc
    from concourse.bass_utils import run_bass_kernel_spmd

    a = {k: np.asarray(v) for k, v in inputs.items()}
    f32 = np.float32

    def chunks(v):
        return v.reshape(-1, P).T

    def columns(w):
        n = w.shape[1] // 256
        return np.ascontiguousarray(w.reshape(KC, P, n, 2, P).transpose(2, 1, 3, 0, 4)).reshape(n, P, 2048)

    def rows(w):
        n = w.shape[0] // 256
        return np.ascontiguousarray(w.reshape(n, 2, P, 1024).transpose(0, 2, 1, 3)).reshape(n, P, 2048)

    w_in, b_in = a["w_in"][0], a["b_in"][0]
    tok_cols = [slice(2056 + 512 * k, 2568 + 512 * k) for k in range(3)] + [slice(1024, 1536)]
    feat_cols = [slice(0, 1024), slice(1536, 2048), slice(3592, 5640)]
    tok = np.stack([w_in[:, s] for s in tok_cols])
    tok = np.ascontiguousarray(tok.reshape(4, 2, 4, P, 512).transpose(0, 1, 3, 2, 4)).reshape(8, P, 2048)
    w_gate, w_up = a["w_gate"][0], a["w_up"][0]
    gate_up = np.stack([w_gate.reshape(D, FC, P), w_up.reshape(D, FC, P)], axis=2).reshape(D, 2 * FF)
    w_in2 = a["w_in_2"][0]
    down = a["expert_down_2"][0].reshape(P, 64, 2, KC, P)
    down = np.ascontiguousarray(down.transpose(1, 4, 2, 3, 0)).reshape(64, P, 2048)
    up = np.ascontiguousarray(a["expert_up_2"][0].reshape(P, 64, 2048).transpose(1, 0, 2))
    keys = np.stack([a["sub_keys1_2"][0], a["sub_keys2_2"][0]], axis=1)
    half = np.arange(32, dtype=f32) / f32(32)
    per_part = {
        "ada_b": chunks(a["ada_b"][0]), "norm1": chunks(a["norm1_g"][0]), "norm2": chunks(a["norm2_g"][0]),
        "normf": chunks(a["normf_g"]), "b_feat": chunks(np.concatenate([b_in[s] for s in feat_cols])),
        "conv_w": a["conv_w"][0].reshape(CONV, 8, P).transpose(2, 1, 0).reshape(P, 32),
        "conv_b": chunks(a["conv_b"][0]), "m_norm": chunks(a["m_norm_g"][0]), "ada_b2": chunks(a["b_ada_2"][0]),
        "norm_mix": chunks(a["norm_mix_2"][0]), "norm_ffn": chunks(a["norm_ffn_2"][0]),
        "norm_final": chunks(a["norm_final_2"]), "pool_b": a["pool_b_2"][0].T, "pool_scale": a["pool_scale_2"][0].T,
        "conv_w2": a["conv_w_2"][0].reshape(CONV, XBC, P).transpose(2, 1, 0).reshape(P, 48),
        "conv_b2": chunks(a["conv_b_2"][0]), "d_skip": chunks(np.repeat(a["d_skip_2"][0], SP)),
        "ssd_norm": chunks(a["ssd_norm_2"][0]), "b_i": b_in[2048:2052, None], "b_f": b_in[2052:2056, None],
        "dt_bias": a["dt_bias_2"][0][:, None], "a_log": a["a_log_2"][0][:, None],
        "inv_freq": np.broadcast_to(np.power(f32(10000.0), -half).astype(f32), (P, 32)),
    }
    cols = np.zeros((P, NCOLS), f32)
    for name, (at, width) in COLS.items():
        cols[:per_part[name].shape[0], at:at + width] = per_part[name]
    arrays = {
        "x": np.ascontiguousarray(a["x"][0].T.reshape(KC, P, T).transpose(1, 0, 2)),
        "c": a["c"], "c_2": a["c_2"],
        "pos": np.ascontiguousarray(a["positions"][0].reshape(NT, P).T),
        "cols_in": cols,
        "bias_tok": np.stack([b_in[s] for s in tok_cols]),
        "w_gates": np.ascontiguousarray(w_in[:, 2048:2056].reshape(KC, P, 8).transpose(1, 0, 2)),
        "w_dt": np.ascontiguousarray(w_in2[:, 3072:3088].reshape(KC, P, SH).transpose(1, 0, 2)),
        "pool_w": np.ascontiguousarray(a["pool_w_2"][0].transpose(1, 0, 2)),
        "keys": np.ascontiguousarray(keys.reshape(16, NK, P).transpose(2, 0, 1)),
        "ada": np.ascontiguousarray(a["ada_w"][0].T).reshape(48, P, D),
        "ada2": np.ascontiguousarray(a["w_ada_2"][0].T).reshape(48, P, D),
        "tok": tok,
        "feat": columns(np.concatenate([w_in[:, s] for s in feat_cols], axis=1)),
        "proj": columns(np.concatenate([a["p_mlstm"][0], a["p_moba"][0]], axis=0)),
        "wout": columns(a["w_out"][0]),
        "gateup": columns(gate_up),
        "down": rows(a["w_down"][0]),
        "win2": columns(w_in2[:, 0:3072]),
        "wout2": rows(a["w_out_2"][0]),
        "query": columns(a["w_query_2"][0]),
        "expert_down": down,
        "expert_up": up,
    }
    nc = bacc.Bacc("TRN2", target_bir_lowering=False, num_devices=1)
    aps = {n: nc.dram_tensor(n, v.shape, mybir.dt.from_np(v.dtype), kind="ExternalInput").ap()
           for n, v in arrays.items()}
    out = nc.dram_tensor("out", (P, KC, T), F32, kind="ExternalOutput").ap()
    two_mixers_program(nc, **aps, out=out)
    r = run_bass_kernel_spmd(nc, [arrays], core_ids=[0])
    y = r.results[0]["out"]
    return np.ascontiguousarray(y.transpose(1, 0, 2).reshape(D, T).T)[None]
```

```python
from contextlib import ExitStack, contextmanager

import concourse.bass as bass
from concourse import mybir

F32 = mybir.dt.float32
F32R = mybir.dt.float32r
I32 = mybir.dt.int32
U32 = mybir.dt.uint32
ALU = mybir.AluOpType
ACT = mybir.ActivationFunctionType
AX = mybir.AxisListType

P = 128
T = 256
NT = T // P
D = 1024
KC = D // P
MH, MD = 4, 128
AH, AD = 8, 64
FF = 2816
FC = FF // P
CONV = 4
SH, SP = 16, 64
SG = 2
POOLS = (2, 4, 8, 16)
NPOOL = len(POOLS)
XBC = 12
MIXC = NPOOL + KC
QH, NK, TOPK = 8, 128, 16
EPS = 1e-6
FAR = -1e30
LOWEST = -3.0e38
MAGIC = 12582912.0
TWO_PI = (6.28125, 0.0019350051879882812, 3.0199157663446432e-07)
PI_BELOW = 3.1415925
SCRATCH = 2048

Z_MQ, Z_MK, Z_MO, Z_GA, Z_GB, Z_N = 0, 4, 8, 12, 20, 28
TOK_BLOCKS = 4

COLS = {}
for _name, _width in (
    ("ada_b", 48), ("norm1", 8), ("norm2", 8), ("normf", 8), ("b_feat", Z_N), ("conv_w", 32), ("conv_b", 8),
    ("m_norm", 4), ("ada_b2", 48), ("norm_mix", 8), ("norm_ffn", 8), ("norm_final", 8), ("pool_b", 4),
    ("pool_scale", 4), ("conv_w2", 48), ("conv_b2", 12), ("d_skip", 8), ("ssd_norm", 8), ("b_i", 1), ("b_f", 1),
    ("dt_bias", 1), ("a_log", 1), ("inv_freq", 32),
):
    COLS[_name] = (sum(w for _, w in COLS.values()), _width)
NCOLS = sum(w for _, w in COLS.values())

STREAM = (("gates", 1), ("tok", 16), ("feat", 28), ("proj", 8), ("wout", 8), ("gateup", 44), ("down", 22),
          ("dt", 1), ("win2", 24), ("wout2", 12), ("query", 16), ("expert_down", 128), ("expert_up", 128))
UNITS = sum(n for _, n in STREAM)
SLOTS = 4
HALF = 512
GATED = 64

RING_A = (("ssq1", 1), ("feat", 28), ("qkT", 8), ("probsT", 8), ("attn", 4), ("ssq2", 1), ("gate", 22),
          ("ssqf", 1), ("ssq_mix", 1), ("win2", 24), ("ssq_ssd", 1), ("ssq_ffn", 1), ("query", 16),
          ("experts", 128), ("expert_up", 4), ("ssq_final", 1))
RING_D = (("gates", 1), ("tok", 8), ("gate_cols", 1), ("attn_scores", 8), ("m_decay", 4), ("m_scores", 4),
          ("m_out", 4), ("ymT", 4), ("proj", 16), ("wout", 8), ("up", 22), ("down", 4), ("dt", 1), ("pool", 4),
          ("dt_cols", 1), ("xs_tok", 4), ("cb", 2), ("ssd", 24), ("wout2", 4), ("scores", 16), ("picksT", 3),
          ("spread", 512))
BANKS = 4


def starts(stages):
    at, n = {}, 0
    for name, count in stages:
        at[name] = n
        n += count
    return at


A_AT, D_AT = starts(RING_A), starts(RING_D)


class Count:

    def __init__(self):
        self.n = 0
        self.loop = None

    def value(self, back=0):
        return self.n - back if self.loop is None else self.loop + (self.n - back)


@contextmanager
def repeat(eng, times, per):
    before = {c: c.n for c in per}
    with eng.Fori(0, times) as i:
        for c, k in per.items():
            c.loop = i * k
        yield i
    for c, k in per.items():
        assert c.n - before[c] == k, (c.n - before[c], k)
        c.loop, c.n = None, before[c] + k * times


class Own:

    def __init__(self, eng, sem):
        self.eng, self.sem, self.count = eng, sem, Count()

    def __call__(self, ins):
        ins.then_inc(self.sem, 1)
        self.count.n += 1
        self.eng.wait_ge(self.sem, self.count.value())


class Fill:

    def __init__(self, pe, psum, ready, drained):
        self.pe, self.psum, self.ready, self.drained, self.count = pe, psum, ready, drained, Count()

    def bank(self):
        n = self.count.n
        self.count.n += 1
        assert n >= BANKS or self.count.loop is None
        if n >= BANKS:
            self.pe.wait_ge(self.drained, self.count.value(BANKS))
        return self.psum[:, n % BANKS, :]

    def full(self, ins):
        ins.then_inc(self.ready, 1)


class Empty:

    def __init__(self, eng, psum, ready, drained):
        self.eng, self.psum, self.ready, self.drained, self.count = eng, psum, ready, drained, Count()

    def bank(self):
        n = self.count.n
        self.count.n += 1
        self.eng.wait_ge(self.ready, self.count.value())
        return self.psum[:, n % BANKS, :]

    def free(self, ins, settle=False):
        ins.then_inc(self.drained, 1)
        if settle:
            self.eng.wait_ge(self.drained, self.count.value())


def two_mixers_program(nc, x, c, c_2, pos, cols_in, bias_tok, pool_w, keys, ada, ada2, gates, tok, feat, proj,
                       wout, gateup, down, dt, win2, wout2, query, expert_down, expert_up, out):
    with ExitStack() as ctx:
        def sb(name, shape, dt=F32):
            return ctx.enter_context(nc.sbuf_tensor(name, shape, dt))

        sems = {}

        def sem(name):
            if name not in sems:
                sems[name] = ctx.enter_context(nc.semaphore(name))
            return sems[name]

        psA = ctx.enter_context(nc.psum_tensor("psA", [P, BANKS, 512], F32))
        psD = ctx.enter_context(nc.psum_tensor("psD", [P, BANKS, 512], F32))

        MAP = 4096 + 2048 + 2048 + 2048 + 2048 + 4096 + 32768
        sb("map", [P, MAP])
        map_at = nc.sbuf_base - 4 * MAP

        def at_place(name, at, n, dt=F32):
            return nc.alloc_sbuf_tensor_at(name, [P, n], dt, offset=map_at + 4 * at)
        RAW, HI, LO, X_AT, M_AT, H_AT, ARENA = 0, 4096, 6144, 8192, 10240, 12288, 16384
        raw = at_place("raw", RAW, SLOTS * 1024)
        w_hi = at_place("w_hi", HI, SLOTS * HALF, F32R)
        w_lo = at_place("w_lo", LO, SLOTS * HALF, F32R)
        xT = at_place("xT", X_AT, KC * T)[:, :].rearrange("p (k t) -> p k t", t=T)
        mT = at_place("mT", M_AT, KC * T)[:, :].rearrange("p (k t) -> p k t", t=T)
        spare = at_place("spare", M_AT, 2048)
        h_hi = at_place("h_hi", H_AT, KC * T, F32R)[:, :].rearrange("p (k t) -> p k t", t=T)
        h_lo = at_place("h_lo", H_AT + KC * T, KC * T, F32R)[:, :].rearrange("p (k t) -> p k t", t=T)
        turned = at_place("turned", H_AT, 4096)
        arena = at_place("arena", ARENA, 32768)
        ident = sb("ident", [P, P])
        ones = sb("ones", [P, P])
        mask_ts = sb("mask_ts", [P, T])
        mask_st = sb("mask_st", [P, T])
        cols = sb("cols", [P, NCOLS])
        mods = sb("mods", [P, 2, 48])
        scale_cols = sb("scale_cols", [P, 2, KC])
        eps = sb("eps", [P, 1])
        late = sb("late", [P, 2304])

        taken = [0]

        def part(tensor, at, *shape):
            n = 1
            for s in shape:
                n *= s
            v = tensor[:, at:at + n]
            names = "abcd"[:len(shape)]
            if len(shape) > 1:
                v = v.rearrange(f"p ({' '.join(names)}) -> p {' '.join(names)}",
                                **{k: s for k, s in zip(names[1:], shape[1:])})
            return v

        def temp(*shape):
            at = taken[0]
            n = 1
            for s in shape:
                n *= s
            taken[0] += n
            assert taken[0] <= 32768, taken[0]
            return part(arena, at, *shape)

        ADA_SLOTS = 4
        ada_ring = temp(ADA_SLOTS, D)
        c_row = temp(2, D)
        b_tok = temp(TOK_BLOCKS, 512)
        zT = temp(Z_N, T)
        toks = temp(NT, 2 * 512)
        v_tok = temp(NT, 512)
        v_ext = temp(NT, MH, MD + 1)
        xn = temp(KC, T)
        qkT = temp(2, 4, T)
        convT = temp(2 * MH, T)
        probs = temp(AH, 3 * P)
        gate_rows = temp(64)
        trig = temp(4, NT, 32)
        assert taken[0] <= 32768
        probsT = part(turned, 0, AH, 3 * P)
        nd = part(arena, ADA_SLOTS * D + 2 * D, NT * MH, MD + 1)
        TOKS_AT = ADA_SLOTS * D + 2 * D + 2048 + Z_N * T

        def split_in(name, at, n):
            return [at_place(name + k, ARENA + at + i * n * T, n * T, F32R)[:, :].rearrange("p (k t) -> p k t", t=T)
                    for i, k in enumerate(("_hi", "_lo"))]
        yaT = part(arena, TOKS_AT, 4, T)
        ymT = part(arena, TOKS_AT + 1024, MH, T)
        PROBS_AT = TOKS_AT + 2048 + 1024 + NT * MH * (MD + 1) + 2048 + 2048 + 2048
        y_hi, y_lo = split_in("y", PROBS_AT - 2048, 8)
        turn = part(xn.rearrange("p a b -> p (a b)"), 0, 2, 2, 16, 32)
        mw = part(xn.rearrange("p a b -> p (a b)"), 0, MH, 3 * P)
        F_AT = ADA_SLOTS * D + 2 * D + 2048
        fT = part(arena, F_AT, FC, T)
        f_hi, f_lo = [at_place(n, ARENA + at, FC * T, F32R)[:, :].rearrange("p (k t) -> p k t", t=T)
                      for n, at in (("f_hi", F_AT + FC * T), ("f_lo", TOKS_AT + 2048 + 1024 + 1032 + 2048))]
        assert F_AT + 2 * FC * T <= TOKS_AT + 2048 + 1024 + 1032

        after = ADA_SLOTS * D + 2 * D
        keysT = part(arena, after, 16, NK)
        z2T = part(arena, after + 2048, 24, T)
        at = after + 2048 + 24 * T
        xbcT = part(arena, at, XBC, T)
        at += XBC * T
        mixT = part(arena, at, MIXC, T)
        at += MIXC * T
        xs_tok = part(arena, at, NT, D)
        at += NT * D
        cbT = part(arena, at, SG, 3 * P)
        at += SG * 3 * P
        ssd_w = part(arena, at, 4, 3 * P)
        at += 4 * 3 * P
        xn2 = part(arena, at, KC, T)
        at += KC * T
        pool_wt = part(arena, at, NPOOL, P)
        at += NPOOL * P
        assert at <= 28672
        PADDED = T + 16
        pool_a = part(arena, at, NPOOL, PADDED)
        at += NPOOL * PADDED
        pool_b = part(arena, at, NPOOL, PADDED)
        at += NPOOL * PADDED
        inv_t = part(arena, at, 2, T)
        at += 2 * T
        assert at <= 32768, at
        mix_hi, mix_lo = split_in("mix", ADA_SLOTS * D + 4096, MIXC)
        u_hi, u_lo = [at_place(n, H_AT + k * 1024, 1024, F32R)[:, :].rearrange("p (k t) -> p k t", t=T)
                      for k, n in enumerate(("u_hi", "u_lo"))]

        U = arena[:, :].rearrange("p (e t) -> p e t", t=T)

        def row(i):
            return late[:, i * T:(i + 1) * T]
        r_i, r_f, r_abs, r_e, r_u, r_t, r_l, r_s = [row(i) for i in range(8)]
        small = part(late, 2048, 256)
        m_cols = part(small, 0, 2, MH, NT)
        mx = part(small, 16, 16)
        nmx = part(small, 32, 16)
        sums = part(small, 48, 16)
        rsums = part(small, 64, 16)
        m_stat = part(small, 80, 5, NT * MH)
        s_cols = part(small, 128, 2, NT, SH)
        a_col = part(small, 192, 2)
        posf = part(small, 200, 2)
        rinv = sb("rinv", [P, T])
        rms = sb("rms", [P, T])
        pos_i = sb("pos_i", [P, NT], I32)

        scores = part(arena, 28672, NT, 2 * QH, NK)
        eq = part(arena, 28672, NT * QH * TOPK, TOPK)
        iota_k = rms[:, P:2 * P]
        top_v = part(late, 0, NT * QH, TOPK)
        pick_a = part(late, 256, NT * QH, TOPK)
        pick_b = part(late, 512, NT * QH, TOPK)
        idx = part(late, 768, NT * QH, 2, TOPK)
        picked = part(late, 1280, 3, NT * QH * TOPK)
        picksT = part(late, 0, 3, T)
        stage = part(rinv, 0, T)
        work = part(rinv, 0, 2, NK)
        work2 = part(rms, 0, NK)
        cand = part(mask_ts, 0, TOPK, TOPK)
        cand2 = mask_st
        v16 = part(small, 208, 2, TOPK)
        i16 = part(spare, 1024, 3, TOPK).bitcast(U32)
        ONEHOTS = 4
        hot = part(spare, 0, ONEHOTS, 2, NK)

        def col(name, j=0, n=1, parts=P):
            a, w = COLS[name]
            assert j + n <= w
            return cols[0:parts, a + j:a + j + n]

        def sel(h, heads):
            return ident[0:heads, h:h + 1].broadcast_to([heads, P])

        raw_full = [sem(f"raw_full{s}") for s in range(SLOTS)]
        ada_full = [sem(f"ada_full{s}") for s in range(ADA_SLOTS)]
        hi_ready, lo_ready, half_used, ada_used = sem("hi_ready"), sem("lo_ready"), sem("half_used"), sem("ada_used")
        a_ready, a_drained = sem("a_ready"), sem("a_drained")
        d_ready, d_drained = sem("d_ready"), sem("d_drained")

        block = ctx.enter_context(nc.Block())

        @block.sync
        def _(sp):
            sp.dma_start(cols[:, :], cols_in[:, :]).then_inc(sem("cols_in"), 16)
            for k, cc in enumerate((c, c_2)):
                sp.dma_start(c_row[:, k, :], cc.broadcast_to([P, D])).then_inc(sem("c_in"), 16)
            sp.dma_start(pos_i[:, :], pos[:, :]).then_inc(sem("pos_in"), 16)
            sp.dma_start(xT[:, :, :], x[:, :, :]).then_inc(sem("x_in"), 16)
            sp.dma_start(b_tok, bias_tok.rearrange("a b -> () (a b)").broadcast_to([P, 2048]).rearrange(
                "p (a b) -> p a b", a=TOK_BLOCKS)).then_inc(sem("b_tok_in"), 16)
            units, adas = Count(), Count()

            def load(src):
                n = units.n
                units.n += 1
                if n >= SLOTS:
                    v = 2 * (n - SLOTS) + 2
                    sp.wait_ge(lo_ready, v if units.loop is None else units.loop * 2 + v)
                sp.dma_start(raw[:, n % SLOTS * 1024:(n % SLOTS + 1) * 1024], src).then_inc(raw_full[n % SLOTS], 16)

            def load_ada(src):
                n = adas.n
                adas.n += 1
                if n >= ADA_SLOTS:
                    sp.wait_ge(ada_used, adas.value(ADA_SLOTS))
                sp.dma_start(ada_ring[:, n % ADA_SLOTS, :], src).then_inc(ada_full[n % ADA_SLOTS], 16)

            def stream(src, n, beside=None):
                turns, rest = divmod(n, 4)
                with repeat(sp, turns, {units: 4, adas: 4} if beside else {units: 4}) as i:
                    for j in range(4):
                        load(src(i * 4 + j))
                        if beside:
                            load_ada(beside(i * 4 + j))
                for j in range(turns * 4, n):
                    load(src(j))

            for j in range(ADA_SLOTS):
                load_ada(ada[j])
            load(gates[0])
            for j in range(3):
                load(tok[j])
            with repeat(sp, 3, {adas: 4}) as i:
                for j in range(4):
                    load_ada(ada[i * 4 + (j + 4)])
            load(tok[3])
            stream(lambda u: tok[u + 4], 12)
            stream(lambda u: feat[u], 28, lambda u: ada[u + 16])
            for j in range(44, 48):
                load_ada(ada[j])
            stream(lambda u: proj[u], 8)
            stream(lambda u: wout[u], 8)
            stream(lambda u: gateup[u], 44, lambda u: ada2[u])
            for j in range(44, 48):
                load_ada(ada2[j])
            stream(lambda u: down[u], 22)
            load(dt[0])
            stream(lambda u: win2[u], 24)
            sp.wait_ge(d_drained, D_AT["down"] + 4)
            sp.dma_start(pool_wt, pool_w[:, :, :]).then_inc(sem("pool_w_in"), 16)
            sp.dma_start(keysT, keys[:, :, :]).then_inc(sem("keys_in"), 16)
            stream(lambda u: wout2[u], 12)
            stream(lambda u: query[u], 16)
            stream(lambda u: expert_down[u], 128)
            stream(lambda u: expert_up[:, u, :], 128)
            sp.wait_ge(sem("y_ready"), KC)
            sp.dma_start(out[:, :, :], mT[:, :, :]).then_inc(sem("out_stored"), 16)
            sp.wait_ge(sem("out_stored"), 16)

        @block.gpsimd
        def _(pool):
            own = Own(pool, sem("pool_own"))
            own(nc.gpsimd.memset(ident[:, :], 0.0))
            own(nc.gpsimd.affine_select(out=ident[:, :], in_=ident[:, :], compare_op=ALU.not_equal, fill=1.0,
                                        base=0, pattern=[[-1, P]], channel_multiplier=1))
            own(nc.gpsimd.memset(mask_ts[:, :], 0.0))
            own(nc.gpsimd.memset(mask_st[:, :], 0.0))
            own(nc.gpsimd.affine_select(out=mask_ts[:, P:T], in_=mask_ts[:, P:T], compare_op=ALU.is_ge, fill=FAR,
                                        base=0, pattern=[[-1, P]], channel_multiplier=1))
            own(nc.gpsimd.affine_select(out=mask_st[:, 0:P], in_=mask_st[:, 0:P], compare_op=ALU.is_ge, fill=FAR,
                                        base=0, pattern=[[1, P]], channel_multiplier=-1))
            nc.gpsimd.memset(ones[:, :], 1.0).then_inc(sem("consts"), 1)

            halves = Count()
            with repeat(pool, UNITS // 4, {halves: 8}):
                for _ in range(8):
                    n = halves.n
                    halves.n += 1
                    pool.wait_ge(hi_ready, halves.value())
                    s = n % SLOTS
                    nc.gpsimd.tensor_tensor(w_lo[:, s * HALF:(s + 1) * HALF], raw[:, n % 8 * HALF:(n % 8 + 1) * HALF],
                                            w_hi[:, s * HALF:(s + 1) * HALF].bitcast(F32),
                                            ALU.subtract).then_inc(lo_ready, 1)

        @block.scalar
        def _(act):
            A = Empty(act, psA, a_ready, a_drained)
            own = Own(act, sem("act_own"))
            act.wait_ge(sem("c_in"), 32)
            nc.scalar.activation(c_row[:, :, :], c_row[:, :, :], ACT.Silu).then_inc(sem("c_act"), 1)

            halves = Count()

            def next_stage():
                next_stage.n += 1
            next_stage.n = 0

            def split(n_units=1):
                for _ in range(2 * n_units):
                    n = halves.n
                    halves.n += 1
                    if n >= SLOTS:
                        act.wait_ge(half_used, halves.value(SLOTS) + next_stage.n)
                    if n % 2 == 0:
                        at = 16 * (n // 8 + 1)
                        act.wait_ge(raw_full[n // 2 % SLOTS], at if halves.loop is None else halves.loop * 2 + at)
                    nc.scalar.copy(w_hi[:, n % SLOTS * HALF:(n % SLOTS + 1) * HALF],
                                   raw[:, n % 8 * HALF:(n % 8 + 1) * HALF]).then_inc(hi_ready, 1)

            def root(src, sq, width):
                nc.scalar.activation(sq, src, ACT.Square).then_inc(sem("sq_ready"), 1)
                b = A.bank()
                A.free(nc.scalar.activation(rms[:, :], b[:, 0:T], ACT.Sqrt, bias=eps[:, 0:1], scale=1.0 / width))

            def norm_modulated(sq, shifts):
                root(xT[:, :, :], sq, D)
                for j in range(KC):
                    norm_modulated.n += 1
                    act.wait_ge(sem("xn_ready"), norm_modulated.n)
                    nc.scalar.activation(h_hi[:, j, :], sq[:, j, :], ACT.Identity, bias=shifts[:, j:j + 1],
                                         scale=1.0).then_inc(sem("h_hi"), 1)
            norm_modulated.n = 0

            split(2)
            act.wait_ge(sem("x_in"), 16)
            act.wait_ge(sem("eps_set"), 1)
            norm_modulated(xn, mods[:, 0, 0:KC])

            def log1p_exp(k):
                n = MH if k == 0 else SH
                act.wait_ge(sem("row_abs"), k + 1)
                nc.scalar.activation(r_e[0:n, :], r_abs[0:n, :], ACT.Exp, scale=-1.0).then_inc(sem("row_exp"), 1)
                if k == 0:
                    split(1)
                act.wait_ge(sem("row_u"), k + 1)
                nc.scalar.activation(r_l[0:n, :], r_u[0:n, :], ACT.Ln).then_inc(sem("row_ln"), 1)

            split(1)
            next_stage()
            log1p_exp(0)
            split(2)
            act.wait_ge(sem("m_rows"), 1)
            nc.scalar.activation(r_e[0:MH, :], r_t[0:MH, :], ACT.Exp, scale=-1.0).then_inc(sem("exp_m"), 1)
            split(1)
            act.wait_ge(sem("angles"), 1)
            nc.scalar.activation(trig[:, 0:2, :, :], trig[:, 0:2, :, :], ACT.Sin).then_inc(sem("trig"), 1)

            with repeat(act, 3, {halves: 8}):
                split(4)
            next_stage()
            with repeat(act, 7, {A.count: 4, halves: 8}) as i:
                for j in range(4):
                    split(1)
                    A.free(nc.scalar.activation(zT[:, i * 4 + j, :], A.bank()[:, 0:T], ACT.Identity,
                                                bias=cols[:, bass.ds(i * 4 + (j + COLS["b_feat"][0]), 1)]))
            act.wait_ge(a_drained, A_AT["feat"] + Z_N)
            nc.scalar.activation(zT[:, Z_MO:Z_N, :], zT[:, Z_MO:Z_N, :], ACT.Sigmoid).then_inc(sem("sig_ready"), 1)
            for j in range(2 * MH):
                act.wait_ge(sem("conv_ready"), j + 1)
                nc.scalar.activation(convT[:, j, :], convT[:, j, :], ACT.Silu,
                                     bias=col("conv_b", j)).then_inc(sem("m_qk"), 1)
            for j in range(8):
                A.free(nc.scalar.copy(qkT[:, j % 2, j // 2, :], A.bank()[:, 0:T]))
            act.wait_ge(sem("nmx"), 1)
            for h in range(AH):
                for t in range(NT):
                    p = probs[:, h, 0:P] if t == 0 else probs[:, h, P:3 * P]
                    k = h * NT + t
                    nc.scalar.activation(p, p, ACT.Exp, bias=nmx[:, k:k + 1], scale=AD ** -0.5,
                                         accum_out=sums[:, k:k + 1]).then_inc(sem("exps"), 1)
            for h in range(MH):
                act.wait_ge(sem("m_args"), h + 1)
                for s in range(NT):
                    a = mw[:, h, 0:T] if s == 0 else mw[:, h, T:3 * P]
                    nc.scalar.activation(a, a, ACT.Exp, bias=m_cols[:, 0, h, s:s + 1]).then_inc(sem("m_w"), 1)
            for h in range(AH):
                A.free(nc.scalar.copy(probsT[:, h, :], A.bank()[:, 0:3 * P]))
            for j in range(4):
                A.free(nc.scalar.copy(yaT[:, j, :], A.bank()[:, 0:T]))
            act.wait_ge(sem("m_ms"), 1)
            nc.scalar.activation(m_stat[:, 3, :], m_stat[:, 2, :], ACT.Sqrt, bias=eps[:, 0:1],
                                 scale=1.0 / MD).then_inc(sem("m_rms"), 1)

            for j in range(MH):
                act.wait_ge(d_drained, D_AT["ymT"] + j + 1)
                nc.scalar.copy(y_hi[:, j, :], ymT[:, j, :]).then_inc(sem("y_hi"), 1)
            for j in range(4):
                act.wait_ge(a_drained, A_AT["attn"] + j + 1)
                nc.scalar.copy(y_hi[:, MH + j, :], yaT[:, j, :]).then_inc(sem("y_hi"), 1)
            next_stage()
            split(8)
            for j in range(KC):
                act.wait_ge(sem("merged"), j + 1)
                nc.scalar.copy(h_hi[:, j, :], mT[:, j, :]).then_inc(sem("m_hi"), 1)
            next_stage()
            split(8)
            act.wait_ge(d_drained, D_AT["wout"] + 8)
            norm_modulated(xn, mods[:, 0, 3 * KC:4 * KC])

            def f_upper(j):
                act.wait_ge(d_drained, j + (D_AT["up"] + 1))
                nc.scalar.copy(f_hi[:, j, :], fT[:, j, :]).then_inc(sem("f_hi"), 1)

            def gate(j):
                split(2)
                A.free(nc.scalar.activation(fT[:, j, :], A.bank()[:, 0:T], ACT.Silu))
            next_stage()
            for j in range(2):
                gate(j)
            f_upper(0)
            with repeat(act, 5, {A.count: 4, halves: 16}) as i:
                for j in range(4):
                    gate(i * 4 + (j + 2))
                    f_upper(i * 4 + (j + 1))
            f_upper(FC - 1)
            next_stage()
            with repeat(act, 5, {halves: 8}):
                split(4)
            split(2)
            act.wait_ge(d_drained, D_AT["down"] + 4)
            root(xT[:, :, :], xn2, D)
            act.wait_ge(sem("x_normed"), KC)
            norm_modulated(xn2, mods[:, 1, 0:KC])
            next_stage()
            split(1)
            next_stage()
            with repeat(act, 6, {A.count: 4, halves: 8}) as i:
                for j in range(4):
                    split(1)
                    A.free(nc.scalar.copy(z2T[:, i * 4 + j, :], A.bank()[:, 0:T]))
            nc.scalar.activation(a_col[0:SH, 0:1], col("a_log", parts=SH), ACT.Exp).then_inc(sem("a_exp"), 1)
            log1p_exp(1)
            act.wait_ge(a_drained, A_AT["win2"] + MIXC)
            nc.scalar.activation(z2T[:, NPOOL:MIXC, :], z2T[:, NPOOL:MIXC, :], ACT.Silu).then_inc(sem("z_silu"), 1)
            for j in range(XBC):
                act.wait_ge(sem("conv2_ready"), j + 1)
                nc.scalar.activation(xbcT[:, j, :], xbcT[:, j, :], ACT.Silu,
                                     bias=col("conv_b2", j)).then_inc(sem("xbc"), 1)
            for h in range(SH):
                act.wait_ge(sem("ssd_args"), h + 1)
                nc.scalar.activation(ssd_w[:, h % 4, :], ssd_w[:, h % 4, :], ACT.Exp).then_inc(sem("ssd_exp"), 1)
            act.wait_ge(sem("ssd_y"), KC)
            root(mixT[:, NPOOL:MIXC, :], xn2, D)
            for j in range(MIXC):
                if j >= NPOOL:
                    act.wait_ge(sem("ssd_normed"), j - NPOOL + 1)
                nc.scalar.copy(mix_hi[:, j, :], mixT[:, j, :]).then_inc(sem("mix_hi"), 1)
            next_stage()
            split(12)
            act.wait_ge(d_drained, D_AT["wout2"] + 4)
            norm_modulated(xn2, mods[:, 1, 3 * KC:4 * KC])
            next_stage()
            for j in range(2 * QH):
                split(1)
                b = A.bank()
                if j >= 4:
                    act.wait_ge(d_ready, D_AT["scores"] + j - 4 + 1)
                A.free(nc.scalar.copy(xn2[:, j % 4, :], b[:, 0:T]))
            act.wait_ge(d_drained, D_AT["scores"] + 2 * QH)

            next_stage()

            def activate(i):
                for j in range(4):
                    split(1)
                    A.free(nc.scalar.activation(U[:, i * 4 + j, :], A.bank()[:, 0:T], ACT.Gelu))
            with repeat(act, 15, {A.count: 4, halves: 8}) as i:
                activate(i)
            act.wait_ge(sem("gate_args"), 1)
            nc.scalar.activation(picked[:, 2, :], picked[:, 2, :], ACT.Exp).then_inc(sem("gate_exp"), 1)
            with repeat(act, 17, {A.count: 4, halves: 8}) as i:
                activate(i + 15)

            def u_upper(j, slot):
                nc.scalar.copy(u_hi[:, slot, :], U[:, j, :]).then_inc(sem("u_hi"), 1)

            def next_expert(j, slot):
                split(1)
                u_upper(j, slot)
            next_stage()
            act.wait_ge(d_drained, D_AT["spread"] + T)
            u_upper(0, 0)
            u_upper(1, 1)
            for first in (2, GATED + 2):
                with repeat(act, (GATED - 4) // 4, {halves: 8}) as i:
                    for j in range(4):
                        next_expert(i * 4 + (first + j), (first + j) % 4)
                for j in range(GATED - 4, GATED - 2):
                    next_expert(first + j, (first + j) % 4)
                if first == 2:
                    split(1)
                    act.wait_ge(d_drained, D_AT["spread"] + 2 * T)
                    u_upper(GATED, 0)
                    next_expert(GATED + 1, 1)
            act.wait_ge(a_drained, A_AT["ssq_final"])
            A.count.n += BANKS
            root(xT[:, :, :], U[:, 0:KC, :], D)

        @block.vector
        def _(dve):
            Dr = Empty(dve, psD, d_ready, d_drained)
            own = Own(dve, sem("dve_own"))
            V = nc.vector
            V.memset(eps[:, :], EPS).then_inc(sem("eps_set"), 1)
            own(V.memset(v_ext[:, :, :, MD:MD + 1], 1.0))
            dve.wait_ge(sem("consts"), 1)
            dve.wait_ge(sem("cols_in"), 16)

            ada_n = Count()

            def ada_block(which, j):
                n = ada_n.n
                ada_n.n += 1
                s = n % ADA_SLOTS
                at = 16 * (n // ADA_SLOTS + 1)
                dve.wait_ge(ada_full[s], at if ada_n.loop is None else ada_n.loop * 4 + at)
                V.scalar_tensor_tensor(out=ada_ring[:, s, :], in0=ada_ring[:, s, :], scalar=1.0,
                                       in1=c_row[:, which, :], op0=ALU.mult, op1=ALU.mult,
                                       accum_out=mods[:, which, bass.ds(j, 1)]).then_inc(ada_used, 1)

            def ada_bias(which, lo, hi, bias):
                dve.wait_ge(ada_used, 48 * which + hi * KC)
                own(V.tensor_tensor(mods[:, which, lo * KC:hi * KC], mods[:, which, lo * KC:hi * KC],
                                    col(bias, lo * KC, (hi - lo) * KC), ALU.add))

            def gains(which, k, vec, name):
                own(V.scalar_tensor_tensor(out=scale_cols[:, k, :], in0=mods[:, which, vec * KC:(vec + 1) * KC],
                                           scalar=1.0, in1=col(name, 0, KC), op0=ALU.add, op1=ALU.mult))

            def inverse_root(name):
                dve.wait_ge(a_drained, A_AT[name] + 1)
                own(V.reciprocal(rinv[:, :], rms[:, :]))

            def scaled(dst, src, gain, signal):
                for j in range(KC):
                    V.scalar_tensor_tensor(out=dst[:, j, :], in0=src[:, j, :], scalar=gain[:, j:j + 1],
                                           in1=rinv[:, :], op0=ALU.mult, op1=ALU.mult).then_inc(sem(signal), 1)

            def norm_modulated(name, xn_, gain, shift):
                inverse_root(name)
                scaled(xn_, xT, gain, "xn_ready")
                for j in range(KC):
                    norm_modulated.n += 1
                    dve.wait_ge(sem("h_hi"), norm_modulated.n)
                    V.scalar_tensor_tensor(out=h_lo[:, j, :], in0=xn_[:, j, :], scalar=shift[:, j:j + 1],
                                           in1=h_hi[:, j, :].bitcast(F32), op0=ALU.add,
                                           op1=ALU.subtract).then_inc(sem("h_lo"), 1)
            norm_modulated.n = 0

            def lower(dst, src, upper, signal):
                V.tensor_tensor(dst, src, upper.bitcast(F32), ALU.subtract).then_inc(sem(signal), 1)

            dve.wait_ge(sem("c_act"), 1)
            with repeat(dve, 4, {ada_n: 4}) as i:
                for j in range(4):
                    ada_block(0, i * 4 + j)
            ada_bias(0, 0, 2, "ada_b")
            gains(0, 0, 1, "norm1")
            norm_modulated("ssq1", xn, scale_cols[:, 0, :], mods[:, 0, 0:KC])

            own(V.memset(r_s[0:SH, :], 0.0))
            b = Dr.bank()
            V.tensor_scalar(r_i[0:MH, :], b[0:MH, 0:T], col("b_i", parts=MH), None, ALU.add)
            Dr.free(V.tensor_scalar(r_f[0:MH, :], b[32:32 + MH, 0:T], col("b_f", parts=MH), None, ALU.add),
                    settle=True)

            def log1p_exp(k, n):
                V.scalar_tensor_tensor(out=r_abs[0:n, :], in0=r_f[0:n, :], scalar=-1.0, in1=r_f[0:n, :],
                                       op0=ALU.mult, op1=ALU.max).then_inc(sem("row_abs"), 1)
                dve.wait_ge(sem("row_exp"), k + 1)
                V.tensor_scalar(r_u[0:n, :], r_e[0:n, :], 1.0, None, ALU.add).then_inc(sem("row_u"), 1)
                dve.wait_ge(sem("row_u"), k + 1)
                own(V.tensor_scalar(r_t[0:n, :], r_u[0:n, :], -1.0, None, ALU.add))
                own(V.tensor_tensor(r_t[0:n, :], r_e[0:n, :], r_t[0:n, :], ALU.subtract))
                own(V.reciprocal(r_abs[0:n, :], r_u[0:n, :]))
                own(V.tensor_tensor(r_t[0:n, :], r_t[0:n, :], r_abs[0:n, :], ALU.mult))
                dve.wait_ge(sem("row_ln"), k + 1)
                own(V.tensor_tensor(r_l[0:n, :], r_l[0:n, :], r_t[0:n, :], ALU.add))

            log1p_exp(0, MH)
            R = slice(0, MH)
            own(V.scalar_tensor_tensor(out=r_f[R, :], in0=r_f[R, :], scalar=0.0, in1=r_l[R, :],
                                       op0=ALU.min, op1=ALU.subtract))
            own(V.tensor_tensor_scan(r_abs[R, :], r_f[R, :], r_s[R, :], 0.0, ALU.add, ALU.add))
            own(V.tensor_tensor(r_i[R, :], r_i[R, :], r_abs[R, :], ALU.subtract))
            own(V.tensor_tensor_scan(r_u[R, :], r_i[R, :], r_i[R, :], 0.0, ALU.max, ALU.max))
            V.tensor_tensor(r_t[R, :], r_abs[R, :], r_u[R, :], ALU.add).then_inc(sem("m_rows"), 1)
            V.tensor_scalar(r_f[R, :], r_u[R, :], -1.0, None, ALU.mult).then_inc(sem("neg_m"), 1)

            dve.wait_ge(sem("pos_in"), 16)
            own(V.tensor_copy(posf, pos_i[:, :]))
            for t in range(NT):
                own(V.tensor_scalar(trig[:, 2, t, :], col("inv_freq", 0, 32), posf[:, t:t + 1], None, ALU.mult))
            ang = trig[:, 2, :, :]
            for k, quarter in ((0, 0.25), (1, 0.0)):
                r = trig[:, k, :, :]
                own(V.tensor_scalar(trig[:, 3, :, :], ang, 1.0 / 6.283185307179586, quarter, ALU.mult, ALU.add))
                own(V.tensor_scalar(trig[:, 3, :, :], trig[:, 3, :, :], MAGIC, -MAGIC, ALU.add, ALU.add))
                for n, piece in enumerate(TWO_PI):
                    own(V.scalar_tensor_tensor(out=r, in0=trig[:, 3, :, :], scalar=-piece, in1=ang if n == 0 else r,
                                               op0=ALU.mult, op1=ALU.add))
                if quarter:
                    own(V.tensor_scalar(r, r, 1.5707963267948966, None, ALU.add))
                last = V.tensor_scalar(r, r, PI_BELOW, -PI_BELOW, ALU.min, ALU.max)
                if k == 0:
                    own(last)
            last.then_inc(sem("angles"), 1)

            dve.wait_ge(sem("b_tok_in"), 16)
            for b in range(2):
                for t in range(NT):
                    Dr.free(V.tensor_tensor(toks[:, t, b * 512:(b + 1) * 512], Dr.bank(), b_tok[:, b, :], ALU.add),
                            settle=True)
            dve.wait_ge(sem("trig"), 1)
            for t in range(NT):
                halves = toks[:, t, 0:1024].rearrange("p (h z d) -> p z h d", z=2, d=32)
                cos = trig[:, 0, t, :].unsqueeze(1).broadcast_to([P, 16, 32])
                sin = trig[:, 1, t, :].unsqueeze(1).broadcast_to([P, 16, 32])
                for z in range(2):
                    V.tensor_tensor(turn[:, 0, z, :, :], halves[:, z, :, :], cos, ALU.mult)
                    own(V.tensor_tensor(turn[:, 1, z, :, :], halves[:, z, :, :], sin, ALU.mult))
                V.tensor_tensor(halves[:, 0, :, :], turn[:, 0, 0, :, :], turn[:, 1, 1, :, :],
                                ALU.subtract).then_inc(sem("roped"), 1)
                V.tensor_tensor(halves[:, 1, :, :], turn[:, 0, 1, :, :], turn[:, 1, 0, :, :],
                                ALU.add).then_inc(sem("roped"), 1)
                dve.wait_ge(sem("roped"), 2 * t + 2)
            for t in range(NT):
                Dr.free(V.tensor_tensor(v_tok[:, t, :], Dr.bank(), b_tok[:, 2, :], ALU.add))
            for t in range(NT):
                Dr.free(V.tensor_tensor(v_ext[:, t, :, 0:MD], Dr.bank().rearrange("p (h d) -> p h d", h=MH),
                                        b_tok[:, 3, :].rearrange("p (h d) -> p h d", h=MH), ALU.add))

            def conv(j, src, dst, weights, ready, first):
                dve.wait_ge(a_drained, j + (first + 1))
                w = COLS[weights][0]

                def tap(k):
                    return cols[:, bass.ds(j * CONV + (w + k), 1)]
                own(V.tensor_scalar(dst[:, j, :], src[:, j, :], tap(CONV - 1), None, ALU.mult))
                for back in range(1, CONV):
                    last = V.scalar_tensor_tensor(out=dst[:, j, back:T], in0=src[:, j, 0:T - back],
                                                  scalar=tap(CONV - 1 - back), in1=dst[:, j, back:T],
                                                  op0=ALU.mult, op1=ALU.add)
                    if back < CONV - 1:
                        own(last)
                last.then_inc(ready, 1)
            with repeat(dve, 2 * MH, {own.count: CONV - 1, ada_n: 4}) as j:
                conv(j, zT[:, 0:2 * MH, :], convT, "conv_w", sem("conv_ready"), A_AT["feat"])
                for k in range(4):
                    ada_block(0, j * 4 + (k + 16))
            ada_bias(0, 2, 6, "ada_b")
            gains(0, 1, 4, "norm2")

            b = Dr.bank()
            Dr.free(V.tensor_copy(m_cols.rearrange("p k h t -> p k t h"),
                                  b[:, 0:16].rearrange("p (k t h) -> p k t h", k=2, t=NT)), settle=True)
            dve.sem_inc(sem("m_cols"), 1)

            for h in range(AH):
                b = Dr.bank()
                own(V.tensor_tensor_reduce(probs[:, h, 0:P], b[:, 0:P], mask_ts[:, P:T], 1.0, LOWEST,
                                           ALU.add, ALU.max, mx[:, 2 * h:2 * h + 1]))
                Dr.free(V.tensor_tensor_reduce(probs[:, h, P:3 * P], b[:, P:3 * P], mask_ts[:, :], 1.0, LOWEST,
                                               ALU.add, ALU.max, mx[:, 2 * h + 1:2 * h + 2]), settle=True)
            V.tensor_scalar(nmx, mx, -(AD ** -0.5), None, ALU.mult).then_inc(sem("nmx"), 1)
            for h in range(MH):
                b = Dr.bank()
                V.tensor_tensor(mw[:, h, T:3 * P], b[:, P:T], mask_st[:, 0:P], ALU.add)
                Dr.free(V.tensor_tensor(mw[:, h, 0:T], b[:, 0:T], mask_st[:, :], ALU.add), settle=True)
                dve.sem_inc(sem("m_args"), 1)
            dve.wait_ge(sem("exps"), AH * NT)
            own(V.reciprocal(rsums, sums))
            for h in range(AH):
                for t in range(NT):
                    p = probs[:, h, 0:P] if t == 0 else probs[:, h, P:3 * P]
                    k = h * NT + t
                    V.tensor_scalar(p, p, rsums[:, k:k + 1], None, ALU.mult).then_inc(sem("probs"), 1)
            for h in range(MH):
                dve.wait_ge(sem("m_w"), 2 * h + 2)
                Dr.free(V.scalar_tensor_tensor(out=mw[:, h, :], in0=Dr.bank()[:, 0:3 * P], scalar=MD ** -0.5,
                                               in1=mw[:, h, :], op0=ALU.mult, op1=ALU.mult))
            for h in range(MH):
                Dr.free(V.tensor_copy(nd[:, 2 * h:2 * h + 2, :],
                                      Dr.bank()[:, 0:2 * (MD + 1)].rearrange("p (t d) -> p t d", t=NT)), settle=True)
            den = nd[:, :, MD:MD + 1].rearrange("p a b -> p (a b)")
            own(V.scalar_tensor_tensor(out=m_stat[:, 0, :], in0=den, scalar=-1.0, in1=den,
                                       op0=ALU.mult, op1=ALU.max))
            own(V.tensor_tensor(m_stat[:, 0, :], m_stat[:, 0, :], m_cols[:, 1, :, :].rearrange("p h t -> p (h t)"),
                                ALU.max))
            own(V.reciprocal(m_stat[:, 1, :], m_stat[:, 0, :]))
            own(V.tensor_tensor(nd[:, :, 0:MD], nd[:, :, 0:MD],
                                m_stat[:, 1, :].unsqueeze(2).broadcast_to([P, NT * MH, MD]), ALU.mult))
            for k in range(NT * MH):
                own(V.tensor_tensor_reduce(xn[:, 0, 0:MD], nd[:, k, 0:MD], nd[:, k, 0:MD], 1.0, 0.0,
                                           ALU.mult, ALU.add, m_stat[:, 2, k:k + 1]))
            dve.sem_inc(sem("m_ms"), 1)
            dve.wait_ge(sem("m_rms"), 1)
            own(V.reciprocal(m_stat[:, 4, :], m_stat[:, 3, :]))
            V.tensor_tensor(nd[:, :, 0:MD], nd[:, :, 0:MD],
                            m_stat[:, 4, :].unsqueeze(2).broadcast_to([P, NT * MH, MD]),
                            ALU.mult).then_inc(sem("m_normed"), 1)
            dve.wait_ge(sem("sig_ready"), 1)
            for h in range(MH):
                Dr.free(V.scalar_tensor_tensor(out=ymT[:, h, :], in0=Dr.bank()[:, 0:T], scalar=col("m_norm", h),
                                               in1=zT[:, Z_MO + h, :], op0=ALU.mult, op1=ALU.mult))
            dve.wait_ge(d_drained, D_AT["ymT"] + MH)
            for j in range(2 * MH):
                dve.wait_ge(sem("y_hi"), j + 1)
                lower(y_lo[:, j, :], ymT[:, j, :] if j < MH else yaT[:, j - MH, :], y_hi[:, j, :], "y_lo")
            for j in range(KC):
                Dr.free(V.tensor_tensor(mT[:, j, :], Dr.bank()[:, 0:T], zT[:, Z_GA + j, :], ALU.mult))
                Dr.free(V.tensor_tensor(xn[:, j, :], Dr.bank()[:, 0:T], zT[:, Z_GB + j, :], ALU.mult), settle=True)
                V.tensor_tensor(mT[:, j, :], mT[:, j, :], xn[:, j, :], ALU.add).then_inc(sem("merged"), 1)
            for j in range(KC):
                dve.wait_ge(sem("m_hi"), j + 1)
                lower(h_lo[:, j, :], mT[:, j, :], h_hi[:, j, :], "m_lo")

            def residual(j, bank, gate_col):
                return V.scalar_tensor_tensor(out=xT[:, j, :], in0=bank, scalar=gate_col[:, j:j + 1],
                                              in1=xT[:, j, :], op0=ALU.mult, op1=ALU.add)

            def residual_all(gate_col):
                for k in range(BANKS):
                    b = Dr.bank()
                    residual(2 * k, b[:, 0:T], gate_col)
                    Dr.free(residual(2 * k + 1, b[:, T:2 * T], gate_col), settle=True)

            for j in range(KC):
                Dr.free(residual(j, Dr.bank()[:, 0:T], mods[:, 0, 2 * KC:3 * KC]), settle=True)
            norm_modulated("ssq2", xn, scale_cols[:, 1, :], mods[:, 0, 3 * KC:4 * KC])

            def f_lower(j):
                dve.wait_ge(sem("f_hi"), j + 1)
                lower(f_lo[:, j, :], fT[:, j, :], f_hi[:, j, :], "f_lo")

            def up_chunk(j, behind=True):
                for k in range(2):
                    ada_block(1, j * 2 + k)
                b = Dr.bank()
                dve.wait_ge(a_drained, j + (A_AT["gate"] + 1))
                Dr.free(V.tensor_tensor(fT[:, j, :], b[:, 0:T], fT[:, j, :], ALU.mult))
                if behind:
                    f_lower(j - 1)
            up_chunk(0, False)
            up_chunk(1)
            with repeat(dve, 5, {Dr.count: 4, ada_n: 8}) as i:
                for j in range(4):
                    up_chunk(i * 4 + (j + 2))
            f_lower(FC - 1)
            for j in range(44, 48):
                ada_block(1, j)
            ada_bias(1, 0, 6, "ada_b2")
            residual_all(mods[:, 0, 5 * KC:6 * KC])
            inverse_root("ssqf")
            scaled(xT, xT, col("normf", 0, KC), "x_normed")
            dve.wait_ge(sem("x_normed"), KC)
            gains(1, 0, 1, "norm_mix")
            norm_modulated("ssq_mix", xn2, scale_cols[:, 0, :], mods[:, 1, 0:KC])
            gains(1, 1, 4, "norm_ffn")

            S = slice(0, SH)
            own(V.memset(r_s[S, :], 0.0))
            Dr.free(V.tensor_scalar(r_f[S, :], Dr.bank()[S, 0:T], col("dt_bias", parts=SH), None, ALU.add),
                    settle=True)
            log1p_exp(1, SH)
            own(V.scalar_tensor_tensor(out=r_i[S, :], in0=r_f[S, :], scalar=0.0, in1=r_l[S, :],
                                       op0=ALU.max, op1=ALU.add))
            dve.wait_ge(sem("a_exp"), 1)
            own(V.tensor_scalar(r_t[S, :], r_i[S, :], a_col[S, 0:1], -1.0, ALU.mult, ALU.mult))
            V.tensor_tensor_scan(r_u[S, :], r_t[S, :], r_s[S, :], 0.0, ALU.add, ALU.add).then_inc(sem("dt_rows"), 1)

            own(V.memset(inv_t[:, 0, :], 1.0))
            own(V.tensor_tensor_scan(inv_t[:, 1, :], inv_t[:, 0, :], inv_t[:, 0, :], 0.0, ALU.add, ALU.max))
            own(V.memset(pool_a[:, :, 0:16], 0.0))
            own(V.memset(pool_b[:, :, 0:16], 0.0))
            dve.wait_ge(a_drained, A_AT["win2"] + NPOOL)
            own(V.tensor_copy(pool_a[:, :, 16:PADDED], z2T[:, 0:NPOOL, :]))
            bufs = [pool_a, pool_b]
            for g in range(NPOOL):
                w = POOLS[g] // 2
                a, b = bufs[g % 2], bufs[(g + 1) % 2]
                own(V.tensor_tensor(b[:, g:NPOOL, 16:PADDED], a[:, g:NPOOL, 16:PADDED],
                                    a[:, g:NPOOL, 16 - w:PADDED - w], ALU.add))
            own(V.reciprocal(inv_t[:, 0, :], inv_t[:, 1, :]))
            for g in range(NPOOL):
                win = bufs[(g + 1) % 2][:, g, 16:PADDED]
                own(V.scalar_tensor_tensor(out=win, in0=inv_t[:, 0, :], scalar=1.0 / POOLS[g], in1=win,
                                           op0=ALU.max, op1=ALU.mult))
                V.tensor_tensor(win, win, z2T[:, g, :], ALU.subtract).then_inc(sem("pooled"), 1)
            with repeat(dve, XBC, {own.count: CONV - 1}) as j:
                conv(j, z2T[:, MIXC:MIXC + XBC, :], xbcT, "conv_w2", sem("conv2_ready"), A_AT["win2"] + MIXC)
            for g in range(NPOOL):
                Dr.free(V.tensor_scalar(mixT[:, g, :], Dr.bank()[:, 0:T], col("pool_b", g), col("pool_scale", g),
                                        ALU.add, ALU.mult))
            b = Dr.bank()
            Dr.free(V.tensor_copy(s_cols.rearrange("p k t h -> p (k t h)"), b[:, 0:4 * SH]), settle=True)
            for j in range(4):
                t, side = divmod(j, 2)
                Dr.free(V.tensor_copy(xs_tok[:, t, side * 512:(side + 1) * 512], Dr.bank()))
            for g in range(SG):
                b = Dr.bank()
                V.scalar_tensor_tensor(out=cbT[:, g, 0:T], in0=mask_st[:, :], scalar=0.0, in1=b[:, 0:T],
                                       op0=ALU.is_equal, op1=ALU.mult)
                Dr.free(V.scalar_tensor_tensor(out=cbT[:, g, T:3 * P], in0=mask_st[:, 0:P], scalar=0.0,
                                               in1=b[:, T:3 * P], op0=ALU.is_equal, op1=ALU.mult), settle=True)

            def ssd_args(h):
                b = Dr.bank()
                own(V.tensor_scalar(ssd_w[:, h % 4, 0:T], b[:, 0:T], s_cols[:, 0, 0, h:h + 1], 0.0,
                                    ALU.subtract, ALU.min))
                Dr.free(V.tensor_scalar(ssd_w[:, h % 4, T:3 * P], b[:, P:T], s_cols[:, 0, 1, h:h + 1], 0.0,
                                        ALU.subtract, ALU.min), settle=True)
                dve.sem_inc(sem("ssd_args"), 1)

            def ssd_weights(h):
                g = h // (SH // SG)
                dve.wait_ge(sem("ssd_exp"), h + 1)
                for s, (a, e) in enumerate(((0, T), (T, 3 * P))):
                    w = ssd_w[:, h % 4, a:e]
                    V.scalar_tensor_tensor(out=w, in0=w, scalar=s_cols[:, 1, s, h:h + 1], in1=cbT[:, g, a:e],
                                           op0=ALU.mult, op1=ALU.mult).then_inc(sem("ssd_w"), 1)

            def ssd_out(j):
                Dr.free(V.scalar_tensor_tensor(out=mixT[:, NPOOL + j, :], in0=xbcT[:, j, :], scalar=col("d_skip", j),
                                               in1=Dr.bank()[:, 0:T], op0=ALU.mult, op1=ALU.add), settle=True)
                V.tensor_tensor(mixT[:, NPOOL + j, :], mixT[:, NPOOL + j, :], z2T[:, NPOOL + j, :],
                                ALU.mult).then_inc(sem("ssd_y"), 1)
            dve.wait_ge(sem("z_silu"), 1)
            dve.wait_ge(sem("xbc"), XBC)
            for j in range(KC + 1):
                if j < KC:
                    ssd_args(2 * j)
                    ssd_args(2 * j + 1)
                if j >= 1:
                    ssd_weights(2 * j - 2)
                    ssd_weights(2 * j - 1)
                    ssd_out(j - 1)
            inverse_root("ssq_ssd")
            scaled(mixT[:, NPOOL:MIXC, :], mixT[:, NPOOL:MIXC, :], col("ssd_norm", 0, KC), "ssd_normed")
            for j in range(MIXC):
                dve.wait_ge(sem("mix_hi"), j + 1)
                lower(mix_lo[:, j, :], mixT[:, j, :], mix_hi[:, j, :], "mix_lo")
            residual_all(mods[:, 1, 2 * KC:3 * KC])
            norm_modulated("ssq_ffn", xn2, scale_cols[:, 1, :], mods[:, 1, 3 * KC:4 * KC])

            for j in range(2 * QH):
                Dr.free(V.tensor_copy(scores[:, :, j, :], Dr.bank()[:, 0:NT * NK].rearrange("p (t n) -> p t n", t=NT)),
                        settle=j == 2 * QH - 1)
            own(V.tensor_tensor_scan(iota_k, ones[:, :], mask_ts[:, 0:P], -1.0, ALU.add, ALU.max))

            def apart(ins):
                own(ins)
                dve.sem_inc(sem("top_steps"), 1)

            def top16(vals, ids, src, spare):
                apart(V.max(vals[:, 0:8], src))
                V.max_index(ids[:, 0:8], vals[:, 0:8], src)
                apart(V.match_replace(spare, vals[:, 0:8], src, LOWEST))
                apart(V.max(vals[:, 8:16], spare))
                apart(V.max_index(ids[:, 8:16], vals[:, 8:16], spare))

            with repeat(dve, NT * QH, {own.count: 1 + 4 * 3 + 1 + 1 + 5}) as k:
                flat = scores.rearrange("p t j n -> p (t j) n")
                apart(V.tensor_copy(work, flat[:, bass.ds(k * 2, 2), :]))
                for z in range(2):
                    top16(v16[:, z, :], i16[:, z, :], work[:, z, :], work2)
                own(V.tensor_copy(idx[:, k, :, :], i16[:, 0:2, :]))
                apart(V.tensor_tensor(cand[:, :, :], v16[:, 0, :].unsqueeze(2).broadcast_to([P, TOPK, TOPK]),
                                    v16[:, 1, :].unsqueeze(1).broadcast_to([P, TOPK, TOPK]), ALU.add))
                top16(v16[:, 0, :], i16[:, 2, :], cand[:, :, :].rearrange("p a b -> p (a b)"), cand2[:, :])
                own(V.tensor_copy(top_v[:, k, :], v16[:, 0, :]))
                own(V.tensor_scalar(i16[:, 0, :], i16[:, 2, :], 4, None, ALU.logical_shift_right))
                own(V.tensor_scalar(i16[:, 1, :], i16[:, 2, :], 15, None, ALU.bitwise_and))
                own(V.tensor_copy(pick_a[:, k, :], i16[:, 0, :]))
                own(V.tensor_copy(pick_b[:, k, :], i16[:, 1, :]))
            for z, pick in ((0, pick_a), (1, pick_b)):
                own(V.tensor_tensor(eq, pick.rearrange("p a k -> p (a k)").unsqueeze(2).broadcast_to([P, 256, TOPK]),
                                    iota_k[:, 0:TOPK].unsqueeze(1).broadcast_to([P, 256, TOPK]), ALU.is_equal))
                own(V.tensor_tensor(eq.rearrange("p (a k) i -> p a k i", k=TOPK),
                                    eq.rearrange("p (a k) i -> p a k i", k=TOPK),
                                    idx[:, :, z, :].unsqueeze(2).broadcast_to([P, NT * QH, TOPK, TOPK]), ALU.mult))
                own(V.tensor_reduce(picked[:, z, :], eq, AX.X, ALU.add))
            gates = picked[:, 2, :].rearrange("p (a k) -> p a k", k=TOPK)
            V.tensor_tensor(gates, top_v, top_v[:, :, 0:1].broadcast_to([P, NT * QH, TOPK]),
                            ALU.subtract).then_inc(sem("gate_args"), 1)
            dve.wait_ge(sem("gate_exp"), 1)
            own(V.tensor_reduce(mx, gates, AX.X, ALU.add))
            own(V.reciprocal(rsums, mx))
            V.tensor_tensor(gates, gates, rsums.unsqueeze(2).broadcast_to([P, NT * QH, TOPK]),
                            ALU.mult).then_inc(sem("picked"), 1)
            for z in range(3):
                Dr.free(V.tensor_copy(picksT[:, z, :], Dr.bank()[:, 0:T]), settle=True)

            hots = Count()

            def one_hots(t, keys):
                n = hots.n
                hots.n += 1
                if n >= ONEHOTS:
                    dve.wait_ge(d_ready, hots.value(ONEHOTS) + D_AT["spread"])
                h = hot[:, n % ONEHOTS, :, :]
                V.tensor_scalar(h[:, 0, :], iota_k, picksT[:, 0, bass.ds(t, 1)], None,
                                ALU.is_equal).then_inc(sem("one_hots"), 1)
                V.tensor_scalar(h[:, 1, 0:GATED], iota_k[:, keys:keys + GATED], picksT[:, 1, bass.ds(t, 1)],
                                picksT[:, 2, bass.ds(t, 1)], ALU.is_equal, ALU.mult).then_inc(sem("one_hots"), 1)

            def gate_experts(t, keys):
                b = Dr.bank()
                u = U[:, keys:keys + GATED, bass.ds(t, 1)].rearrange("p e t -> p (e t)")
                Dr.free(V.tensor_tensor(u, b[:, 0:GATED], u, ALU.mult))

            dve.wait_ge(a_drained, A_AT["experts"] + GATED)
            for t in range(4):
                one_hots(t, 0)
            with repeat(dve, (T - 4) // 4, {hots: 4, Dr.count: 4}) as i:
                for t in range(4):
                    gate_experts(i * 4 + t, 0)
                    one_hots(i * 4 + (t + 4), 0)
            for t in range(T - 4, T):
                gate_experts(t, 0)
            dve.wait_ge(a_drained, A_AT["experts"] + P)

            def u_lower(j, slot, n):
                dve.wait_ge(sem("u_hi"), n)
                lower(u_lo[:, slot, :], U[:, j, :], u_hi[:, slot, :], "u_lo")
            for t in range(4):
                u_lower(t, t, t + 1) if t < 2 else None
                one_hots(t, GATED)
            with repeat(dve, (T - 16) // 16, {hots: 16, Dr.count: 16}) as i:
                for j in range(4):
                    for t in range(4):
                        gate_experts(i * 16 + (4 * j + t), GATED)
                        one_hots(i * 16 + (4 * j + t + 4), GATED)
                    u_lower(i * 4 + (j + 2), (j + 2) % 4, i * 4 + (j + 3))
            for j in range(GATED - 4, GATED):
                for t in range(4):
                    gate_experts(4 * j + t, GATED)
                    if j < GATED - 1:
                        one_hots(4 * j + t + 4, GATED)
                if j < GATED - 2:
                    u_lower(j + 2, (j + 2) % 4, j + 3)
            with repeat(dve, GATED // 4, {hots: 0}) as i:
                for j in range(4):
                    u_lower(i * 4 + (j + GATED), j, i * 4 + (j + GATED + 1))
            dve.wait_ge(a_drained, A_AT["expert_up"])
            for k in range(BANKS):
                dve.wait_ge(a_ready, A_AT["expert_up"] + k + 1)
                b = psA[:, (A_AT["expert_up"] + k) % BANKS, :]
                residual(2 * k, b[:, 0:T], mods[:, 1, 5 * KC:6 * KC])
                residual(2 * k + 1, b[:, T:2 * T], mods[:, 1, 5 * KC:6 * KC]).then_inc(a_drained, 1)
            inverse_root("ssq_final")
            scaled(mT, xT, col("norm_final", 0, KC), "y_ready")

        @block.tensor
        def _(pe):
            A = Fill(pe, psA, a_ready, a_drained)
            Dr = Fill(pe, psD, d_ready, d_drained)
            mm = nc.tensor.matmul
            halves = Count()
            norms = Count()

            def half():
                n = halves.n
                halves.n += 1
                pe.wait_ge(lo_ready, halves.value())
                s = slice(n % SLOTS * HALF, (n % SLOTS + 1) * HALF)
                return w_hi[:, s], w_lo[:, s]

            def begun(ins):
                if halves.n > 1:
                    ins.then_inc(half_used, 1)

            def stage_ends():
                pe.drain().then_inc(half_used, 1)

            def product(o, w, m, start, stop, opens=False):
                first = mm(o, w[0], m[0], start=start, stop=False, skip_group_check=True)
                if opens:
                    begun(first)
                mm(o, w[0], m[1], start=False, stop=False, skip_group_check=True)
                return mm(o, w[1], m[0], start=False, stop=stop, skip_group_check=True)

            def ssq(src):
                norms.n += 1
                pe.wait_ge(sem("sq_ready"), norms.n)
                b = A.bank()
                for j in range(KC):
                    last = mm(b[:, 0:T], ones[:, :], src[:, j, :], start=j == 0, stop=j == KC - 1)
                A.full(last)

            def half_blocks(b, w, rhs, first, last, ready=None):
                for k in range(4):
                    if ready is not None:
                        pe.wait_ge(*ready(first + k))
                    done = product(b[:, 0:T], [part_[:, k * P:(k + 1) * P] for part_ in w],
                                   [part_[:, first + k, :] for part_ in rhs],
                                   start=first + k == 0, stop=last and k == 3, opens=k == 0)
                return done

            def unit(R, rhs, ready=None, beside=None):
                b = R.bank()
                for h in range(2):
                    done = half_blocks(b, half(), rhs, 4 * h, h == 1, ready)
                    if h == 1:
                        R.full(done)
                    if beside:
                        beside(h)

            def columns(R, n, rhs, second=None, ends=True):
                per = 4 if second is None else 8
                turns, rest = divmod(n, per)

                def body(count):
                    for j in range(count):
                        unit(R if second is None or j % 2 == 0 else second, rhs)
                if turns and R.count.n < BANKS:
                    turns -= 1
                    body(per)
                counts = {halves: 2 * per, R.count: 4}
                if second is not None:
                    counts[second.count] = 4
                if turns:
                    with repeat(pe, turns, counts):
                        body(per)
                body(rest)
                if ends:
                    stage_ends()

            def row_unit(banks, rhs, first, last, R=None, beside=None):
                for h in range(2):
                    w = half()
                    for k in range(4):
                        n = 4 * h + k
                        done = product(banks[n // 2][:, (n % 2) * T:(n % 2 + 1) * T],
                                       [part_[:, k * P:(k + 1) * P] for part_ in w], rhs,
                                       start=first and n % 2 == 0, stop=last, opens=k == 0)
                        if last and n % 2 == 1:
                            R.full(done)
                    if beside:
                        beside(h)

            def row_blocks(n, rhs, ready):
                banks = [Dr.bank() for _ in range(BANKS)]

                def one(k, first=False, last=False):
                    pe.wait_ge(*ready(k))
                    row_unit(banks, [part_[:, k, :] for part_ in rhs], first, last, Dr)
                one(0, first=True)
                turns, rest = divmod(n - 2, 4)
                with repeat(pe, turns, {halves: 8}) as i:
                    for j in range(4):
                        one(i * 4 + (j + 1))
                for j in range(rest):
                    one(turns * 4 + 1 + j)
                one(n - 1, last=True)
                stage_ends()

            pe.wait_ge(sem("consts"), 1)
            ssq(xn)
            h_parts = (h_hi, h_lo)
            unit(Dr, h_parts, lambda k: (sem("h_lo"), k + 1))
            stage_ends()
            for blk in range(TOK_BLOCKS):
                bs = [Dr.bank() for _ in range(NT)]
                for kc in range(KC):
                    w = half()
                    for t in range(NT):
                        last = product(bs[t], [part_[:, kc, t * P:(t + 1) * P] for part_ in h_parts], w,
                                       start=kc == 0, stop=kc == KC - 1, opens=t == 0)
                        if kc == KC - 1:
                            Dr.full(last)
            stage_ends()
            columns(A, 28, h_parts)

            pe.wait_ge(sem("exp_m"), 1)
            b = Dr.bank()
            for k, src in ((0, r_i), (1, r_e)):
                for t in range(NT):
                    at = (k * NT + t) * MH
                    last = nc.tensor.transpose(b[:, at:at + MH], src[0:MH, t * P:(t + 1) * P], ident[0:MH, 0:MH])
            Dr.full(last)
            pe.wait_ge(sem("roped"), 2 * NT)
            for j in range(8):
                b = A.bank()
                z, pr = j % 2, j // 2
                for t in range(NT):
                    last = nc.tensor.transpose(b[:, t * P:(t + 1) * P],
                                               toks[:, t, z * 512 + pr * P:z * 512 + (pr + 1) * P], ident[:, :])
                A.full(last)
            for h in range(AH):
                pe.wait_ge(a_drained, A_AT["qkT"] + 2 * (h // 2) + 2)
                lo = (h % 2) * AD
                q, k = qkT[lo:lo + AD, 0, h // 2, :], qkT[lo:lo + AD, 1, h // 2, :]
                b = Dr.bank()
                mm(b[:, 0:P], q[:, 0:P], k[:, 0:P], start=True, stop=True)
                Dr.full(mm(b[:, P:3 * P], q[:, P:T], k[:, 0:T], start=True, stop=True))
            pe.wait_ge(sem("neg_m"), 1)
            for h in range(MH):
                b = Dr.bank()
                Dr.full(mm(b[:, 0:T], sel(h, MH), r_f[0:MH, :], start=True, stop=True))
            pe.wait_ge(sem("m_qk"), 2 * MH)
            for h in range(MH):
                q, k = convT[:, h, :], convT[:, MH + h, :]
                b = Dr.bank()
                mm(b[:, 0:T], k[:, 0:P], q, start=True, stop=True)
                Dr.full(mm(b[:, T:3 * P], k[:, P:T], q[:, P:T], start=True, stop=True))
            for h in range(AH):
                pe.wait_ge(sem("probs"), NT * (h + 1))
                b = A.bank()
                for n in range(3):
                    last = nc.tensor.transpose(b[:, n * P:(n + 1) * P],
                                               probs[:, h, (0, P, 2 * P)[n]:(0, P, 2 * P)[n] + P], ident[:, :])
                A.full(last)
            for pr in range(4):
                b = A.bank()
                for z in range(2):
                    h = 2 * pr + z
                    pe.wait_ge(a_drained, A_AT["probsT"] + h + 1)
                    o = b[z * AD:(z + 1) * AD, :]
                    mm(o[:, 0:T], v_tok[:, 0, h * AD:(h + 1) * AD], probsT[:, h, 0:T],
                       start=True, stop=False, skip_group_check=True)
                    last = mm(o[:, P:T], v_tok[:, 1, h * AD:(h + 1) * AD], probsT[:, h, T:3 * P],
                              start=False, stop=True, skip_group_check=True)
                A.full(last)
            for h in range(MH):
                pe.wait_ge(d_drained, D_AT["m_scores"] + h + 1)
                b = Dr.bank()
                mm(b[:, 0:MD + 1], mw[:, h, 0:P], v_ext[:, 0, h, :], start=True, stop=True)
                mm(b[:, MD + 1:2 * (MD + 1)], mw[:, h, P:T], v_ext[:, 0, h, :], start=True, stop=False)
                Dr.full(mm(b[:, MD + 1:2 * (MD + 1)], mw[:, h, T:3 * P], v_ext[:, 1, h, :], start=False, stop=True))
            pe.wait_ge(sem("m_normed"), 1)
            for h in range(MH):
                b = Dr.bank()
                for t in range(NT):
                    last = nc.tensor.transpose(b[:, t * P:(t + 1) * P], nd[:, 2 * h + t, 0:MD], ident[:, :])
                Dr.full(last)
            pe.wait_ge(sem("y_lo"), 8)
            with repeat(pe, 2, {halves: 8, Dr.count: 8}):
                for _ in range(8):
                    b = Dr.bank()
                    y = [part_[:, _ % 2 * 4:_ % 2 * 4 + 4, :] for part_ in (y_hi, y_lo)]
                    Dr.full(half_blocks(b, half(), y, 0, True))
            stage_ends()
            pe.wait_ge(sem("m_lo"), KC)
            columns(Dr, 8, h_parts)
            ssq(xn)
            pe.wait_ge(sem("h_lo"), 2 * KC)
            columns(A, 44, h_parts, Dr)
            row_blocks(FC, (f_hi, f_lo), lambda k: (sem("f_lo"), k + 1))
            ssq(xn2)
            ssq(xn2)
            unit(Dr, h_parts, lambda k: (sem("h_lo"), 2 * KC + k + 1))
            stage_ends()
            columns(A, 24, h_parts)
            pe.wait_ge(sem("pool_w_in"), 16)
            for g in range(NPOOL):
                pe.wait_ge(sem("pooled"), g + 1)
                b = Dr.bank()
                Dr.full(mm(b[:, 0:T], pool_wt[:, g, :], (pool_b, pool_a)[g % 2][:, g, 16:PADDED],
                           start=True, stop=True))
            pe.wait_ge(sem("dt_rows"), 1)
            b = Dr.bank()
            for k, src in ((0, r_u), (1, r_i)):
                for t in range(NT):
                    at = (k * NT + t) * SH
                    last = nc.tensor.transpose(b[:, at:at + SH], src[0:SH, t * P:(t + 1) * P], ident[0:SH, 0:SH])
            Dr.full(last)
            pe.wait_ge(sem("xbc"), XBC)
            for j in range(4):
                t, side = divmod(j, 2)
                b = Dr.bank()
                for k in range(4):
                    last = nc.tensor.transpose(b[:, k * P:(k + 1) * P], xbcT[:, side * 4 + k, t * P:(t + 1) * P],
                                               ident[:, :])
                Dr.full(last)
            for g in range(SG):
                bs_, cs_ = xbcT[:, KC + g, :], xbcT[:, KC + SG + g, :]
                b = Dr.bank()
                mm(b[:, 0:T], bs_[:, 0:P], cs_, start=True, stop=True)
                Dr.full(mm(b[:, T:3 * P], bs_[:, P:T], cs_[:, P:T], start=True, stop=True))

            def ssd_decay(h):
                b = Dr.bank()
                Dr.full(mm(b[:, 0:T], sel(h, SH), r_u[0:SH, :], start=True, stop=True))

            def ssd_pair(j):
                b = Dr.bank()
                for z in range(2):
                    h = 2 * j + z
                    pe.wait_ge(sem("ssd_w"), 2 * h + 2)
                    o = b[z * SP:(z + 1) * SP, :]
                    w = ssd_w[:, h % 4, :]
                    mm(o[:, 0:T], xs_tok[:, 0, h * SP:(h + 1) * SP], w[:, 0:T], start=True, stop=False,
                       skip_group_check=True)
                    last = mm(o[:, P:T], xs_tok[:, 1, h * SP:(h + 1) * SP], w[:, T:3 * P], start=False, stop=True,
                              skip_group_check=True)
                Dr.full(last)
            for j in range(KC + 1):
                if j < KC:
                    ssd_decay(2 * j)
                    ssd_decay(2 * j + 1)
                if j >= 1:
                    ssd_pair(j - 1)
            ssq(xn2)
            row_blocks(MIXC, (mix_hi, mix_lo), lambda k: (sem("mix_lo"), k + 1))
            ssq(xn2)
            pe.wait_ge(sem("h_lo"), 4 * KC)
            pe.wait_ge(sem("keys_in"), 16)

            def key_scores(j):
                pe.wait_ge(a_drained, A_AT["query"] + j + 1)
                b = Dr.bank()
                for t in range(NT):
                    last = mm(b[:, t * NK:(t + 1) * NK], xn2[:, j % 4, t * P:(t + 1) * P], keysT[:, j, :],
                              start=True, stop=True)
                Dr.full(last)
            for j in range(2 * QH):
                unit(A, h_parts)
                if j == 2 * QH - 1:
                    stage_ends()
                if j >= 1:
                    key_scores(j - 1)
            key_scores(2 * QH - 1)
            columns(A, GATED, h_parts, ends=False)
            pe.wait_ge(sem("picked"), 1)
            for z in range(3):
                b = Dr.bank()
                for t in range(NT):
                    last = nc.tensor.transpose(b[:, t * P:(t + 1) * P], picked[:, z, t * P:(t + 1) * P], ident[:, :])
                Dr.full(last)
            one_hot = Count()

            def spread():
                n = one_hot.n
                one_hot.n += 1
                at = 2 * (n + 1)
                pe.wait_ge(sem("one_hots"), at if one_hot.loop is None else one_hot.loop * 2 + at)
                b = Dr.bank()
                h = hot[:, n % ONEHOTS, :, :]
                Dr.full(mm(b[:, 0:GATED], h[:, 0, :], h[:, 1, 0:GATED], start=True, stop=True))

            def two_tokens(_):
                spread()
                spread()
            with repeat(pe, GATED // 4, {halves: 8, A.count: 4, Dr.count: 16, one_hot: 16}):
                for _ in range(4):
                    unit(A, h_parts, beside=two_tokens)
            stage_ends()
            banks = [A.bank() for _ in range(BANKS)]

            def expert(j, n, first=False, last=False, beside=None):
                pe.wait_ge(sem("u_lo"), n)
                s = j % 4
                row_unit(banks, (u_hi[:, s, :], u_lo[:, s, :]), first, last, A, beside)
            for j in range(4):
                expert(j, j + 1, first=j == 0, beside=two_tokens)
            with repeat(pe, GATED // 4 - 1, {halves: 8, Dr.count: 16, one_hot: 16}) as i:
                for j in range(4):
                    expert(j, i * 4 + (j + 5), beside=two_tokens)
            with repeat(pe, GATED // 4 - 1, {halves: 8}) as i:
                for j in range(4):
                    expert(j, i * 4 + (j + GATED + 1))
            for j in range(4):
                expert(j, P - 3 + j, last=j == 3)
            ssq(U[:, 0:KC, :])


def kernel(**inputs):
    import numpy as np
    import concourse.bacc as bacc
    from concourse.bass_utils import run_bass_kernel_spmd

    a = {k: np.asarray(v) for k, v in inputs.items()}
    f32 = np.float32

    def chunks(v):
        return v.reshape(-1, P).T

    def columns(w):
        n = w.shape[1] // P
        return np.ascontiguousarray(w.reshape(KC, P, n, P).transpose(2, 1, 0, 3)).reshape(n, P, D)

    def padded(at):
        out = np.zeros((D, P), f32)
        for src, to in at:
            out[:, to:to + src.shape[1]] = src
        return columns(out)

    w_in, b_in = a["w_in"][0], a["b_in"][0]
    tok_cols = [slice(2056 + 512 * k, 2568 + 512 * k) for k in range(3)] + [slice(1024, 1536)]
    feat_cols = [slice(0, 1024), slice(1536, 2048), slice(3592, 5640)]
    tok = np.stack([w_in[:, s] for s in tok_cols])
    tok = np.ascontiguousarray(tok.reshape(4, 4, 2, P, 512).transpose(0, 1, 3, 2, 4)).reshape(16, P, D)
    w_gate, w_up = a["w_gate"][0], a["w_up"][0]
    gate_up = np.stack([w_gate.reshape(D, FC, P), w_up.reshape(D, FC, P)], axis=2).reshape(D, 2 * FF)
    w_in2 = a["w_in_2"][0]
    down = a["expert_down_2"][0].reshape(P, P, KC, P)
    down = np.ascontiguousarray(down.transpose(1, 3, 2, 0)).reshape(P, P, D)
    keys = np.stack([a["sub_keys1_2"][0], a["sub_keys2_2"][0]], axis=1)
    half = np.arange(32, dtype=f32) / f32(32)
    per_part = {
        "ada_b": chunks(a["ada_b"][0]), "norm1": chunks(a["norm1_g"][0]), "norm2": chunks(a["norm2_g"][0]),
        "normf": chunks(a["normf_g"]), "b_feat": chunks(np.concatenate([b_in[s] for s in feat_cols])),
        "conv_w": a["conv_w"][0].reshape(CONV, 8, P).transpose(2, 1, 0).reshape(P, 32),
        "conv_b": chunks(a["conv_b"][0]), "m_norm": chunks(a["m_norm_g"][0]), "ada_b2": chunks(a["b_ada_2"][0]),
        "norm_mix": chunks(a["norm_mix_2"][0]), "norm_ffn": chunks(a["norm_ffn_2"][0]),
        "norm_final": chunks(a["norm_final_2"]), "pool_b": a["pool_b_2"][0].T, "pool_scale": a["pool_scale_2"][0].T,
        "conv_w2": a["conv_w_2"][0].reshape(CONV, XBC, P).transpose(2, 1, 0).reshape(P, 48),
        "conv_b2": chunks(a["conv_b_2"][0]), "d_skip": chunks(np.repeat(a["d_skip_2"][0], SP)),
        "ssd_norm": chunks(a["ssd_norm_2"][0]), "b_i": b_in[2048:2052, None], "b_f": b_in[2052:2056, None],
        "dt_bias": a["dt_bias_2"][0][:, None], "a_log": a["a_log_2"][0][:, None],
        "inv_freq": np.broadcast_to(np.power(f32(10000.0), -half).astype(f32), (P, 32)),
    }
    cols = np.zeros((P, NCOLS), f32)
    for name, (at, width) in COLS.items():
        cols[:per_part[name].shape[0], at:at + width] = per_part[name]
    arrays = {
        "x": np.ascontiguousarray(a["x"][0].T.reshape(KC, P, T).transpose(1, 0, 2)),
        "c": a["c"], "c_2": a["c_2"],
        "pos": np.ascontiguousarray(a["positions"][0].reshape(NT, P).T),
        "cols_in": cols,
        "bias_tok": np.stack([b_in[s] for s in tok_cols]),
        "gates": padded([(w_in[:, 2048:2052], 0), (w_in[:, 2052:2056], 32)]),
        "dt": padded([(w_in2[:, 3072:3088], 0)]),
        "pool_w": np.ascontiguousarray(a["pool_w_2"][0].transpose(1, 0, 2)),
        "keys": np.ascontiguousarray(keys.reshape(16, NK, P).transpose(2, 0, 1)),
        "ada": np.ascontiguousarray(a["ada_w"][0].T).reshape(48, P, D),
        "ada2": np.ascontiguousarray(a["w_ada_2"][0].T).reshape(48, P, D),
        "tok": tok,
        "feat": columns(np.concatenate([w_in[:, s] for s in feat_cols], axis=1)),
        "proj": columns(np.concatenate([a["p_mlstm"][0], a["p_moba"][0]], axis=0)),
        "wout": columns(a["w_out"][0]),
        "gateup": columns(gate_up),
        "down": a["w_down"][0].reshape(FC, P, D),
        "win2": columns(w_in2[:, 0:3072]),
        "wout2": a["w_out_2"][0].reshape(MIXC, P, D),
        "query": columns(a["w_query_2"][0]),
        "expert_down": down,
        "expert_up": a["expert_up_2"][0].reshape(P, P, D),
    }
    nc = bacc.Bacc("TRN2", target_bir_lowering=False, num_devices=1)
    aps = {n: nc.dram_tensor(n, v.shape, mybir.dt.from_np(v.dtype), kind="ExternalInput").ap()
           for n, v in arrays.items()}
    out = nc.dram_tensor("out", (P, KC, T), F32, kind="ExternalOutput").ap()
    two_mixers_program(nc, **aps, out=out)
    r = run_bass_kernel_spmd(nc, [arrays], core_ids=[0])
    y = r.results[0]["out"]
    return np.ascontiguousarray(y.transpose(1, 0, 2).reshape(D, T).T)[None]
```

```python
from contextlib import ExitStack, contextmanager

import concourse.bass as bass
from concourse import mybir

F32 = mybir.dt.float32
F32R = mybir.dt.float32r
I32 = mybir.dt.int32
U32 = mybir.dt.uint32
ALU = mybir.AluOpType
ACT = mybir.ActivationFunctionType
AX = mybir.AxisListType

P = 128
T = 256
NT = T // P
D = 1024
KC = D // P
MH, MD = 4, 128
AH, AD = 8, 64
FF = 2816
FC = FF // P
CONV = 4
SH, SP = 16, 64
SG = 2
POOLS = (2, 4, 8, 16)
NPOOL = len(POOLS)
XBC = 12
MIXC = NPOOL + KC
Z2_Z, Z2_POOL = XBC, XBC + KC
QH, NK, TOPK = 8, 128, 16
EPS = 1e-6
FAR = -1e30
LOWEST = -3.0e38
LATE = 64
EARLY = LATE - 16
MAGIC = 12582912.0
TWO_PI = (6.28125, 0.0019350051879882812, 3.0199157663446432e-07)
PI_BELOW = 3.1415925

Z_MO, Z_GA, Z_GB, Z_N = 8, 12, 20, 28
TOK_BLOCKS = 4

COLS = {}
for _name, _width in (
    ("ada_b", 48), ("norm1", 8), ("norm2", 8), ("normf", 8), ("b_feat", Z_N), ("conv_w", 32), ("conv_b", 8),
    ("m_norm", 4), ("ada_b2", 48), ("norm_mix", 8), ("norm_ffn", 8), ("norm_final", 8), ("pool_b", 4),
    ("pool_scale", 4), ("conv_w2", 48), ("conv_b2", 12), ("d_skip", 8), ("ssd_norm", 8), ("b_i", 1), ("b_f", 1),
    ("dt_bias", 1), ("a_log", 1), ("inv_freq", 32),
):
    COLS[_name] = (sum(w for _, w in COLS.values()), _width)
NCOLS = sum(w for _, w in COLS.values())

STREAM = (("gates", 1), ("tok", 16), ("feat", 28), ("proj", 8), ("wout", 8), ("gateup", 44), ("down", 22),
          ("dt", 1), ("win2", 24), ("wout2", 12), ("query", 16), ("expert_down", 128), ("expert_up", 128))
UNITS = sum(n for _, n in STREAM)
SLOTS = 4
HALF = 512

RING_A = (("ssq1", 1), ("mixers", 48), ("ssq2", 1), ("gate", 22),
          ("ssqf", 1), ("ssq_mix", 1), ("win2", 20), ("ssd_decay", 20), ("ssq_ssd", 1), ("ssq_ffn", 1), ("query", 16),
          ("experts", 128), ("expert_up", 4), ("ssq_final", 1))
RING_D = (("gates", 1), ("tok", 8), ("gate_cols", 1), ("attn_scores", 8), ("m_decay", 4), ("m_scores", 4),
          ("m_out", 4), ("ymT", 4), ("proj", 16), ("wout", 8), ("up", 22), ("down", 4), ("dt", 1), ("dt_cols", 1),
          ("xs_tok", 4), ("cb", 2), ("ssd", 8), ("pool", 4), ("wout2", 4), ("scores", 16), ("picksT", 3),
          ("spread", T))
BANKS = 4


def starts(stages):
    at, n = {}, 0
    for name, count in stages:
        at[name] = n
        n += count
    return at


A_AT, D_AT = starts(RING_A), starts(RING_D)


BESIDE_Z = {8: ("qkT", 0), 9: ("qkT", 2), 10: ("qkT", 4), 11: ("qkT", 6), 17: ("probsT", 0), 18: ("probsT", 2),
            19: ("probsT", 4), 20: ("probsT", 6), 21: ("attn", 0), 22: ("attn", 2)}
MIXER_BANKS = {}
for _u in range(Z_N):
    MIXER_BANKS["z", _u] = A_AT["mixers"] + len(MIXER_BANKS)
    if _u in BESIDE_Z:
        for _k in range(2):
            MIXER_BANKS[BESIDE_Z[_u][0], BESIDE_Z[_u][1] + _k] = A_AT["mixers"] + len(MIXER_BANKS)


def decay_bank(h):
    return A_AT["ssd_decay"] + h + min(h // 2 + 1, NPOOL)


def pool_bank(g):
    return A_AT["ssd_decay"] + 3 * g


class Count:

    def __init__(self):
        self.n = 0
        self.loop = None

    def value(self, back=0):
        return self.n - back if self.loop is None else self.loop + (self.n - back)


@contextmanager
def repeat(eng, times, per):
    before = {c: c.n for c in per}
    with eng.Fori(0, times) as i:
        for c, k in per.items():
            c.loop = i * k
        yield i
    for c, k in per.items():
        assert c.n - before[c] == k, (c.n - before[c], k)
        c.loop, c.n = None, before[c] + k * times


class Own:

    def __init__(self, eng, sem):
        self.eng, self.sem, self.count = eng, sem, Count()

    def __call__(self, ins):
        ins.then_inc(self.sem, 1)
        self.count.n += 1
        self.eng.wait_ge(self.sem, self.count.value())


class Fill:

    def __init__(self, pe, psum, ready, drained):
        self.pe, self.psum, self.ready, self.drained, self.count = pe, psum, ready, drained, Count()

    def bank(self):
        n = self.count.n
        self.count.n += 1
        assert n >= BANKS or self.count.loop is None
        if n >= BANKS:
            self.pe.wait_ge(self.drained, self.count.value(BANKS))
        return self.psum[:, n % BANKS, :]

    def full(self, ins):
        ins.then_inc(self.ready, 1)


class Empty:

    def __init__(self, eng, psum, ready, drained):
        self.eng, self.psum, self.ready, self.drained, self.count = eng, psum, ready, drained, Count()

    def bank(self):
        n = self.count.n
        self.count.n += 1
        self.eng.wait_ge(self.ready, self.count.value())
        return self.psum[:, n % BANKS, :]

    def free(self, ins, settle=False):
        ins.then_inc(self.drained, 1)
        if settle:
            self.eng.wait_ge(self.drained, self.count.value())


def two_mixers_program(nc, x, c, c_2, pos, cols_in, bias_tok, pool_w, keys, ada, ada2, gates, tok, feat, proj,
                       wout, gateup, down, dt, win2, wout2, query, expert_down, expert_up, out):
    with ExitStack() as ctx:
        def sb(name, shape, dt=F32):
            return ctx.enter_context(nc.sbuf_tensor(name, shape, dt))

        sems = {}

        def sem(name):
            if name not in sems:
                sems[name] = ctx.enter_context(nc.semaphore(name))
            return sems[name]

        psA = ctx.enter_context(nc.psum_tensor("psA", [P, BANKS, 512], F32))
        psD = ctx.enter_context(nc.psum_tensor("psD", [P, BANKS, 512], F32))

        MAP = 4096 + 2048 + 2048 + 2048 + 2048 + 4096 + 32768
        sb("map", [P, MAP])
        map_at = nc.sbuf_base - 4 * MAP

        def at_place(name, at, n, dt=F32):
            return nc.alloc_sbuf_tensor_at(name, [P, n], dt, offset=map_at + 4 * at)
        RAW, HI, LO, X_AT, M_AT, H_AT, ARENA = 0, 4096, 6144, 8192, 10240, 12288, 16384
        raw = at_place("raw", RAW, SLOTS * 1024)
        w_hi = at_place("w_hi", HI, SLOTS * HALF, F32R)
        w_lo = at_place("w_lo", LO, SLOTS * HALF, F32R)
        xT = at_place("xT", X_AT, KC * T)[:, :].rearrange("p (k t) -> p k t", t=T)
        mT = at_place("mT", M_AT, KC * T)[:, :].rearrange("p (k t) -> p k t", t=T)
        spare = at_place("spare", M_AT, 2048)
        h_hi = at_place("h_hi", H_AT, KC * T, F32R)[:, :].rearrange("p (k t) -> p k t", t=T)
        h_lo = at_place("h_lo", H_AT + KC * T, KC * T, F32R)[:, :].rearrange("p (k t) -> p k t", t=T)
        arena = at_place("arena", ARENA, 32768)
        ident = sb("ident", [P, P])
        ones = sb("ones", [P, P])
        mask_ts = sb("mask_ts", [P, T])
        mask_st = sb("mask_st", [P, T])
        cols = sb("cols", [P, NCOLS])
        mods = sb("mods", [P, 2, 48])
        scale_cols = sb("scale_cols", [P, 2, KC])
        eps = sb("eps", [P, 1])
        late = sb("late", [P, 2304])

        taken = [0]

        def part(tensor, at, *shape):
            n = 1
            for s in shape:
                n *= s
            v = tensor[:, at:at + n]
            names = "abcd"[:len(shape)]
            if len(shape) > 1:
                v = v.rearrange(f"p ({' '.join(names)}) -> p {' '.join(names)}",
                                **{k: s for k, s in zip(names[1:], shape[1:])})
            return v

        def temp(*shape):
            at = taken[0]
            n = 1
            for s in shape:
                n *= s
            taken[0] += n
            assert taken[0] <= 32768, taken[0]
            return part(arena, at, *shape)

        ADA_SLOTS = 4
        ada_ring = temp(ADA_SLOTS, D)
        c_row = temp(2, D)
        b_tok = temp(TOK_BLOCKS, 512)
        zT = temp(Z_N, T)
        toks = temp(NT, 2 * 512)
        v_tok = temp(NT, 512)
        v_ext = temp(NT, MH, MD + 1)
        xn = temp(KC, T)
        qkT = temp(2, 4, T)
        convT = temp(2 * MH, T)
        probs = temp(AH, 3 * P)
        probsT = temp(AH, 3 * P)
        trig = temp(4, NT, 32)
        assert taken[0] <= 32768
        nd = part(arena, ADA_SLOTS * D + 2 * D, NT * MH, MD + 1)
        TOKS_AT = ADA_SLOTS * D + 2 * D + 2048 + Z_N * T

        def split_in(name, at, n):
            return [at_place(name + k, ARENA + at + i * n * T, n * T, F32R)[:, :].rearrange("p (k t) -> p k t", t=T)
                    for i, k in enumerate(("_hi", "_lo"))]
        yaT = part(arena, TOKS_AT, 4, T)
        ymT = part(arena, TOKS_AT + 1024, MH, T)
        PROBS_AT = TOKS_AT + 2048 + 1024 + NT * MH * (MD + 1) + 2048 + 2048 + 2048
        y_hi, y_lo = split_in("y", PROBS_AT - 2048, 8)
        turn = part(xn.rearrange("p a b -> p (a b)"), 0, 2, 2, 16, 32)
        mw = part(xn.rearrange("p a b -> p (a b)"), 0, MH, 3 * P)
        F_AT = ADA_SLOTS * D + 2 * D + 2048
        fT = part(arena, F_AT, FC, T)
        f_hi, f_lo = [at_place(n, ARENA + at, FC * T, F32R)[:, :].rearrange("p (k t) -> p k t", t=T)
                      for n, at in (("f_hi", F_AT + FC * T), ("f_lo", TOKS_AT + 2048 + 1024 + 1032 + 2048))]
        assert F_AT + 2 * FC * T <= TOKS_AT + 2048 + 1024 + 1032

        after = ADA_SLOTS * D + 2 * D
        keysT = part(arena, after, 16, NK)
        z2T = part(arena, after + 2048, 24, T)
        at = after + 2048 + 24 * T
        xbcT = part(arena, at, XBC, T)
        at += XBC * T
        mixT = part(arena, at, MIXC, T)
        at += MIXC * T
        xs_tok = part(arena, at, NT, D)
        at += NT * D
        cbT = part(arena, at, SG, 3 * P)
        at += SG * 3 * P
        ssd_w = part(arena, at, 4, 3 * P)
        at += 4 * 3 * P
        xn2 = part(arena, at, KC, T)
        at += KC * T
        pool_wt = part(arena, at, NPOOL, P)
        at += NPOOL * P
        assert at <= 28672
        PADDED = T + 16
        pool_a = part(arena, at, NPOOL, PADDED)
        at += NPOOL * PADDED
        pool_b = part(arena, at, NPOOL, PADDED)
        at += NPOOL * PADDED
        inv_t = part(arena, at, 2, T)
        at += 2 * T
        assert at <= 32768, at
        mix_hi, mix_lo = split_in("mix", ADA_SLOTS * D + 4096, MIXC)
        u_hi, u_lo = [at_place(n, H_AT + k * 1024, 1024, F32R)[:, :].rearrange("p (k t) -> p k t", t=T)
                      for k, n in enumerate(("u_hi", "u_lo"))]

        U = arena[:, :].rearrange("p (e t) -> p e t", t=T)

        def row(i):
            return late[:, i * T:(i + 1) * T]
        r_i, r_f, r_abs, r_e, r_u, r_t, r_l, r_s = [row(i) for i in range(8)]
        small = part(late, 2048, 256)
        m_cols = part(small, 0, 2, MH, NT)
        mx = part(small, 16, 16)
        nmx = part(small, 32, 16)
        sums = part(small, 48, 16)
        rsums = part(small, 64, 16)
        m_stat = part(small, 80, 5, NT * MH)
        s_cols = part(small, 128, 2, NT, SH)
        a_col = part(small, 192, 2)
        posf = part(small, 200, 2)
        rinv = sb("rinv", [P, T])
        rms = sb("rms", [P, T])
        pos_i = sb("pos_i", [P, NT], I32)

        scores = part(arena, 28672, NT, 2 * QH, NK)
        eq = part(arena, 28672, TOPK, NT * QH, TOPK)
        iota_k = rms[:, P:2 * P]
        top_v = part(late, 0, NT * QH, TOPK)
        pick_a = part(late, 256, NT * QH, TOPK)
        pick_b = part(late, 512, NT * QH, TOPK)
        idx = part(late, 768, NT * QH, 2, TOPK)
        picked = part(late, 1280, 3, NT * QH * TOPK)
        picksT = part(late, 0, 3, T)
        late_act = part(late, 768, 4, T)
        work = part(spare, 0, NT, 2, NK)
        work2 = part(spare, 512, NT, NK)
        i16 = part(spare, 768, NT, 3, TOPK).bitcast(U32)
        v16 = part(spare, 864, NT, 2, TOPK)
        cand = part(spare, 1024, NT, TOPK, TOPK)
        cand2 = part(spare, 1536, NT, TOPK * TOPK)
        pick_ab = part(rinv, 0, NT * QH, TOPK).bitcast(U32)
        pick_u = part(mask_st, 0, NT * QH, TOPK).bitcast(U32)
        ONEHOTS = 4
        hot = part(spare, 0, ONEHOTS, 2, NK)

        def col(name, j=0, n=1, parts=P):
            a, w = COLS[name]
            assert j + n <= w
            return cols[0:parts, a + j:a + j + n]

        def sel(h, heads):
            return ident[0:heads, h:h + 1].broadcast_to([heads, P])

        raw_full = [sem(f"raw_full{s}") for s in range(SLOTS)]
        ada_full = [sem(f"ada_full{s}") for s in range(ADA_SLOTS)]
        hi_ready, lo_ready, half_used, ada_used = sem("hi_ready"), sem("lo_ready"), sem("half_used"), sem("ada_used")
        a_ready, a_drained = sem("a_ready"), sem("a_drained")
        d_ready, d_drained = sem("d_ready"), sem("d_drained")

        block = ctx.enter_context(nc.Block())

        @block.sync
        def _(sp):
            sp.dma_start(cols[:, :], cols_in[:, :]).then_inc(sem("cols_in"), 16)
            sp.dma_start(c_row[:, 0, :], c.broadcast_to([P, D])).then_inc(sem("c_in"), 16)
            units, adas = Count(), Count()

            def load(src):
                n = units.n
                units.n += 1
                if n >= SLOTS:
                    v = 2 * (n - SLOTS) + 2
                    sp.wait_ge(lo_ready, v if units.loop is None else units.loop * 2 + v)
                sp.dma_start(raw[:, n % SLOTS * 1024:(n % SLOTS + 1) * 1024], src).then_inc(raw_full[n % SLOTS], 16)

            def load_ada(src):
                n = adas.n
                adas.n += 1
                if n >= ADA_SLOTS:
                    sp.wait_ge(ada_used, adas.value(ADA_SLOTS))
                sp.dma_start(ada_ring[:, n % ADA_SLOTS, :], src).then_inc(ada_full[n % ADA_SLOTS], 16)

            def stream(src, n, beside=None):
                turns, rest = divmod(n, 4)
                with repeat(sp, turns, {units: 4, adas: 4} if beside else {units: 4}) as i:
                    for j in range(4):
                        load(src(i * 4 + j))
                        if beside:
                            load_ada(beside(i * 4 + j))
                for j in range(turns * 4, n):
                    load(src(j))

            for j in range(ADA_SLOTS):
                load_ada(ada[j])
            sp.dma_start(xT[:, :, :], x[:, :, :]).then_inc(sem("x_in"), 16)
            load(gates[0])
            with repeat(sp, 3, {adas: 4}) as i:
                for j in range(4):
                    load_ada(ada[i * 4 + (j + 4)])
            for j in range(3):
                load(tok[j])
            sp.dma_start(pos_i[:, :], pos[:, :]).then_inc(sem("pos_in"), 16)
            sp.dma_start(b_tok, bias_tok.rearrange("a b -> () (a b)").broadcast_to([P, 2048]).rearrange(
                "p (a b) -> p a b", a=TOK_BLOCKS)).then_inc(sem("b_tok_in"), 16)
            sp.dma_start(c_row[:, 1, :], c_2.broadcast_to([P, D])).then_inc(sem("c_in"), 16)
            load(tok[3])
            stream(lambda u: tok[u + 4], 12, lambda u: ada[u + 16])
            stream(lambda u: feat[u], 8, lambda u: ada[u + 28])
            stream(lambda u: feat[u + 8], 4)
            stream(lambda u: feat[u + 12], 16, lambda u: ada2[u])
            stream(lambda u: proj[u], 8, lambda u: ada[u + 36])
            stream(lambda u: wout[u], 4, lambda u: ada[u + 44])
            stream(lambda u: wout[u + 4], 4)
            stream(lambda u: gateup[u], 4)
            with repeat(sp, 5, {units: 8, adas: 4}) as i:
                for j in range(8):
                    load(gateup[i * 8 + (j + 4)])
                    if j % 2 == 1:
                        load_ada(ada2[i * 4 + (j // 2 + 16)])
            stream(lambda u: down[u], 12, lambda u: ada2[u + 36])
            stream(lambda u: down[u + 12], 10)
            load(dt[0])
            stream(lambda u: win2[u], 24)
            sp.wait_ge(d_drained, D_AT["down"] + 4)
            sp.dma_start(pool_wt, pool_w[:, :, :]).then_inc(sem("pool_w_in"), 16)
            sp.dma_start(keysT, keys[:, :, :]).then_inc(sem("keys_in"), 16)
            stream(lambda u: wout2[u], 12)
            stream(lambda u: query[u], 16)
            stream(lambda u: expert_down[u], 128)
            stream(lambda u: expert_up[:, u, :], 128)
            sp.wait_ge(sem("y_ready"), KC)
            sp.dma_start(out[:, :, :], mT[:, :, :]).then_inc(sem("out_stored"), 16)
            sp.wait_ge(sem("out_stored"), 16)

        @block.gpsimd
        def _(pool):
            own = Own(pool, sem("pool_own"))
            own(nc.gpsimd.memset(ident[:, :], 0.0))
            own(nc.gpsimd.affine_select(out=ident[:, :], in_=ident[:, :], compare_op=ALU.not_equal, fill=1.0,
                                        base=0, pattern=[[-1, P]], channel_multiplier=1))
            own(nc.gpsimd.memset(mask_ts[:, :], 0.0))
            own(nc.gpsimd.memset(mask_st[:, :], 0.0))
            own(nc.gpsimd.affine_select(out=mask_ts[:, P:T], in_=mask_ts[:, P:T], compare_op=ALU.is_ge, fill=FAR,
                                        base=0, pattern=[[-1, P]], channel_multiplier=1))
            own(nc.gpsimd.affine_select(out=mask_st[:, 0:P], in_=mask_st[:, 0:P], compare_op=ALU.is_ge, fill=FAR,
                                        base=0, pattern=[[1, P]], channel_multiplier=-1))
            nc.gpsimd.memset(ones[:, :], 1.0).then_inc(sem("consts"), 1)

            halves = Count()
            with repeat(pool, UNITS // 4, {halves: 8}):
                for _ in range(8):
                    n = halves.n
                    halves.n += 1
                    pool.wait_ge(hi_ready, halves.value())
                    s = n % SLOTS
                    nc.gpsimd.tensor_tensor(w_lo[:, s * HALF:(s + 1) * HALF], raw[:, n % 8 * HALF:(n % 8 + 1) * HALF],
                                            w_hi[:, s * HALF:(s + 1) * HALF].bitcast(F32),
                                            ALU.subtract).then_inc(lo_ready, 1)

        @block.scalar
        def _(act):
            A = Empty(act, psA, a_ready, a_drained)
            own = Own(act, sem("act_own"))

            def silu_c(k):
                act.wait_ge(sem("c_in"), 16 * (k + 1))
                nc.scalar.activation(c_row[:, k, :], c_row[:, k, :], ACT.Silu).then_inc(sem("c_act"), 1)
            silu_c(0)

            halves = Count()

            def next_stage():
                next_stage.n += 1
            next_stage.n = 0

            def split_half():
                n = halves.n
                halves.n += 1
                if n >= SLOTS:
                    act.wait_ge(half_used, halves.value(SLOTS) + next_stage.n)
                if n % 2 == 0:
                    at = 16 * (n // 8 + 1)
                    act.wait_ge(raw_full[n // 2 % SLOTS], at if halves.loop is None else halves.loop * 2 + at)
                nc.scalar.copy(w_hi[:, n % SLOTS * HALF:(n % SLOTS + 1) * HALF],
                               raw[:, n % 8 * HALF:(n % 8 + 1) * HALF]).then_inc(hi_ready, 1)

            def split(n_units=1):
                for _ in range(2 * n_units):
                    split_half()

            def root(src, sq, width, ready):
                for k in range(KC // 2):
                    act.wait_ge(*ready(k))
                    nc.scalar.activation(sq[:, 2 * k:2 * k + 2, :], src[:, 2 * k:2 * k + 2, :],
                                         ACT.Square).then_inc(sem("sq_ready"), 1)
                b = A.bank()
                A.free(nc.scalar.activation(rms[:, :], b[:, 0:T], ACT.Sqrt, bias=eps[:, 0:1], scale=1.0 / width))

            def norm_modulated(sq, shifts, ready):
                root(xT[:, :, :], sq, D, ready)
                for j in range(KC):
                    norm_modulated.n += 1
                    act.wait_ge(sem("xn_ready"), norm_modulated.n)
                    nc.scalar.activation(h_hi[:, j, :], sq[:, j, :], ACT.Identity, bias=shifts[:, j:j + 1],
                                         scale=1.0).then_inc(sem("h_hi"), 1)
            norm_modulated.n = 0

            split(1)
            act.wait_ge(sem("eps_set"), 1)
            norm_modulated(xn, mods[:, 0, 0:KC], lambda k: (sem("x_in"), 16))

            def log1p_exp(k):
                n = MH if k == 0 else SH
                act.wait_ge(sem("row_abs"), k + 1)
                nc.scalar.activation(r_e[0:n, :], r_abs[0:n, :], ACT.Exp, scale=-1.0).then_inc(sem("row_exp"), 1)
                if k == 0:
                    split(1)
                act.wait_ge(sem("row_u"), k + 1)
                nc.scalar.activation(r_l[0:n, :], r_u[0:n, :], ACT.Ln).then_inc(sem("row_ln"), 1)

            split(2)
            next_stage()
            log1p_exp(0)
            split(2)
            act.wait_ge(sem("m_rows"), 1)
            nc.scalar.activation(r_e[0:MH, :], r_t[0:MH, :], ACT.Exp, scale=-1.0).then_inc(sem("exp_m"), 1)
            split(1)
            act.wait_ge(sem("angles"), 1)
            nc.scalar.activation(trig[:, 0:2, :, :], trig[:, 0:2, :, :], ACT.Sin).then_inc(sem("trig"), 1)

            silu_c(1)
            with repeat(act, 3, {halves: 8}):
                split(4)
            next_stage()
            with repeat(act, 2, {A.count: 4, halves: 8}) as i:
                for j in range(4):
                    split(1)
                    A.free(nc.scalar.activation(zT[:, i * 4 + j, :], A.bank()[:, 0:T], ACT.Identity,
                                                bias=cols[:, bass.ds(i * 4 + (j + COLS["b_feat"][0]), 1)]))

            def m_silu(first):
                for j in range(first, first + 4):
                    act.wait_ge(sem("conv_ready"), j + 1)
                    nc.scalar.activation(convT[:, j, :], convT[:, j, :], ACT.Silu,
                                         bias=col("conv_b", j)).then_inc(sem("m_qk"), 1)

            def softmax_exp(first):
                act.wait_ge(sem("nmx"), first // 4 + 1)
                for h in range(first, first + 2):
                    for t in range(NT):
                        p = probs[:, h, 0:P] if t == 0 else probs[:, h, P:3 * P]
                        k = h * NT + t
                        nc.scalar.activation(p, p, ACT.Exp, bias=nmx[:, k:k + 1], scale=AD ** -0.5,
                                             accum_out=sums[:, k:k + 1]).then_inc(sem("exps"), 1)

            def m_decay_exp(first):
                for h in range(first, first + 2):
                    act.wait_ge(sem("m_args"), h + 1)
                    for t in range(NT):
                        a = mw[:, h, 0:T] if t == 0 else mw[:, h, T:3 * P]
                        nc.scalar.activation(a, a, ACT.Exp, bias=m_cols[:, 0, h, t:t + 1]).then_inc(sem("m_w"), 1)

            def z_sigmoid(a, b):
                act.wait_ge(a_drained, MIXER_BANKS["z", b - 1] + 1)
                nc.scalar.activation(zT[:, a:b, :], zT[:, a:b, :], ACT.Sigmoid).then_inc(sem("sig_ready"), 1)

            def m_root():
                act.wait_ge(sem("m_ms"), 1)
                nc.scalar.activation(m_stat[:, 3, :], m_stat[:, 2, :], ACT.Sqrt, bias=eps[:, 0:1],
                                     scale=1.0 / MD).then_inc(sem("m_rms"), 1)

            def upper_y(j):
                nc.scalar.copy(y_hi[:, j, :], ymT[:, j, :] if j < MH else yaT[:, j - MH, :]).then_inc(sem("y_hi"), 1)

            beside = {10: lambda: m_silu(0), 11: lambda: m_silu(4), 12: lambda: softmax_exp(0),
                      13: lambda: softmax_exp(2), 14: lambda: softmax_exp(4), 15: lambda: softmax_exp(6),
                      16: lambda: m_decay_exp(0), 17: lambda: m_decay_exp(2), 19: lambda: z_sigmoid(Z_MO, 14),
                      20: lambda: z_sigmoid(14, 20), 23: m_root, 25: lambda: z_sigmoid(20, 25)}
            for u in range(8, Z_N):
                split_half()
                A.free(nc.scalar.activation(zT[:, u, :], A.bank()[:, 0:T], ACT.Identity,
                                            bias=col("b_feat", u)))
                if u in BESIDE_Z:
                    step, first = BESIDE_Z[u]
                    for j in range(first, first + 2):
                        b = A.bank()
                        if step == "qkT":
                            A.free(nc.scalar.copy(qkT[:, j % 2, j // 2, :], b[:, 0:T]))
                        elif step == "probsT":
                            A.free(nc.scalar.copy(probsT[:, j, :], b[:, 0:3 * P]))
                        else:
                            A.free(nc.scalar.copy(yaT[:, j, :], b[:, 0:T]))
                if u in beside:
                    beside[u]()
                if u == 24:
                    act.wait_ge(a_drained, MIXER_BANKS["attn", 3] + 1)
                    for j in range(4):
                        upper_y(MH + j)
                split_half()
            for j in range(MH):
                act.wait_ge(d_drained, D_AT["ymT"] + j + 1)
                upper_y(j)
            z_sigmoid(25, Z_N)
            next_stage()

            def upper_m(j):
                act.wait_ge(sem("merged"), j + 1)
                nc.scalar.copy(h_hi[:, j, :], mT[:, j, :]).then_inc(sem("m_hi"), 1)
            for j in range(KC):
                split(1)
                if j >= 1:
                    upper_m(j - 1)
            upper_m(KC - 1)
            next_stage()
            split(8)
            norm_modulated(xn, mods[:, 0, 3 * KC:4 * KC], lambda k: (d_drained, D_AT["wout"] + 2 * k + 2))

            def f_upper(j):
                act.wait_ge(d_drained, j + (D_AT["up"] + 1))
                nc.scalar.copy(f_hi[:, j, :], fT[:, j, :]).then_inc(sem("f_hi"), 1)

            def gate(j):
                split(2)
                A.free(nc.scalar.activation(fT[:, j, :], A.bank()[:, 0:T], ACT.Silu))
            next_stage()
            for j in range(2):
                gate(j)
            f_upper(0)
            with repeat(act, 5, {A.count: 4, halves: 16}) as i:
                for j in range(4):
                    gate(i * 4 + (j + 2))
                    f_upper(i * 4 + (j + 1))
            f_upper(FC - 1)
            next_stage()
            with repeat(act, 5, {halves: 8}):
                split(4)
            split(2)
            root(xT[:, :, :], xn2, D, lambda k: (d_drained, D_AT["down"] + k + 1))
            norm_modulated(xn2, mods[:, 1, 0:KC], lambda k: (sem("x_normed"), 2 * k + 2))
            next_stage()
            split(1)
            next_stage()
            nc.scalar.activation(a_col[0:SH, 0:1], col("a_log", parts=SH), ACT.Exp).then_inc(sem("a_exp"), 1)
            log1p_exp(1)
            with repeat(act, XBC // 4, {A.count: 4, halves: 8}) as i:
                for j in range(4):
                    split(1)
                    A.free(nc.scalar.copy(z2T[:, i * 4 + j, :], A.bank()[:, 0:T]))

            def xbc_silu(j):
                act.wait_ge(sem("conv2_ready"), j + 1)
                nc.scalar.activation(xbcT[:, j, :], xbcT[:, j, :], ACT.Silu,
                                     bias=col("conv_b2", j)).then_inc(sem("xbc"), 1)
            for j in range(KC):
                if j < KC - 1:
                    split(1)
                A.free(nc.scalar.activation(z2T[:, Z2_Z + j, :], A.bank()[:, 0:T], ACT.Silu))
                if j >= 1:
                    xbc_silu(j - 1)
            for j in range(KC - 1, XBC):
                xbc_silu(j)
            split(1)
            act.wait_ge(d_drained, D_AT["dt_cols"] + 1)
            for h in range(SH):
                if h % 2 == 0 and h // 2 < NPOOL:
                    A.free(nc.scalar.copy(z2T[:, Z2_POOL + h // 2, :], A.bank()[:, 0:T]))
                if h >= 4:
                    act.wait_ge(d_ready, D_AT["ssd"] + (h - 4) // 2 + 1)
                b = A.bank()
                nc.scalar.activation(ssd_w[:, h % 4, 0:T], b[:, 0:T], ACT.Exp, bias=s_cols[:, 0, 0, h:h + 1])
                A.free(nc.scalar.activation(ssd_w[:, h % 4, T:3 * P], b[:, T:3 * P], ACT.Exp,
                                            bias=s_cols[:, 0, 1, h:h + 1]))
                if h % 2 == 1 and h // 2 < NPOOL:
                    split(1)
            root(mixT[:, NPOOL:MIXC, :], xn2, D, lambda k: (sem("ssd_y"), 2 * k + 2))
            for j in range(MIXC):
                if j < NPOOL:
                    act.wait_ge(d_drained, D_AT["pool"] + j + 1)
                else:
                    act.wait_ge(sem("ssd_normed"), j - NPOOL + 1)
                nc.scalar.copy(mix_hi[:, j, :], mixT[:, j, :]).then_inc(sem("mix_hi"), 1)
            next_stage()
            split(12)
            norm_modulated(xn2, mods[:, 1, 3 * KC:4 * KC], lambda k: (d_drained, D_AT["wout2"] + k + 1))
            next_stage()
            for j in range(2 * QH):
                split(1)
                b = A.bank()
                if j >= 4:
                    act.wait_ge(d_ready, D_AT["scores"] + j - 4 + 1)
                A.free(nc.scalar.copy(xn2[:, j % 4, :], b[:, 0:T]))
            act.wait_ge(d_drained, D_AT["scores"] + 2 * QH)

            next_stage()

            def activate(dst):
                split(1)
                A.free(nc.scalar.activation(dst, A.bank()[:, 0:T], ACT.Gelu))
            with repeat(act, EARLY // 4, {A.count: 4, halves: 8}) as i:
                for j in range(4):
                    activate(U[:, i * 4 + j, :])
                    nc.scalar.copy(U[:, i * 4 + (j + P - LATE), :], ones[:, :].unsqueeze(1).broadcast_to([P, 2, P]))
            with repeat(act, 2, {A.count: 4, halves: 8}) as i:
                for j in range(4):
                    activate(U[:, i * 4 + (j + EARLY), :])
            act.wait_ge(sem("gate_args"), 1)
            nc.scalar.activation(picked[:, 2, :], picked[:, 2, :], ACT.Exp).then_inc(sem("gate_exp"), 1)
            with repeat(act, (P - LATE - EARLY) // 4 - 2, {A.count: 4, halves: 8}) as i:
                for j in range(4):
                    activate(U[:, i * 4 + (j + EARLY + 8), :])
            late_n = Count()
            act.wait_ge(d_drained, D_AT["picksT"] + 3)

            def activate_late():
                split(1)
                n = late_n.n
                late_n.n += 1
                if n >= 4:
                    act.wait_ge(sem("late_used"), late_n.value(4))
                A.free(nc.scalar.activation(late_act[:, n % 4, :], A.bank()[:, 0:T], ACT.Gelu))
            for j in range(4):
                activate_late()
            with repeat(act, LATE // 4 - 1, {A.count: 4, halves: 8, late_n: 4}):
                for j in range(4):
                    activate_late()

            def u_upper(j, slot):
                nc.scalar.copy(u_hi[:, slot, :], U[:, j, :]).then_inc(sem("u_hi"), 1)

            def next_expert(j, slot):
                split(1)
                u_upper(j, slot)
            next_stage()
            act.wait_ge(d_drained, D_AT["spread"] + T)
            act.wait_ge(sem("late_used"), LATE)
            u_upper(0, 0)
            u_upper(1, 1)
            with repeat(act, (P - 4) // 4, {halves: 8}) as i:
                for j in range(4):
                    next_expert(i * 4 + (2 + j), (2 + j) % 4)
            for j in range(P - 2, P):
                next_expert(j, j % 4)
            A.count.n += BANKS
            root(xT[:, :, :], U[:, 0:KC, :], D, lambda k: (a_drained, A_AT["expert_up"] + k + 1))

        @block.vector
        def _(dve):
            Dr = Empty(dve, psD, d_ready, d_drained)
            own = Own(dve, sem("dve_own"))
            V = nc.vector
            V.memset(eps[:, :], EPS).then_inc(sem("eps_set"), 1)
            own(V.memset(v_ext[:, :, :, MD:MD + 1], 1.0))
            dve.wait_ge(sem("consts"), 1)
            dve.wait_ge(sem("cols_in"), 16)

            ada_n = Count()

            def ada_block(which, j):
                n = ada_n.n
                ada_n.n += 1
                s = n % ADA_SLOTS
                at = 16 * (n // ADA_SLOTS + 1)
                dve.wait_ge(ada_full[s], at if ada_n.loop is None else ada_n.loop * 4 + at)
                V.scalar_tensor_tensor(out=ada_ring[:, s, :], in0=ada_ring[:, s, :], scalar=1.0,
                                       in1=c_row[:, which, :], op0=ALU.mult, op1=ALU.mult,
                                       accum_out=mods[:, which, bass.ds(j, 1)]).then_inc(ada_used, 1)

            def ada_bias(which, lo, hi, bias, blocks):
                dve.wait_ge(ada_used, blocks)
                own(V.tensor_tensor(mods[:, which, lo * KC:hi * KC], mods[:, which, lo * KC:hi * KC],
                                    col(bias, lo * KC, (hi - lo) * KC), ALU.add))

            def gains(which, k, vec, name):
                own(V.scalar_tensor_tensor(out=scale_cols[:, k, :], in0=mods[:, which, vec * KC:(vec + 1) * KC],
                                           scalar=1.0, in1=col(name, 0, KC), op0=ALU.add, op1=ALU.mult))

            def inverse_root(name):
                dve.wait_ge(a_drained, A_AT[name] + 1)
                own(V.reciprocal(rinv[:, :], rms[:, :]))

            def scaled(dst, src, gain, signal):
                for j in range(KC):
                    V.scalar_tensor_tensor(out=dst[:, j, :], in0=src[:, j, :], scalar=gain[:, j:j + 1],
                                           in1=rinv[:, :], op0=ALU.mult, op1=ALU.mult).then_inc(sem(signal), 1)

            def norm_modulated(name, xn_, gain, shift):
                if name != "ssq1":
                    inverse_root(name)
                for j in range(KC + 1):
                    if j < KC:
                        V.scalar_tensor_tensor(out=xn_[:, j, :], in0=xT[:, j, :], scalar=gain[:, j:j + 1],
                                               in1=rinv[:, :], op0=ALU.mult,
                                               op1=ALU.mult).then_inc(sem("xn_ready"), 1)
                    if j >= 1:
                        norm_modulated.n += 1
                        dve.wait_ge(sem("h_hi"), norm_modulated.n)
                        V.scalar_tensor_tensor(out=h_lo[:, j - 1, :], in0=xn_[:, j - 1, :],
                                               scalar=shift[:, j - 1:j], in1=h_hi[:, j - 1, :].bitcast(F32),
                                               op0=ALU.add, op1=ALU.subtract).then_inc(sem("h_lo"), 1)
            norm_modulated.n = 0

            def lower(dst, src, upper, signal):
                V.tensor_tensor(dst, src, upper.bitcast(F32), ALU.subtract).then_inc(sem(signal), 1)

            dve.wait_ge(sem("c_act"), 1)
            with repeat(dve, 3, {ada_n: 4}) as i:
                for j in range(4):
                    ada_block(0, i * 4 + j)
            inverse_root("ssq1")
            for j in range(12, 16):
                ada_block(0, j)
            ada_bias(0, 0, 2, "ada_b", 16)
            gains(0, 0, 1, "norm1")
            norm_modulated("ssq1", xn, scale_cols[:, 0, :], mods[:, 0, 0:KC])

            own(V.memset(r_s[0:SH, :], 0.0))
            b = Dr.bank()
            V.tensor_scalar(r_i[0:MH, :], b[0:MH, 0:T], col("b_i", parts=MH), None, ALU.add)
            Dr.free(V.tensor_scalar(r_f[0:MH, :], b[32:32 + MH, 0:T], col("b_f", parts=MH), None, ALU.add),
                    settle=True)

            def log1p_exp(k, n):
                V.scalar_tensor_tensor(out=r_abs[0:n, :], in0=r_f[0:n, :], scalar=-1.0, in1=r_f[0:n, :],
                                       op0=ALU.mult, op1=ALU.max).then_inc(sem("row_abs"), 1)
                dve.wait_ge(sem("row_exp"), k + 1)
                V.tensor_scalar(r_u[0:n, :], r_e[0:n, :], 1.0, None, ALU.add).then_inc(sem("row_u"), 1)
                dve.wait_ge(sem("row_u"), k + 1)
                own(V.tensor_scalar(r_t[0:n, :], r_u[0:n, :], -1.0, None, ALU.add))
                own(V.tensor_tensor(r_t[0:n, :], r_e[0:n, :], r_t[0:n, :], ALU.subtract))
                own(V.reciprocal(r_abs[0:n, :], r_u[0:n, :]))
                own(V.tensor_tensor(r_t[0:n, :], r_t[0:n, :], r_abs[0:n, :], ALU.mult))
                dve.wait_ge(sem("row_ln"), k + 1)
                own(V.tensor_tensor(r_l[0:n, :], r_l[0:n, :], r_t[0:n, :], ALU.add))

            log1p_exp(0, MH)
            R = slice(0, MH)
            own(V.scalar_tensor_tensor(out=r_f[R, :], in0=r_f[R, :], scalar=0.0, in1=r_l[R, :],
                                       op0=ALU.min, op1=ALU.subtract))
            own(V.tensor_tensor_scan(r_abs[R, :], r_f[R, :], r_s[R, :], 0.0, ALU.add, ALU.add))
            own(V.tensor_tensor(r_i[R, :], r_i[R, :], r_abs[R, :], ALU.subtract))
            own(V.tensor_tensor_scan(r_u[R, :], r_i[R, :], r_i[R, :], 0.0, ALU.max, ALU.max))
            V.tensor_tensor(r_t[R, :], r_abs[R, :], r_u[R, :], ALU.add).then_inc(sem("m_rows"), 1)
            V.tensor_scalar(r_f[R, :], r_u[R, :], -1.0, None, ALU.mult).then_inc(sem("neg_m"), 1)

            dve.wait_ge(sem("pos_in"), 16)
            own(V.tensor_copy(posf, pos_i[:, :]))
            for t in range(NT):
                own(V.tensor_scalar(trig[:, 2, t, :], col("inv_freq", 0, 32), posf[:, t:t + 1], None, ALU.mult))
            ang = trig[:, 2, :, :]
            for k, quarter in ((0, 0.25), (1, 0.0)):
                r = trig[:, k, :, :]
                own(V.tensor_scalar(trig[:, 3, :, :], ang, 1.0 / 6.283185307179586, quarter, ALU.mult, ALU.add))
                own(V.tensor_scalar(trig[:, 3, :, :], trig[:, 3, :, :], MAGIC, -MAGIC, ALU.add, ALU.add))
                for n, piece in enumerate(TWO_PI):
                    own(V.scalar_tensor_tensor(out=r, in0=trig[:, 3, :, :], scalar=-piece, in1=ang if n == 0 else r,
                                               op0=ALU.mult, op1=ALU.add))
                if quarter:
                    own(V.tensor_scalar(r, r, 1.5707963267948966, None, ALU.add))
                last = V.tensor_scalar(r, r, PI_BELOW, -PI_BELOW, ALU.min, ALU.max)
                if k == 0:
                    own(last)
            last.then_inc(sem("angles"), 1)

            dve.wait_ge(sem("b_tok_in"), 16)

            def other_mods(first):
                for j in range(first, first + 4):
                    ada_block(0, j)
            for b in range(2):
                for t in range(NT):
                    Dr.free(V.tensor_tensor(toks[:, t, b * 512:(b + 1) * 512], Dr.bank(), b_tok[:, b, :], ALU.add),
                            settle=True)
                other_mods(16 + 4 * b)
            dve.wait_ge(sem("trig"), 1)
            for t in range(NT):
                halves = toks[:, t, 0:1024].rearrange("p (h z d) -> p z h d", z=2, d=32)
                cos = trig[:, 0, t, :].unsqueeze(1).broadcast_to([P, 16, 32])
                sin = trig[:, 1, t, :].unsqueeze(1).broadcast_to([P, 16, 32])
                for z in range(2):
                    V.tensor_tensor(turn[:, 0, z, :, :], halves[:, z, :, :], cos, ALU.mult)
                    own(V.tensor_tensor(turn[:, 1, z, :, :], halves[:, z, :, :], sin, ALU.mult))
                V.tensor_tensor(halves[:, 0, :, :], turn[:, 0, 0, :, :], turn[:, 1, 1, :, :],
                                ALU.subtract).then_inc(sem("roped"), 1)
                V.tensor_tensor(halves[:, 1, :, :], turn[:, 0, 1, :, :], turn[:, 1, 0, :, :],
                                ALU.add).then_inc(sem("roped"), 1)
                dve.wait_ge(sem("roped"), 2 * t + 2)
            for t in range(NT):
                Dr.free(V.tensor_tensor(v_tok[:, t, :], Dr.bank(), b_tok[:, 2, :], ALU.add))
            other_mods(24)
            for t in range(NT):
                Dr.free(V.tensor_tensor(v_ext[:, t, :, 0:MD], Dr.bank().rearrange("p (h d) -> p h d", h=MH),
                                        b_tok[:, 3, :].rearrange("p (h d) -> p h d", h=MH), ALU.add))

            def convs(j, src, dst, weights, ready, first):
                w = COLS[weights][0]
                for back in range(CONV):
                    for k in range(4):
                        tap = cols[:, bass.ds(j * CONV + (w + k * CONV + CONV - 1 - back), 1)]
                        if back == 0:
                            dve.wait_ge(a_drained, j + (first + k + 1))
                            ins = V.tensor_scalar(dst[:, j + k, :], src[:, j + k, :], tap, None, ALU.mult)
                        else:
                            dve.wait_ge(own.sem, own.count.value(3 if back < CONV - 1 else 3 - k))
                            ins = V.scalar_tensor_tensor(out=dst[:, j + k, back:T], in0=src[:, j + k, 0:T - back],
                                                         scalar=tap, in1=dst[:, j + k, back:T],
                                                         op0=ALU.mult, op1=ALU.add)
                        if back < CONV - 1:
                            ins.then_inc(own.sem, 1)
                            own.count.n += 1
                        else:
                            ins.then_inc(ready, 1)
            with repeat(dve, 2 * MH // 4, {own.count: 4 * (CONV - 1), ada_n: 4}) as i:
                for k in range(4):
                    ada_block(0, i * 4 + (k + 28))
                convs(i * 4, zT, convT, "conv_w", sem("conv_ready"), A_AT["mixers"])

            b = Dr.bank()
            Dr.free(V.tensor_copy(m_cols.rearrange("p k h t -> p k t h"),
                                  b[:, 0:16].rearrange("p (k t h) -> p k t h", k=2, t=NT)), settle=True)
            dve.sem_inc(sem("m_cols"), 1)

            dve.wait_ge(sem("c_act"), 2)
            for h in range(AH):
                b = Dr.bank()
                own(V.tensor_tensor_reduce(probs[:, h, 0:P], b[:, 0:P], mask_ts[:, P:T], 1.0, LOWEST,
                                           ALU.add, ALU.max, mx[:, 2 * h:2 * h + 1]))
                Dr.free(V.tensor_tensor_reduce(probs[:, h, P:3 * P], b[:, P:3 * P], mask_ts[:, :], 1.0, LOWEST,
                                               ALU.add, ALU.max, mx[:, 2 * h + 1:2 * h + 2]), settle=True)
                if h % 2 == 1:
                    ada_block(1, h // 2)
                if h % 4 == 3:
                    V.tensor_scalar(nmx[:, 2 * h - 6:2 * h + 2], mx[:, 2 * h - 6:2 * h + 2], -(AD ** -0.5), None,
                                    ALU.mult).then_inc(sem("nmx"), 1)
            for h in range(MH):
                b = Dr.bank()
                V.tensor_tensor(mw[:, h, T:3 * P], b[:, P:T], mask_st[:, 0:P], ALU.add)
                Dr.free(V.tensor_tensor(mw[:, h, 0:T], b[:, 0:T], mask_st[:, :], ALU.add), settle=True)
                dve.sem_inc(sem("m_args"), 1)
                ada_block(1, h + 4)
            dve.wait_ge(sem("exps"), AH * NT)
            own(V.reciprocal(rsums, sums))
            for h in range(AH):
                for t in range(NT):
                    p = probs[:, h, 0:P] if t == 0 else probs[:, h, P:3 * P]
                    k = h * NT + t
                    V.tensor_scalar(p, p, rsums[:, k:k + 1], None, ALU.mult).then_inc(sem("probs"), 1)
            for h in range(MH):
                dve.wait_ge(sem("m_w"), 2 * h + 2)
                Dr.free(V.scalar_tensor_tensor(out=mw[:, h, :], in0=Dr.bank()[:, 0:3 * P], scalar=MD ** -0.5,
                                               in1=mw[:, h, :], op0=ALU.mult, op1=ALU.mult))
                ada_block(1, h + 8)
            for h in range(MH):
                Dr.free(V.tensor_copy(nd[:, 2 * h:2 * h + 2, :],
                                      Dr.bank()[:, 0:2 * (MD + 1)].rearrange("p (t d) -> p t d", t=NT)), settle=True)
                ada_block(1, h + 12)
            den = nd[:, :, MD:MD + 1].rearrange("p a b -> p (a b)")
            own(V.scalar_tensor_tensor(out=m_stat[:, 0, :], in0=den, scalar=-1.0, in1=den,
                                       op0=ALU.mult, op1=ALU.max))
            own(V.tensor_tensor(m_stat[:, 0, :], m_stat[:, 0, :], m_cols[:, 1, :, :].rearrange("p h t -> p (h t)"),
                                ALU.max))
            own(V.reciprocal(m_stat[:, 1, :], m_stat[:, 0, :]))
            own(V.tensor_tensor(nd[:, :, 0:MD], nd[:, :, 0:MD],
                                m_stat[:, 1, :].unsqueeze(2).broadcast_to([P, NT * MH, MD]), ALU.mult))
            for k in range(NT * MH):
                own(V.tensor_tensor_reduce(xn[:, 0, 0:MD], nd[:, k, 0:MD], nd[:, k, 0:MD], 1.0, 0.0,
                                           ALU.mult, ALU.add, m_stat[:, 2, k:k + 1]))
            dve.sem_inc(sem("m_ms"), 1)
            dve.wait_ge(sem("m_rms"), 1)
            own(V.reciprocal(m_stat[:, 4, :], m_stat[:, 3, :]))
            V.tensor_tensor(nd[:, :, 0:MD], nd[:, :, 0:MD],
                            m_stat[:, 4, :].unsqueeze(2).broadcast_to([P, NT * MH, MD]),
                            ALU.mult).then_inc(sem("m_normed"), 1)
            dve.wait_ge(sem("sig_ready"), 1)
            for h in range(MH):
                Dr.free(V.scalar_tensor_tensor(out=ymT[:, h, :], in0=Dr.bank()[:, 0:T], scalar=col("m_norm", h),
                                               in1=zT[:, Z_MO + h, :], op0=ALU.mult, op1=ALU.mult))
            dve.wait_ge(d_drained, D_AT["ymT"] + MH)
            for n, j in enumerate((4, 5, 6, 7, 0, 1, 2, 3)):
                dve.wait_ge(sem("y_hi"), n + 1)
                lower(y_lo[:, j, :], ymT[:, j, :] if j < MH else yaT[:, j - MH, :], y_hi[:, j, :], "y_lo")

            def lower_m(j):
                dve.wait_ge(sem("m_hi"), j + 1)
                lower(h_lo[:, j, :], mT[:, j, :], h_hi[:, j, :], "m_lo")
            dve.wait_ge(sem("sig_ready"), 4)
            for j in range(KC):
                Dr.free(V.tensor_tensor(mT[:, j, :], Dr.bank()[:, 0:T], zT[:, Z_GA + j, :], ALU.mult))
                Dr.free(V.tensor_tensor(xn[:, j, :], Dr.bank()[:, 0:T], zT[:, Z_GB + j, :], ALU.mult), settle=True)
                V.tensor_tensor(mT[:, j, :], mT[:, j, :], xn[:, j, :], ALU.add).then_inc(sem("merged"), 1)
                ada_block(0, j + 36)
                if j >= 2:
                    lower_m(j - 2)
            lower_m(KC - 2)
            lower_m(KC - 1)
            ada_bias(0, 2, 3, "ada_b", 24)

            def residual(j, bank, gate_col):
                return V.scalar_tensor_tensor(out=xT[:, j, :], in0=bank, scalar=gate_col[:, j:j + 1],
                                              in1=xT[:, j, :], op0=ALU.mult, op1=ALU.add)

            def residual_all(gate_col):
                for k in range(BANKS):
                    b = Dr.bank()
                    residual(2 * k, b[:, 0:T], gate_col)
                    Dr.free(residual(2 * k + 1, b[:, T:2 * T], gate_col), settle=True)

            for j in range(KC):
                if j < 4:
                    ada_block(0, j + 44)
                if j == 4:
                    ada_bias(0, 3, 6, "ada_b", 64)
                    gains(0, 1, 4, "norm2")
                Dr.free(residual(j, Dr.bank()[:, 0:T], mods[:, 0, 2 * KC:3 * KC]), settle=True)
            norm_modulated("ssq2", xn, scale_cols[:, 1, :], mods[:, 0, 3 * KC:4 * KC])

            def f_lower(j):
                dve.wait_ge(sem("f_hi"), j + 1)
                lower(f_lo[:, j, :], fT[:, j, :], f_hi[:, j, :], "f_lo")

            def up_chunk(j, behind=True):
                b = Dr.bank()
                dve.wait_ge(a_drained, j + (A_AT["gate"] + 1))
                Dr.free(V.tensor_tensor(fT[:, j, :], b[:, 0:T], fT[:, j, :], ALU.mult))
                if behind:
                    f_lower(j - 1)
            up_chunk(0, False)
            up_chunk(1)
            with repeat(dve, 5, {Dr.count: 4, ada_n: 4}) as i:
                for j in range(4):
                    ada_block(1, i * 4 + (j + 16))
                    up_chunk(i * 4 + (j + 2))
            f_lower(FC - 1)
            for j in range(36, 48):
                ada_block(1, j)
            ada_bias(1, 0, 6, "ada_b2", 96)
            residual_all(mods[:, 0, 5 * KC:6 * KC])
            inverse_root("ssqf")
            scaled(xT, xT, col("normf", 0, KC), "x_normed")
            dve.wait_ge(sem("x_normed"), KC)
            gains(1, 0, 1, "norm_mix")
            norm_modulated("ssq_mix", xn2, scale_cols[:, 0, :], mods[:, 1, 0:KC])
            gains(1, 1, 4, "norm_ffn")

            S = slice(0, SH)
            own(V.memset(r_s[S, :], 0.0))
            Dr.free(V.tensor_scalar(r_f[S, :], Dr.bank()[S, 0:T], col("dt_bias", parts=SH), None, ALU.add),
                    settle=True)
            log1p_exp(1, SH)
            own(V.scalar_tensor_tensor(out=r_i[S, :], in0=r_f[S, :], scalar=0.0, in1=r_l[S, :],
                                       op0=ALU.max, op1=ALU.add))
            dve.wait_ge(sem("a_exp"), 1)
            own(V.tensor_scalar(r_t[S, :], r_i[S, :], a_col[S, 0:1], -1.0, ALU.mult, ALU.mult))
            V.tensor_tensor_scan(r_u[S, :], r_t[S, :], r_s[S, :], 0.0, ALU.add, ALU.add).then_inc(sem("dt_rows"), 1)

            with repeat(dve, XBC // 4, {own.count: 4 * (CONV - 1)}) as i:
                convs(i * 4, z2T, xbcT, "conv_w2", sem("conv2_ready"), A_AT["win2"])
            own(V.memset(inv_t[:, 0, :], 1.0))
            own(V.tensor_tensor_scan(inv_t[:, 1, :], inv_t[:, 0, :], inv_t[:, 0, :], 0.0, ALU.add, ALU.max))
            own(V.memset(pool_a[:, :, 0:16], 0.0))
            own(V.memset(pool_b[:, :, 0:16], 0.0))
            own(V.reciprocal(inv_t[:, 0, :], inv_t[:, 1, :]))
            b = Dr.bank()
            V.tensor_scalar(s_cols[:, 0, :, :].rearrange("p t h -> p (t h)"), b[:, 0:2 * SH], -1.0, None, ALU.mult)
            Dr.free(V.tensor_copy(s_cols[:, 1, :, :].rearrange("p t h -> p (t h)"), b[:, 2 * SH:4 * SH]), settle=True)
            for j in range(4):
                t, side = divmod(j, 2)
                Dr.free(V.tensor_copy(xs_tok[:, t, side * 512:(side + 1) * 512], Dr.bank()))
            for g in range(SG):
                Dr.free(V.tensor_copy(cbT[:, g, :], Dr.bank()[:, 0:3 * P]), settle=True)

            def ssd_weights(h):
                g = h // (SH // SG)
                dve.wait_ge(a_drained, decay_bank(h) + 1)
                for s, (a, e) in enumerate(((0, T), (T, 3 * P))):
                    w = ssd_w[:, h % 4, a:e]
                    V.scalar_tensor_tensor(out=w, in0=w, scalar=s_cols[:, 1, s, h:h + 1], in1=cbT[:, g, a:e],
                                           op0=ALU.mult, op1=ALU.mult).then_inc(sem("ssd_w"), 1)

            def ssd_out(j):
                Dr.free(V.scalar_tensor_tensor(out=mixT[:, NPOOL + j, :], in0=xbcT[:, j, :], scalar=col("d_skip", j),
                                               in1=Dr.bank()[:, 0:T], op0=ALU.mult, op1=ALU.add), settle=True)
                V.tensor_tensor(mixT[:, NPOOL + j, :], mixT[:, NPOOL + j, :], z2T[:, Z2_Z + j, :],
                                ALU.mult).then_inc(sem("ssd_y"), 1)

            bufs = [pool_a, pool_b]

            def pool_sums(g):
                if g == 0:
                    dve.wait_ge(a_drained, pool_bank(NPOOL - 1) + 1)
                    own(V.tensor_copy(pool_a[:, :, 16:PADDED], z2T[:, Z2_POOL:Z2_POOL + NPOOL, :]))
                w = POOLS[g] // 2
                a, b = bufs[g % 2], bufs[(g + 1) % 2]
                own(V.tensor_tensor(b[:, g:NPOOL, 16:PADDED], a[:, g:NPOOL, 16:PADDED],
                                    a[:, g:NPOOL, 16 - w:PADDED - w], ALU.add))

            def pool_means():
                wins = [bufs[(g + 1) % 2][:, g, 16:PADDED] for g in range(NPOOL)]
                for g, win in enumerate(wins):
                    own(V.scalar_tensor_tensor(out=win, in0=inv_t[:, 0, :], scalar=1.0 / POOLS[g], in1=win,
                                               op0=ALU.max, op1=ALU.mult))
                    V.tensor_tensor(win, win, z2T[:, Z2_POOL + g, :], ALU.subtract).then_inc(sem("pooled"), 1)
            dve.wait_ge(sem("xbc"), XBC)
            for j in range(KC):
                ssd_weights(2 * j)
                ssd_weights(2 * j + 1)
                if j >= 1:
                    ssd_out(j - 1)
                if j >= KC - NPOOL:
                    pool_sums(j - (KC - NPOOL))
            ssd_out(KC - 1)
            pool_means()
            for g in range(NPOOL):
                Dr.free(V.tensor_scalar(mixT[:, g, :], Dr.bank()[:, 0:T], col("pool_b", g), col("pool_scale", g),
                                        ALU.add, ALU.mult))

            def lower_mix(j):
                dve.wait_ge(sem("mix_hi"), j + 1)
                lower(mix_lo[:, j, :], mixT[:, j, :], mix_hi[:, j, :], "mix_lo")
            for j in range(NPOOL):
                lower_mix(j)
            inverse_root("ssq_ssd")
            for j in range(KC + 1):
                if j < KC:
                    y = mixT[:, NPOOL + j, :]
                    V.scalar_tensor_tensor(out=y, in0=y, scalar=col("ssd_norm", j), in1=rinv[:, :], op0=ALU.mult,
                                           op1=ALU.mult).then_inc(sem("ssd_normed"), 1)
                if j >= 1:
                    lower_mix(NPOOL + j - 1)
            residual_all(mods[:, 1, 2 * KC:3 * KC])
            norm_modulated("ssq_ffn", xn2, scale_cols[:, 1, :], mods[:, 1, 3 * KC:4 * KC])

            for j in range(2 * QH):
                Dr.free(V.tensor_copy(scores[:, :, j, :], Dr.bank()[:, 0:NT * NK].rearrange("p (t n) -> p t n", t=NT)),
                        settle=j == 2 * QH - 1)
            own(V.tensor_tensor_scan(iota_k, ones[:, :], mask_ts[:, 0:P], -1.0, ALU.add, ALU.max))

            def step(fn):
                for t in range(NT):
                    dve.wait_ge(own.sem, own.count.value(1))
                    dve.sem_inc(sem("top_steps"), 1)
                    fn(t).then_inc(own.sem, 1)
                    own.count.n += 1

            def top16(vals, ids, src, spare):
                step(lambda t: V.max(vals(t)[:, 0:8], src(t)))
                step(lambda t: V.max_index(ids(t)[:, 0:8], vals(t)[:, 0:8], src(t)))
                step(lambda t: V.match_replace(spare(t), vals(t)[:, 0:8], src(t), LOWEST))
                step(lambda t: V.max(vals(t)[:, 8:16], spare(t)))
                step(lambda t: V.max_index(ids(t)[:, 8:16], vals(t)[:, 8:16], spare(t)))

            flat = scores.rearrange("p t j n -> p (t j) n")
            with repeat(dve, QH, {own.count: NT * 20}) as h:
                step(lambda t: V.tensor_copy(work[:, t, :, :], flat[:, bass.ds(h * 2 + t * 2 * QH, 2), :]))
                for z in range(2):
                    top16(lambda t: v16[:, t, z, :], lambda t: i16[:, t, z, :], lambda t: work[:, t, z, :],
                          lambda t: work2[:, t, :])
                step(lambda t: V.tensor_copy(idx[:, h + t * QH, :, :], i16[:, t, 0:2, :]))
                step(lambda t: V.tensor_tensor(cand[:, t, :, :],
                                               v16[:, t, 0, :].unsqueeze(2).broadcast_to([P, TOPK, TOPK]),
                                               v16[:, t, 1, :].unsqueeze(1).broadcast_to([P, TOPK, TOPK]), ALU.add))
                top16(lambda t: v16[:, t, 0, :], lambda t: i16[:, t, 2, :],
                      lambda t: cand[:, t, :, :].rearrange("p a b -> p (a b)"), lambda t: cand2[:, t, :])
                step(lambda t: V.tensor_copy(top_v[:, h + t * QH, :], v16[:, t, 0, :]))
                step(lambda t: V.tensor_copy(pick_ab[:, h + t * QH, :], i16[:, t, 2, :]))
            dve.wait_ge(own.sem, own.count.value())
            own(V.tensor_scalar(pick_u, pick_ab, 4, None, ALU.logical_shift_right))
            own(V.tensor_copy(pick_a, pick_u))
            own(V.tensor_scalar(pick_u, pick_ab, 15, None, ALU.bitwise_and))
            own(V.tensor_copy(pick_b, pick_u))
            for z, pick in ((0, pick_a), (1, pick_b)):
                for i in range(TOPK):
                    last = V.scalar_tensor_tensor(out=eq[:, i, :, :], in0=pick, scalar=float(i),
                                                  in1=idx[:, :, z, i:i + 1].broadcast_to([P, NT * QH, TOPK]),
                                                  op0=ALU.is_equal, op1=ALU.mult)
                own(last)
                own(V.tensor_reduce(picked[:, z, :], eq.rearrange("p i a k -> p (a k) i"), AX.X, ALU.add))
            gates = picked[:, 2, :].rearrange("p (a k) -> p a k", k=TOPK)
            V.tensor_tensor(gates, top_v, top_v[:, :, 0:1].broadcast_to([P, NT * QH, TOPK]),
                            ALU.subtract).then_inc(sem("gate_args"), 1)
            own(V.memset(U[:, P - LATE + EARLY:P, :], 1.0))
            dve.wait_ge(sem("gate_exp"), 1)
            own(V.tensor_reduce(mx, gates, AX.X, ALU.add))
            own(V.reciprocal(rsums, mx))
            V.tensor_tensor(gates, gates, rsums.unsqueeze(2).broadcast_to([P, NT * QH, TOPK]),
                            ALU.mult).then_inc(sem("picked"), 1)
            for z in range(3):
                Dr.free(V.tensor_copy(picksT[:, z, :], Dr.bank()[:, 0:T]), settle=True)

            hots = Count()

            def one_hots(t):
                n = hots.n
                hots.n += 1
                if n >= ONEHOTS:
                    dve.wait_ge(d_ready, hots.value(ONEHOTS) + D_AT["spread"])
                h = hot[:, n % ONEHOTS, :, :]
                V.tensor_scalar(h[:, 0, :], iota_k, picksT[:, 0, bass.ds(t, 1)], None,
                                ALU.is_equal).then_inc(sem("one_hots"), 1)
                V.tensor_scalar(h[:, 1, :], iota_k, picksT[:, 1, bass.ds(t, 1)], picksT[:, 2, bass.ds(t, 1)],
                                ALU.is_equal, ALU.mult).then_inc(sem("one_hots"), 1)

            def gate_experts(t):
                u = U[:, :, bass.ds(t, 1)].rearrange("p e t -> p (e t)")
                Dr.free(V.tensor_tensor(u, Dr.bank()[:, 0:P], u, ALU.mult))

            late_n = Count()

            def multiply_late(j):
                n = late_n.n
                late_n.n += 1
                dve.wait_ge(a_drained, late_n.value() + (A_AT["experts"] + P - LATE))
                dve.wait_ge(d_drained, Dr.count.value())
                V.tensor_tensor(U[:, j, :], late_act[:, n % 4, :], U[:, j, :], ALU.mult).then_inc(sem("late_used"), 1)
                dve.wait_ge(sem("late_used"), late_n.value())

            for t in range(4):
                one_hots(t)
            dve.wait_ge(a_drained, A_AT["experts"] + P - LATE)

            def four_tokens(t, late):
                for k in range(4):
                    one_hots(t + (k + 4))
                    if k == 3 and late is not None:
                        multiply_late(late)
                    gate_experts(t + k)
            four_tokens(0, None)
            for j in range(1, 4):
                four_tokens(4 * j, P - LATE + j - 1)
            with repeat(dve, LATE // 4 - 2, {hots: 16, Dr.count: 16, late_n: 4}) as i:
                for j in range(4):
                    four_tokens(i * 16 + 4 * (j + 4), i * 4 + (P - LATE + j + 3))
            for j in range(LATE - 4, LATE):
                if j < LATE - 1:
                    four_tokens(4 * j, P - LATE + j - 1)
            for t in range(T - 4, T):
                gate_experts(t)
            for j in range(P - 2, P):
                multiply_late(j)

            def u_lower(j, slot, n):
                dve.wait_ge(sem("u_hi"), n)
                lower(u_lo[:, slot, :], U[:, j, :], u_hi[:, slot, :], "u_lo")
            with repeat(dve, P // 4, {late_n: 0}) as i:
                for j in range(4):
                    u_lower(i * 4 + j, j, i * 4 + (j + 1))
            dve.wait_ge(a_drained, A_AT["expert_up"])
            for k in range(BANKS):
                dve.wait_ge(a_ready, A_AT["expert_up"] + k + 1)
                b = psA[:, (A_AT["expert_up"] + k) % BANKS, :]
                residual(2 * k, b[:, 0:T], mods[:, 1, 5 * KC:6 * KC])
                residual(2 * k + 1, b[:, T:2 * T], mods[:, 1, 5 * KC:6 * KC]).then_inc(a_drained, 1)
            inverse_root("ssq_final")
            scaled(mT, xT, col("norm_final", 0, KC), "y_ready")

        @block.tensor
        def _(pe):
            A = Fill(pe, psA, a_ready, a_drained)
            Dr = Fill(pe, psD, d_ready, d_drained)
            mm = nc.tensor.matmul
            halves = Count()
            norms = Count()

            def half():
                n = halves.n
                halves.n += 1
                pe.wait_ge(lo_ready, halves.value())
                s = slice(n % SLOTS * HALF, (n % SLOTS + 1) * HALF)
                return w_hi[:, s], w_lo[:, s]

            def begun(ins):
                if halves.n > 1:
                    ins.then_inc(half_used, 1)

            def stage_ends():
                pe.drain().then_inc(half_used, 1)

            def product(o, w, m, start, stop, opens=False):
                first = mm(o, w[0], m[0], start=start, stop=False, skip_group_check=True)
                if opens:
                    begun(first)
                mm(o, w[0], m[1], start=False, stop=False, skip_group_check=True)
                return mm(o, w[1], m[0], start=False, stop=stop, skip_group_check=True)

            def ssq(src):
                b = A.bank()
                for j in range(KC):
                    if j % 2 == 0:
                        norms.n += 1
                        pe.wait_ge(sem("sq_ready"), norms.n)
                    last = mm(b[:, 0:T], ones[:, :], src[:, j, :], start=j == 0, stop=j == KC - 1)
                A.full(last)

            def half_blocks(b, w, rhs, first, last, ready=None):
                for k in range(4):
                    if ready is not None:
                        pe.wait_ge(*ready(first + k))
                    done = product(b[:, 0:T], [part_[:, k * P:(k + 1) * P] for part_ in w],
                                   [part_[:, first + k, :] for part_ in rhs],
                                   start=first + k == 0, stop=last and k == 3, opens=k == 0)
                return done

            def unit(R, rhs, ready=None, beside=None):
                b = R.bank()
                for h in range(2):
                    done = half_blocks(b, half(), rhs, 4 * h, h == 1, ready)
                    if h == 1:
                        R.full(done)
                    if beside:
                        beside(h)

            def columns(R, n, rhs, second=None, ends=True, ready=None):
                per = 4 if second is None else 8
                turns, rest = divmod(n, per)

                def body(count, ready=None):
                    for j in range(count):
                        unit(R if second is None or j % 2 == 0 else second, rhs, ready if j == 0 else None)
                if R.count.n < BANKS or ready:
                    turns -= 1
                    body(per, ready)
                counts = {halves: 2 * per, R.count: 4}
                if second is not None:
                    counts[second.count] = 4
                if turns:
                    with repeat(pe, turns, counts):
                        body(per)
                body(rest)
                if ends:
                    stage_ends()

            def row_unit(banks, rhs, first, last, R):
                for h in range(2):
                    w = half()
                    for k in range(4):
                        n = 4 * h + k
                        done = product(banks[n // 2][:, (n % 2) * T:(n % 2 + 1) * T],
                                       [part_[:, k * P:(k + 1) * P] for part_ in w], rhs,
                                       start=first and n % 2 == 0, stop=last, opens=k == 0)
                        if last and n % 2 == 1:
                            R.full(done)

            def row_blocks(n, rhs, ready):
                banks = [Dr.bank() for _ in range(BANKS)]

                def one(k, first=False, last=False):
                    pe.wait_ge(*ready(k))
                    row_unit(banks, [part_[:, k, :] for part_ in rhs], first, last, Dr)
                one(0, first=True)
                turns, rest = divmod(n - 2, 4)
                with repeat(pe, turns, {halves: 8}) as i:
                    for j in range(4):
                        one(i * 4 + (j + 1))
                for j in range(rest):
                    one(turns * 4 + 1 + j)
                one(n - 1, last=True)
                stage_ends()

            pe.wait_ge(sem("consts"), 1)
            ssq(xn)
            h_parts = (h_hi, h_lo)
            unit(Dr, h_parts, lambda k: (sem("h_lo"), k + 1))
            stage_ends()
            for _ in range(TOK_BLOCKS):
                bs = [Dr.bank() for _ in range(NT)]
                for kc in range(KC):
                    w = half()
                    for t in range(NT):
                        last = product(bs[t], [part_[:, kc, t * P:(t + 1) * P] for part_ in h_parts], w,
                                       start=kc == 0, stop=kc == KC - 1, opens=t == 0)
                        if kc == KC - 1:
                            Dr.full(last)
            stage_ends()
            columns(A, 8, h_parts, ends=False)

            def gate_cols():
                pe.wait_ge(sem("exp_m"), 1)
                b = Dr.bank()
                for k, src in ((0, r_i), (1, r_e)):
                    for t in range(NT):
                        at = (k * NT + t) * MH
                        last = nc.tensor.transpose(b[:, at:at + MH], src[0:MH, t * P:(t + 1) * P],
                                                   ident[0:MH, 0:MH])
                Dr.full(last)

            def turn_qk(j):
                pe.wait_ge(sem("roped"), 2 * NT)
                b = A.bank()
                z, pr = j % 2, j // 2
                for t in range(NT):
                    last = nc.tensor.transpose(b[:, t * P:(t + 1) * P],
                                               toks[:, t, z * 512 + pr * P:z * 512 + (pr + 1) * P], ident[:, :])
                A.full(last)

            def attn_scores(h):
                pe.wait_ge(a_drained, MIXER_BANKS["qkT", 2 * (h // 2) + 1] + 1)
                lo = (h % 2) * AD
                q, k = qkT[lo:lo + AD, 0, h // 2, :], qkT[lo:lo + AD, 1, h // 2, :]
                b = Dr.bank()
                mm(b[:, 0:P], q[:, 0:P], k[:, 0:P], start=True, stop=True)
                Dr.full(mm(b[:, P:3 * P], q[:, P:T], k[:, 0:T], start=True, stop=True))

            def m_decay(h):
                pe.wait_ge(sem("neg_m"), 1)
                b = Dr.bank()
                Dr.full(mm(b[:, 0:T], sel(h, MH), r_f[0:MH, :], start=True, stop=True))

            def m_scores(h):
                pe.wait_ge(sem("m_qk"), 2 * MH)
                q, k = convT[:, h, :], convT[:, MH + h, :]
                b = Dr.bank()
                mm(b[:, 0:T], k[:, 0:P], q, start=True, stop=True)
                Dr.full(mm(b[:, T:3 * P], k[:, P:T], q[:, P:T], start=True, stop=True))

            def turn_probs(h):
                pe.wait_ge(sem("probs"), NT * (h + 1))
                b = A.bank()
                for n in range(3):
                    last = nc.tensor.transpose(b[:, n * P:(n + 1) * P], probs[:, h, n * P:(n + 1) * P], ident[:, :])
                A.full(last)

            def attn_out(pr):
                b = A.bank()
                for z in range(2):
                    h = 2 * pr + z
                    pe.wait_ge(a_drained, MIXER_BANKS["probsT", h] + 1)
                    o = b[z * AD:(z + 1) * AD, :]
                    mm(o[:, 0:T], v_tok[:, 0, h * AD:(h + 1) * AD], probsT[:, h, 0:T],
                       start=True, stop=False, skip_group_check=True)
                    last = mm(o[:, P:T], v_tok[:, 1, h * AD:(h + 1) * AD], probsT[:, h, T:3 * P],
                              start=False, stop=True, skip_group_check=True)
                A.full(last)

            def m_out(h):
                pe.wait_ge(d_drained, D_AT["m_scores"] + h + 1)
                b = Dr.bank()
                mm(b[:, 0:MD + 1], mw[:, h, 0:P], v_ext[:, 0, h, :], start=True, stop=True)
                mm(b[:, MD + 1:2 * (MD + 1)], mw[:, h, P:T], v_ext[:, 0, h, :], start=True, stop=False)
                Dr.full(mm(b[:, MD + 1:2 * (MD + 1)], mw[:, h, T:3 * P], v_ext[:, 1, h, :], start=False, stop=True))

            def turn_y(h):
                pe.wait_ge(sem("m_normed"), 1)
                b = Dr.bank()
                for t in range(NT):
                    last = nc.tensor.transpose(b[:, t * P:(t + 1) * P], nd[:, 2 * h + t, 0:MD], ident[:, :])
                Dr.full(last)

            in_ring_a = {"qkT": turn_qk, "probsT": turn_probs, "attn": attn_out}
            in_ring_d = {9: (attn_scores, 0), 10: (attn_scores, 2), 11: (attn_scores, 4), 12: (attn_scores, 6),
                         13: (m_decay, 0), 14: (m_decay, 2), 16: (m_scores, 0), 17: (m_scores, 2),
                         19: (m_out, 0), 20: (m_out, 2), 25: (turn_y, 0), 26: (turn_y, 2)}
            for u in range(8, Z_N):
                unit(A, h_parts)
                if u == 8:
                    gate_cols()
                if u in BESIDE_Z:
                    step, first = BESIDE_Z[u]
                    for j in range(2):
                        in_ring_a[step](first + j)
                if u in in_ring_d:
                    step, first = in_ring_d[u]
                    for j in range(2):
                        step(first + j)
            stage_ends()
            with repeat(pe, 2, {halves: 8, Dr.count: 8}):
                for _ in range(8):
                    b = Dr.bank()
                    y = [part_[:, _ % 2 * 4:_ % 2 * 4 + 4, :] for part_ in (y_hi, y_lo)]
                    ready = (lambda k: (sem("y_lo"), 4 + k + 1)) if _ == 0 else None
                    Dr.full(half_blocks(b, half(), y, 0, True, ready))
            stage_ends()
            columns(Dr, 8, h_parts, ready=lambda k: (sem("m_lo"), k + 1))
            ssq(xn)
            columns(A, 44, h_parts, Dr, ready=lambda k: (sem("h_lo"), KC + k + 1))
            row_blocks(FC, (f_hi, f_lo), lambda k: (sem("f_lo"), k + 1))
            ssq(xn2)
            ssq(xn2)
            unit(Dr, h_parts, lambda k: (sem("h_lo"), 2 * KC + k + 1))
            stage_ends()
            columns(A, XBC + KC, h_parts, ends=False)
            pe.wait_ge(sem("dt_rows"), 1)
            b = Dr.bank()
            for k, src in ((0, r_u), (1, r_i)):
                for t in range(NT):
                    at = (k * NT + t) * SH
                    last = nc.tensor.transpose(b[:, at:at + SH], src[0:SH, t * P:(t + 1) * P], ident[0:SH, 0:SH])
            Dr.full(last)
            pe.wait_ge(sem("xbc"), XBC)
            for j in range(4):
                t, side = divmod(j, 2)
                b = Dr.bank()
                for k in range(4):
                    last = nc.tensor.transpose(b[:, k * P:(k + 1) * P], xbcT[:, side * 4 + k, t * P:(t + 1) * P],
                                               ident[:, :])
                Dr.full(last)
            for g in range(SG):
                bs_, cs_ = xbcT[:, KC + g, :], xbcT[:, KC + SG + g, :]
                b = Dr.bank()
                mm(b[:, 0:T], bs_[:, 0:P], cs_, start=True, stop=True)
                Dr.full(mm(b[:, T:3 * P], bs_[:, P:T], cs_[:, P:T], start=True, stop=True))

            def ssd_decay(h):
                b = A.bank()
                u = r_u[0:SH, :]
                mm(b[:, 0:T], sel(h, SH), u, start=True, stop=False, skip_group_check=True)
                mm(b[:, 0:P], ident[:, :], mask_st[:, 0:P], start=False, stop=True, skip_group_check=True)
                mm(b[:, T:3 * P], sel(h, SH), u[:, P:T], start=True, stop=False, skip_group_check=True)
                A.full(mm(b[:, T:3 * P], ident[:, :], mask_st[:, 0:P], start=False, stop=True,
                          skip_group_check=True))

            def ssd_pair(j):
                b = Dr.bank()
                for z in range(2):
                    h = 2 * j + z
                    pe.wait_ge(sem("ssd_w"), 2 * h + 2)
                    o = b[z * SP:(z + 1) * SP, :]
                    w = ssd_w[:, h % 4, :]
                    mm(o[:, 0:T], xs_tok[:, 0, h * SP:(h + 1) * SP], w[:, 0:T], start=True, stop=False,
                       skip_group_check=True)
                    last = mm(o[:, P:T], xs_tok[:, 1, h * SP:(h + 1) * SP], w[:, T:3 * P], start=False, stop=True,
                              skip_group_check=True)
                Dr.full(last)
            for j in range(KC + 1):
                if j < NPOOL:
                    unit(A, h_parts)
                    if j == NPOOL - 1:
                        stage_ends()
                if j < KC:
                    ssd_decay(2 * j)
                    ssd_decay(2 * j + 1)
                if j >= 1:
                    ssd_pair(j - 1)
            ssq(xn2)
            pe.wait_ge(sem("pool_w_in"), 16)
            for g in range(NPOOL):
                pe.wait_ge(sem("pooled"), g + 1)
                b = Dr.bank()
                Dr.full(mm(b[:, 0:T], pool_wt[:, g, :], (pool_b, pool_a)[g % 2][:, g, 16:PADDED],
                           start=True, stop=True))
            row_blocks(MIXC, (mix_hi, mix_lo), lambda k: (sem("mix_lo"), k + 1))
            ssq(xn2)
            pe.wait_ge(sem("keys_in"), 16)

            def key_scores(j):
                pe.wait_ge(a_drained, A_AT["query"] + j + 1)
                b = Dr.bank()
                for t in range(NT):
                    last = mm(b[:, t * NK:(t + 1) * NK], xn2[:, j % 4, t * P:(t + 1) * P], keysT[:, j, :],
                              start=True, stop=True)
                Dr.full(last)
            for j in range(2 * QH):
                unit(A, h_parts, (lambda k: (sem("h_lo"), 3 * KC + k + 1)) if j == 0 else None)
                if j == 2 * QH - 1:
                    stage_ends()
                if j >= 1:
                    key_scores(j - 1)
            key_scores(2 * QH - 1)
            columns(A, P - LATE, h_parts, ends=False)
            pe.wait_ge(sem("picked"), 1)
            for z in range(3):
                b = Dr.bank()
                for t in range(NT):
                    last = nc.tensor.transpose(b[:, t * P:(t + 1) * P], picked[:, z, t * P:(t + 1) * P], ident[:, :])
                Dr.full(last)
            one_hot = Count()

            def spread():
                n = one_hot.n
                one_hot.n += 1
                at = 2 * (n + 1)
                pe.wait_ge(sem("one_hots"), at if one_hot.loop is None else one_hot.loop * 2 + at)
                b = Dr.bank()
                h = hot[:, n % ONEHOTS, :, :]
                Dr.full(mm(b[:, 0:P], h[:, 0, :], h[:, 1, :], start=True, stop=True))

            def two_tokens(_):
                spread()
                spread()
            with repeat(pe, LATE // 4, {halves: 8, A.count: 4, Dr.count: 16, one_hot: 16}):
                for _ in range(4):
                    unit(A, h_parts, beside=two_tokens)
            stage_ends()
            banks = [A.bank() for _ in range(BANKS)]

            def expert(j, n, first=False, last=False):
                pe.wait_ge(sem("u_lo"), n)
                s = j % 4
                row_unit(banks, (u_hi[:, s, :], u_lo[:, s, :]), first, last, A)
            for j in range(4):
                expert(j, j + 1, first=j == 0)
            with repeat(pe, P // 4 - 2, {halves: 8}) as i:
                for j in range(4):
                    expert(j, i * 4 + (j + 5))
            for j in range(4):
                expert(j, P - 3 + j, last=j == 3)
            ssq(U[:, 0:KC, :])


def kernel(**inputs):
    import numpy as np
    import concourse.bacc as bacc
    from concourse.bass_utils import run_bass_kernel_spmd

    a = {k: np.asarray(v) for k, v in inputs.items()}
    f32 = np.float32

    def chunks(v):
        return v.reshape(-1, P).T

    def columns(w):
        n = w.shape[1] // P
        return np.ascontiguousarray(w.reshape(KC, P, n, P).transpose(2, 1, 0, 3)).reshape(n, P, D)

    def padded(at):
        out = np.zeros((D, P), f32)
        for src, to in at:
            out[:, to:to + src.shape[1]] = src
        return columns(out)

    w_in, b_in = a["w_in"][0], a["b_in"][0]
    tok_cols = [slice(2056 + 512 * k, 2568 + 512 * k) for k in range(3)] + [slice(1024, 1536)]
    feat_cols = [slice(0, 1024), slice(1536, 2048), slice(3592, 5640)]
    tok = np.stack([w_in[:, s] for s in tok_cols])
    tok = np.ascontiguousarray(tok.reshape(4, 4, 2, P, 512).transpose(0, 1, 3, 2, 4)).reshape(16, P, D)
    w_gate, w_up = a["w_gate"][0], a["w_up"][0]
    gate_up = np.stack([w_gate.reshape(D, FC, P), w_up.reshape(D, FC, P)], axis=2).reshape(D, 2 * FF)
    w_in2 = a["w_in_2"][0]
    win2 = np.concatenate([w_in2[:, 1536:3072], w_in2[:, 512:1536], w_in2[:, 0:512]], axis=1)
    down = a["expert_down_2"][0].reshape(P, P, KC, P)
    down = np.ascontiguousarray(down.transpose(1, 3, 2, 0)).reshape(P, P, D)
    keys = np.stack([a["sub_keys1_2"][0], a["sub_keys2_2"][0]], axis=1)
    half = np.arange(32, dtype=f32) / f32(32)
    per_part = {
        "ada_b": chunks(a["ada_b"][0]), "norm1": chunks(a["norm1_g"][0]), "norm2": chunks(a["norm2_g"][0]),
        "normf": chunks(a["normf_g"]), "b_feat": chunks(np.concatenate([b_in[s] for s in feat_cols])),
        "conv_w": a["conv_w"][0].reshape(CONV, 8, P).transpose(2, 1, 0).reshape(P, 32),
        "conv_b": chunks(a["conv_b"][0]), "m_norm": chunks(a["m_norm_g"][0]), "ada_b2": chunks(a["b_ada_2"][0]),
        "norm_mix": chunks(a["norm_mix_2"][0]), "norm_ffn": chunks(a["norm_ffn_2"][0]),
        "norm_final": chunks(a["norm_final_2"]), "pool_b": a["pool_b_2"][0].T, "pool_scale": a["pool_scale_2"][0].T,
        "conv_w2": a["conv_w_2"][0].reshape(CONV, XBC, P).transpose(2, 1, 0).reshape(P, 48),
        "conv_b2": chunks(a["conv_b_2"][0]), "d_skip": chunks(np.repeat(a["d_skip_2"][0], SP)),
        "ssd_norm": chunks(a["ssd_norm_2"][0]), "b_i": b_in[2048:2052, None], "b_f": b_in[2052:2056, None],
        "dt_bias": a["dt_bias_2"][0][:, None], "a_log": a["a_log_2"][0][:, None],
        "inv_freq": np.broadcast_to(np.power(f32(10000.0), -half).astype(f32), (P, 32)),
    }
    cols = np.zeros((P, NCOLS), f32)
    for name, (at, width) in COLS.items():
        cols[:per_part[name].shape[0], at:at + width] = per_part[name]
    arrays = {
        "x": np.ascontiguousarray(a["x"][0].T.reshape(KC, P, T).transpose(1, 0, 2)),
        "c": a["c"], "c_2": a["c_2"],
        "pos": np.ascontiguousarray(a["positions"][0].reshape(NT, P).T),
        "cols_in": cols,
        "bias_tok": np.stack([b_in[s] for s in tok_cols]),
        "gates": padded([(w_in[:, 2048:2052], 0), (w_in[:, 2052:2056], 32)]),
        "dt": padded([(w_in2[:, 3072:3088], 0)]),
        "pool_w": np.ascontiguousarray(a["pool_w_2"][0].transpose(1, 0, 2)),
        "keys": np.ascontiguousarray(keys.reshape(16, NK, P).transpose(2, 0, 1)),
        "ada": np.ascontiguousarray(a["ada_w"][0].T).reshape(48, P, D),
        "ada2": np.ascontiguousarray(a["w_ada_2"][0].T).reshape(48, P, D),
        "tok": tok,
        "feat": columns(np.concatenate([w_in[:, s] for s in feat_cols], axis=1)),
        "proj": columns(np.concatenate([a["p_mlstm"][0], a["p_moba"][0]], axis=0)),
        "wout": columns(a["w_out"][0]),
        "gateup": columns(gate_up),
        "down": a["w_down"][0].reshape(FC, P, D),
        "win2": columns(win2),
        "wout2": a["w_out_2"][0].reshape(MIXC, P, D),
        "query": columns(a["w_query_2"][0]),
        "expert_down": down,
        "expert_up": a["expert_up_2"][0].reshape(P, P, D),
    }
    nc = bacc.Bacc("TRN2", target_bir_lowering=False, num_devices=1)
    aps = {n: nc.dram_tensor(n, v.shape, mybir.dt.from_np(v.dtype), kind="ExternalInput").ap()
           for n, v in arrays.items()}
    out = nc.dram_tensor("out", (P, KC, T), F32, kind="ExternalOutput").ap()
    two_mixers_program(nc, **aps, out=out)
    r = run_bass_kernel_spmd(nc, [arrays], core_ids=[0])
    y = r.results[0]["out"]
    return np.ascontiguousarray(y.transpose(1, 0, 2).reshape(D, T).T)[None]
```
